# Optimizing a Trainium2 kernel written in Bass

```python
import jax
import jax.numpy as jnp
from jax import lax
import numpy as np
import jax, jax.numpy as jnp

D_MODEL = 2048
BATCH = 1
SEQ = 256
DEPTH = 1

EPS = 1e-6
HEAD_DIM = 128

GLA_HEADS = 4
GLA_DK = 64
GLA_DV = 128
GLA_GATE_RANK = 16
GLA_TAU = 16.0
GLA_CHUNK = 64

DIL_HEADS = 12
DIL_PATTERNS = ((128, 1), (512, 4), (2048, 16))
ROPE_THETA = 500000.0
ROPE_DIM = HEAD_DIM // 4
MASK_VALUE = -1e30

PEER_HEADS = 8
PEER_NKEYS = 128
PEER_NEXPERTS = PEER_NKEYS * PEER_NKEYS
PEER_QDIM = 256
PEER_TOPK = 16
PEER_TOKEN_BLOCK = 128

GLA_QK_W = GLA_HEADS * GLA_DK
GLA_V_W = GLA_HEADS * GLA_DV
DIL_W = DIL_HEADS * HEAD_DIM
MIX_W = GLA_V_W + DIL_W
IN_SPLITS = (GLA_QK_W, GLA_QK_W, GLA_V_W, GLA_GATE_RANK, GLA_GATE_RANK, GLA_V_W, DIL_W, DIL_W, DIL_W)
IN_W = sum(IN_SPLITS)


def rms_norm(x, g):
    xf = x.astype(jnp.float32)
    y = xf * lax.rsqrt(jnp.mean(xf * xf, axis=-1, keepdims=True) + EPS)
    return (y * g.astype(jnp.float32)).astype(x.dtype)

def partial_rope(t, positions):
    half = ROPE_DIM // 2
    inv_freq = ROPE_THETA ** (-jnp.arange(half, dtype=jnp.float32) / half)
    ang = positions.astype(jnp.float32)[:, None] * inv_freq[None, :]
    cos = jnp.cos(ang)[None, :, None, :]
    sin = jnp.sin(ang)[None, :, None, :]
    tf = t.astype(jnp.float32)
    x1 = tf[..., :half]
    x2 = tf[..., half:ROPE_DIM]
    return jnp.concatenate([x1 * cos - x2 * sin, x2 * cos + x1 * sin, tf[..., ROPE_DIM:]], axis=-1)

def gla_direction(q, k, v, log_a, include_diag):
    Bsz, H, S, dk = q.shape
    dv = v.shape[-1]
    C = GLA_CHUNK
    N = S // C
    q = q.reshape(Bsz, H, N, C, dk)
    k = k.reshape(Bsz, H, N, C, dk)
    v = v.reshape(Bsz, H, N, C, dv)
    b = jnp.cumsum(log_a.reshape(Bsz, H, N, C, dk), axis=3)
    b_last = b[:, :, :, -1:, :]
    q_in = q * jnp.exp(b)
    k_in = k * jnp.exp(-b)
    scores = jnp.einsum('bhnik,bhnjk->bhnij', q_in, k_in)
    mask = jnp.tril(jnp.ones((C, C), dtype=bool), k=0 if include_diag else -1)
    o_intra = jnp.einsum('bhnij,bhnjv->bhniv', jnp.where(mask, scores, 0.0), v)
    k_state = k * jnp.exp(b_last - b)
    inc = jnp.einsum('bhnjk,bhnjv->bhnkv', k_state, v)
    decay = jnp.exp(b_last[:, :, :, 0, :])

    def step(state, inp):
        dec, add = inp
        return dec[..., None] * state + add, state

    s0 = jnp.zeros((Bsz, H, dk, dv), jnp.float32)
    _, s_before = lax.scan(step, s0, (jnp.moveaxis(decay, 2, 0), jnp.moveaxis(inc, 2, 0)))
    s_before = jnp.moveaxis(s_before, 0, 2)
    o_inter = jnp.einsum('bhnik,bhnkv->bhniv', q_in, s_before)
    return (o_intra + o_inter).reshape(Bsz, H, S, dv)

def gla_mixer(q, k, v, gate_down_f, gate_down_b, r, up_f, bias_f, up_b, bias_b, out_g):
    Bsz, S, _ = q.shape
    f32 = jnp.float32

    def heads(t, d):
        return t.astype(f32).reshape(Bsz, S, GLA_HEADS, d).transpose(0, 2, 1, 3)

    qh = heads(q, GLA_DK) * (GLA_DK ** -0.5)
    kh = heads(k, GLA_DK)
    vh = heads(v, GLA_DV)
    la_f = heads(jax.nn.log_sigmoid(gate_down_f.astype(f32) @ up_f.astype(f32) + bias_f.astype(f32)) / GLA_TAU, GLA_DK)
    la_b = heads(jax.nn.log_sigmoid(gate_down_b.astype(f32) @ up_b.astype(f32) + bias_b.astype(f32)) / GLA_TAU, GLA_DK)

    def rev(t):
        return jnp.flip(t, axis=2)

    o_fwd = gla_direction(qh, kh, vh, la_f, True)
    o_bwd = rev(gla_direction(rev(qh), rev(kh), rev(vh), rev(la_b), False))
    o = (o_fwd + o_bwd).transpose(0, 2, 1, 3)
    o = rms_norm(o, out_g.reshape(GLA_HEADS, GLA_DV))
    return o.reshape(Bsz, S, GLA_V_W) * jax.nn.silu(r.astype(f32))

def dilated_window_attention(q, k, v, window, dilation):
    Bsz, S, H, hd = q.shape
    half = window // (2 * dilation)
    L = S // dilation
    nb = -(-L // half)
    Lp = nb * half

    def to_blocks(t):
        t = t.reshape(Bsz, L, dilation, H, hd)
        t = jnp.pad(t, ((0, 0), (0, Lp - L), (0, 0), (0, 0), (0, 0)))
        return t.reshape(Bsz, nb, half, dilation, H, hd)

    def with_neighbours(t):
        tp = jnp.pad(t, ((0, 0), (1, 1), (0, 0), (0, 0), (0, 0), (0, 0)))
        return jnp.concatenate([tp[:, :-2], tp[:, 1:-1], tp[:, 2:]], axis=2)

    qb = to_blocks(q)
    kn = with_neighbours(to_blocks(k))
    vn = with_neighbours(to_blocks(v))
    s = jnp.einsum('bnqrhe,bnkrhe->bnrhqk', qb, kn)
    qpos = jnp.arange(nb)[:, None] * half + jnp.arange(half)[None, :]
    kpos = jnp.arange(nb)[:, None] * half - half + jnp.arange(3 * half)[None, :]
    rel = kpos[:, None, :] - qpos[:, :, None]
    valid = (jnp.abs(rel) <= half) & (kpos[:, None, :] >= 0) & (kpos[:, None, :] < L)
    s = jnp.where(valid[None, :, None, None], s, MASK_VALUE)
    m = jnp.max(s, axis=-1)
    p = jnp.exp(s - m[..., None])
    den = jnp.sum(p, axis=-1)
    m_t = jnp.moveaxis(m, (2, 3, 4), (3, 4, 2))
    den_t = jnp.moveaxis(den, (2, 3, 4), (3, 4, 2))
    o = jnp.einsum('bnrhqk,bnkrhe->bnqrhe', p, vn) / den_t[..., None]

    def back(t):
        t = t.reshape((Bsz, Lp, dilation, H) + t.shape[5:])[:, :L]
        return t.reshape((Bsz, S, H) + t.shape[4:])

    return back(o), back(m_t), back(den_t)

def dilated_mixer(q, k, v, q_norm_g, k_norm_g, positions):
    Bsz, S, _ = q.shape
    shp = (Bsz, S, DIL_HEADS, HEAD_DIM)
    qh = partial_rope(rms_norm(q.reshape(shp), q_norm_g), positions) * (HEAD_DIM ** -0.5)
    kh = partial_rope(rms_norm(k.reshape(shp), k_norm_g), positions)
    vh = v.reshape(shp).astype(jnp.float32)
    outs, maxes, dens = [], [], []
    for window, dilation in DIL_PATTERNS:
        o, m, d = dilated_window_attention(qh, kh, vh, window, dilation)
        outs.append(o)
        maxes.append(m)
        dens.append(d)
    m_all = jnp.stack(maxes)
    w = jnp.stack(dens) * jnp.exp(m_all - jnp.max(m_all, axis=0, keepdims=True))
    w = w / jnp.sum(w, axis=0, keepdims=True)
    o = jnp.sum(w[..., None] * jnp.stack(outs), axis=0)
    return o.reshape(Bsz, S, DIL_W)

def peer_ffn(xn, w_query, sub_keys, expert_down, expert_up):
    Bsz, S, D = xn.shape
    f32 = jnp.float32
    T = Bsz * S
    xt = xn.reshape(T, D)
    qry = (xt @ w_query).reshape(T, PEER_HEADS, 2, PEER_QDIM // 2)
    sc = jnp.einsum('thcd,hckd->thck', qry.astype(f32), sub_keys.astype(f32))
    top_s, top_i = lax.top_k(sc, PEER_TOPK)
    kk = PEER_TOPK * PEER_TOPK
    cand_s = (top_s[:, :, 0, :, None] + top_s[:, :, 1, None, :]).reshape(T, PEER_HEADS, kk)
    cand_i = (top_i[:, :, 0, :, None] * PEER_NKEYS + top_i[:, :, 1, None, :]).reshape(T, PEER_HEADS, kk)
    best_s, best_pos = lax.top_k(cand_s, PEER_TOPK)
    idx = jnp.take_along_axis(cand_i, best_pos, axis=-1)
    gates = jax.nn.softmax(best_s, axis=-1)
    K = PEER_HEADS * PEER_TOPK
    nblk = T // PEER_TOKEN_BLOCK

    def block(args):
        xb, ib, gb = args
        u = expert_down[ib]
        act = jax.nn.gelu(jnp.einsum('tkd,td->tk', u, xb).astype(f32))
        vv = expert_up[ib]
        return jnp.einsum('tk,tkd->td', (gb * act).astype(vv.dtype), vv)

    out = lax.map(block, (xt.reshape(nblk, PEER_TOKEN_BLOCK, D),
                          idx.reshape(nblk, PEER_TOKEN_BLOCK, K),
                          gates.reshape(nblk, PEER_TOKEN_BLOCK, K)))
    return out.reshape(Bsz, S, D).astype(xn.dtype)

def first_inputs(seed: int = 0) -> dict:
    key = jax.random.key(seed)
    ks = jax.random.split(key, 16)
    f32 = jnp.float32

    def nrm(k, shape, scale):
        return jax.random.normal(k, shape, f32) * scale

    def gain(k, shape):
        return 1.0 + 0.02 * jax.random.normal(k, shape, f32)

    L = DEPTH
    return {
        'x': nrm(ks[0], (BATCH, SEQ, D_MODEL), 1.0),
        'norm1_g': gain(ks[1], (L, D_MODEL)),
        'w_in': nrm(ks[2], (L, D_MODEL, IN_W), D_MODEL ** -0.5),
        'gla_up_f': nrm(ks[3], (L, GLA_GATE_RANK, GLA_QK_W), GLA_GATE_RANK ** -0.5),
        'gla_bias_f': nrm(ks[4], (L, GLA_QK_W), 0.1),
        'gla_up_b': nrm(ks[5], (L, GLA_GATE_RANK, GLA_QK_W), GLA_GATE_RANK ** -0.5),
        'gla_bias_b': nrm(ks[6], (L, GLA_QK_W), 0.1),
        'gla_out_g': gain(ks[7], (L, GLA_V_W)),
        'q_norm_g': gain(ks[8], (L, HEAD_DIM)),
        'k_norm_g': gain(ks[9], (L, HEAD_DIM)),
        'w_out': nrm(ks[10], (L, MIX_W, D_MODEL), MIX_W ** -0.5),
        'norm2_g': gain(ks[11], (L, D_MODEL)),
        'peer_w_query': nrm(ks[12], (L, D_MODEL, PEER_HEADS * PEER_QDIM), D_MODEL ** -0.5),
        'peer_sub_keys': nrm(ks[13], (L, PEER_HEADS, 2, PEER_NKEYS, PEER_QDIM // 2), (PEER_QDIM // 2) ** -0.5),
        'peer_down': nrm(ks[14], (L, PEER_NEXPERTS, D_MODEL), D_MODEL ** -0.5),
        'peer_up': nrm(ks[15], (L, PEER_NEXPERTS, D_MODEL), PEER_HEADS ** -0.5),
    }

def first_block(x, norm1_g, w_in, gla_up_f, gla_bias_f, gla_up_b, gla_bias_b, gla_out_g, q_norm_g, k_norm_g, w_out, norm2_g, peer_w_query, peer_sub_keys, peer_down, peer_up):
    positions = jnp.arange(x.shape[1], dtype=jnp.int32)
    split_points = [int(c) for c in np.cumsum(IN_SPLITS)[:-1]]
    for l in range(DEPTH):
        xn = rms_norm(x, norm1_g[l])
        h = xn @ w_in[l]
        qa, ka, va, gdf, gdb, ra, qd, kd, vd = jnp.split(h, split_points, axis=-1)
        oa = gla_mixer(qa, ka, va, gdf, gdb, ra, gla_up_f[l], gla_bias_f[l], gla_up_b[l], gla_bias_b[l], gla_out_g[l])
        od = dilated_mixer(qd, kd, vd, q_norm_g[l], k_norm_g[l], positions)
        mixed = jnp.concatenate([oa, od], axis=-1).astype(x.dtype)
        x = x + mixed @ w_out[l]
        x = x + peer_ffn(rms_norm(x, norm2_g[l]), peer_w_query[l], peer_sub_keys[l], peer_down[l], peer_up[l])
    return x


DEPTH_2 = 2

EXPAND = 2
D_INNER = EXPAND * D_MODEL
PLE_DIM = 256
N_MIXERS = 2
POOL_WINDOWS = (2, 4, 8, 16)
N_POOL_GROUPS = len(POOL_WINDOWS)
POOL_GROUP_DIM = D_INNER // N_POOL_GROUPS
LRU_HEADS = 16
LRU_BLOCK = D_INNER // LRU_HEADS
CONV_WIDTH = 4
LRU_C = 8.0
RMS_EPS = 1e-6
N_POOL_LAYERS = (DEPTH_2 + 1) // 2
N_LRU_LAYERS = DEPTH_2 // 2


def rmsnorm(x, g):
    xf = x.astype(jnp.float32)
    var = jnp.mean(xf * xf, axis=-1, keepdims=True)
    return (xf * lax.rsqrt(var + RMS_EPS) * g.astype(jnp.float32)).astype(x.dtype)

def pool_mixer(u, w_grp, b, scale):
    B, S, E = u.shape
    maxw = POOL_WINDOWS[-1]
    uf = u.astype(jnp.float32)
    cs = jnp.cumsum(uf, axis=1)
    csp = jnp.pad(cs, ((0, 0), (maxw, 0), (0, 0)))
    pos = jnp.arange(1, S + 1, dtype=jnp.int32)
    diffs = []
    for g, w in enumerate(POOL_WINDOWS):
        c0, c1 = g * POOL_GROUP_DIM, (g + 1) * POOL_GROUP_DIM
        win_sum = csp[:, maxw:, c0:c1] - csp[:, maxw - w:maxw - w + S, c0:c1]
        count = jnp.minimum(pos, w).astype(jnp.float32)[None, :, None]
        diffs.append(win_sum / count - uf[..., c0:c1])
    d = jnp.stack(diffs, axis=2).astype(u.dtype)
    y = jnp.einsum('bsgc,gcd->bsgd', d, w_grp).reshape(B, S, E) + b
    return y * scale

def causal_depthwise_conv(x, w, b):
    S = x.shape[1]
    xp = jnp.pad(x, ((0, 0), (CONV_WIDTH - 1, 0), (0, 0)))
    y = b
    for k in range(CONV_WIDTH):
        y = y + xp[:, k:k + S] * w[k]
    return y

def rglru(x, wa, ba, wx, bx, lam):
    B, S, E = x.shape
    xb = x.reshape(B, S, LRU_HEADS, LRU_BLOCK)
    r = jax.nn.sigmoid((jnp.einsum('bshi,hij->bshj', xb, wa).reshape(B, S, E) + ba).astype(jnp.float32))
    ig = jax.nn.sigmoid((jnp.einsum('bshi,hij->bshj', xb, wx).reshape(B, S, E) + bx).astype(jnp.float32))
    log_a = -LRU_C * r * jax.nn.softplus(-lam.astype(jnp.float32))
    a = jnp.exp(log_a)
    mult = jnp.sqrt(jnp.maximum(-jnp.expm1(2.0 * log_a), 0.0))
    bterm = mult * ig * x.astype(jnp.float32)

    def combine(left, right):
        a1, b1 = left
        a2, b2 = right
        return a1 * a2, a2 * b1 + b2

    _, h = lax.associative_scan(combine, (a, bterm), axis=1)
    return h.astype(x.dtype)

def second_inputs(seed: int = 0) -> dict:
    key = jax.random.key(seed)
    ks = jax.random.split(key, 24)
    f32 = jnp.float32

    def nrm(k, shape, fan_in):
        return jax.random.normal(k, shape, f32) * (fan_in ** -0.5)

    def gain(k, shape):
        return 1.0 + 0.05 * jax.random.normal(k, shape, f32)

    def bias(k, shape):
        return 0.01 * jax.random.normal(k, shape, f32)

    a0 = jax.random.uniform(ks[15], (N_LRU_LAYERS, D_INNER), f32, 0.9, 0.999)
    lru_L = jnp.log(a0) - jnp.log1p(-a0)
    return {
        "x": jax.random.normal(ks[0], (BATCH, SEQ, D_MODEL), f32),
        "p": jax.random.normal(ks[1], (DEPTH_2, BATCH, SEQ, PLE_DIM), f32),
        "w_in": nrm(ks[2], (DEPTH_2, D_MODEL, 2 * D_INNER), D_MODEL),
        "w_out": nrm(ks[3], (DEPTH_2, D_INNER, D_MODEL), D_INNER),
        "g_pre": gain(ks[4], (DEPTH_2, D_MODEL)),
        "g_post": gain(ks[5], (DEPTH_2, D_MODEL)),
        "pool_w": nrm(ks[6], (N_POOL_LAYERS, N_POOL_GROUPS, POOL_GROUP_DIM, POOL_GROUP_DIM), POOL_GROUP_DIM),
        "pool_b": bias(ks[7], (N_POOL_LAYERS, D_INNER)),
        "pool_scale": gain(ks[8], (N_POOL_LAYERS, D_INNER)),
        "conv_w": nrm(ks[9], (N_LRU_LAYERS, CONV_WIDTH, D_INNER), CONV_WIDTH),
        "conv_b": bias(ks[10], (N_LRU_LAYERS, D_INNER)),
        "lru_wa": nrm(ks[11], (N_LRU_LAYERS, LRU_HEADS, LRU_BLOCK, LRU_BLOCK), LRU_BLOCK),
        "lru_ba": bias(ks[12], (N_LRU_LAYERS, D_INNER)),
        "lru_wx": nrm(ks[13], (N_LRU_LAYERS, LRU_HEADS, LRU_BLOCK, LRU_BLOCK), LRU_BLOCK),
        "lru_bx": bias(ks[14], (N_LRU_LAYERS, D_INNER)),
        "lru_L": lru_L,
        "w_ple": nrm(ks[16], (DEPTH_2, PLE_DIM, D_MODEL), PLE_DIM),
        "w_ple_gate": nrm(ks[17], (DEPTH_2, D_MODEL, D_MODEL), D_MODEL),
        "g_ple_in": gain(ks[18], (DEPTH_2, D_MODEL)),
        "g_ple_out": gain(ks[19], (DEPTH_2, D_MODEL)),
    }

def second_block(x, p, w_in, w_out, g_pre, g_post, pool_w, pool_b, pool_scale,
              conv_w, conv_b, lru_wa, lru_ba, lru_wx, lru_bx, lru_L,
              w_ple, w_ple_gate, g_ple_in, g_ple_out):
    for i in range(DEPTH_2):
        h = rmsnorm(x, g_pre[i])
        uz = jnp.einsum('bsd,de->bse', h, w_in[i])
        u, z = uz[..., :D_INNER], uz[..., D_INNER:]
        j = i // N_MIXERS
        if i % N_MIXERS == 0:
            y = pool_mixer(u, pool_w[j], pool_b[j], pool_scale[j])
        else:
            uc = causal_depthwise_conv(u, conv_w[j], conv_b[j])
            y = rglru(uc, lru_wa[j], lru_ba[j], lru_wx[j], lru_bx[j], lru_L[j])
        y = y * jax.nn.silu(z)
        o = jnp.einsum('bse,ed->bsd', y, w_out[i])
        x = x + rmsnorm(o, g_post[i])
        gate = jax.nn.sigmoid(jnp.einsum('bsd,de->bse', rmsnorm(x, g_ple_in[i]), w_ple_gate[i]))
        e = jnp.einsum('bsk,kd->bsd', p[i], w_ple[i])
        x = x + rmsnorm(e * gate, g_ple_out[i])
    return x


def setup_inputs(seed=0):
    out = dict(first_inputs(seed))
    for name, value in second_inputs(seed + 1).items():
        if name != "x":
            out[name + "_2"] = value
    return out


def reference(
    x, norm1_g, w_in, gla_up_f, gla_bias_f, gla_up_b, gla_bias_b, gla_out_g, q_norm_g, k_norm_g,
    w_out, norm2_g, peer_w_query, peer_sub_keys, peer_down, peer_up, p_2, w_in_2, w_out_2,
    g_pre_2, g_post_2, pool_w_2, pool_b_2, pool_scale_2, conv_w_2, conv_b_2, lru_wa_2, lru_ba_2,
    lru_wx_2, lru_bx_2, lru_L_2, w_ple_2, w_ple_gate_2, g_ple_in_2, g_ple_out_2,
):
    x = first_block(
        x, norm1_g, w_in, gla_up_f, gla_bias_f, gla_up_b, gla_bias_b, gla_out_g, q_norm_g,
        k_norm_g, w_out, norm2_g, peer_w_query, peer_sub_keys, peer_down, peer_up,
    )
    return second_block(
        x, p_2, w_in_2, w_out_2, g_pre_2, g_post_2, pool_w_2, pool_b_2, pool_scale_2, conv_w_2,
        conv_b_2, lru_wa_2, lru_ba_2, lru_wx_2, lru_bx_2, lru_L_2, w_ple_2, w_ple_gate_2,
        g_ple_in_2, g_ple_out_2,
    )


_drawn_inputs = setup_inputs


def setup_inputs(seed=0):
    import zlib

    import numpy as np

    out = dict(_drawn_inputs(seed))
    spreads = {}
    factors = {'gla_bias_f': 3.072,
     'gla_bias_b': 2.828,
     'gla_out_g': 10.739,
     'q_norm_g': 6.163,
     'k_norm_g': 5.665,
     'conv_b_2': 3.192,
     'lru_ba_2': 61.381,
     'lru_bx_2': 36.427,
     'g_ple_in_2': 15.799,
     'norm2_g': 9.599,
     'g_post_2': 3.086,
     'pool_b_2': 3.018,
     'pool_scale_2': 4.132,
     'g_ple_out_2': 3.058}
    for name, (base, spread) in spreads.items():
        noise = np.random.default_rng([zlib.crc32(name.encode()), seed]).standard_normal(out[name].shape)
        drawn = base * np.exp(spread * noise) if base else spread * noise
        out[name] = jnp.asarray(drawn.astype(out[name].dtype))
    for name, factor in factors.items():
        out[name] = (out[name] * factor).astype(out[name].dtype)
    return out
```

```python
from contextlib import ExitStack

import concourse.bass as bass
from concourse import mybir

F32 = mybir.dt.float32
FR = mybir.dt.float32r
U32 = mybir.dt.uint32
ALU = mybir.AluOpType
ACT = mybir.ActivationFunctionType
AX = mybir.AxisListType

T = 256
D = 2048
KD = 16
NRAW = 3
NSPL = 3
PARTS = [(0, 64), (64, 64)]
NEG = -3.0e38

VECS = [
    ("norm1_g", 16), ("norm2_g", 16), ("gla_bias", 4), ("gla_out_g", 4), ("q_norm_g", 1), ("k_norm_g", 1),
    ("g_pre_2", 32), ("g_post_2", 32), ("g_ple_in_2", 32), ("g_ple_out_2", 32),
    ("pool_b_2", 32), ("pool_scale_2", 32), ("conv_w_2", 128), ("conv_b_2", 32),
    ("lru_ba_2", 32), ("lru_bx_2", 32), ("lru_L_2", 32), ("eps", 1), ("one", 1),
]
VOFF = {}
_n = 0
for _k, _w in VECS:
    VOFF[_k] = _n
    _n += _w
NVEC = _n

SETS = {"logexp": "natural_log_exp_and_others", "gelu": "gelu_apprx_tanh_and_others",
        "sigmoid": "sigmoid_and_others"}


class Queue:

    def __init__(self, eng, sem):
        self.eng, self.sem = eng, sem
        self.count = 0
        self.seen = {}

    def wait(self, after):
        for sem, val in after:
            if self.seen.get(id(sem), 0) < val:
                self.seen[id(sem)] = val
                self.eng.wait_ge(sem, val)

    def put(self, fn, after=(), inc=True):
        self.wait(after)
        ins = fn(self.eng)
        if inc:
            ins.then_inc(self.sem, 1)
            self.count += 1
        return (self.sem, self.count)

    def dma(self, fn, sem, after=()):
        self.wait(after)
        fn(self.eng).then_inc(sem, 16)


class Pool:

    def __init__(self, places):
        self.free = [(p, []) for p in places]

    def take(self):
        assert self.free, "no place free"
        return self.free.pop(0)

    def give(self, place, ticks):
        self.free.append((place, list(ticks)))


def build(nc, d, out, stop=None):
    ctx = ExitStack()
    with ctx:
        def sb(name, shape, dt=F32, c=ctx):
            return c.enter_context(nc.sbuf_tensor(name, shape, dt))

        def sem(name):
            return ctx.enter_context(nc.semaphore(name))

        pe, act, dve, sp, pool = (
            Queue(e, sem("s_" + n)) for e, n in ((nc.tensor, "pe"), (nc.scalar, "act"), (nc.vector, "dve"),
                                                 (nc.sync, "sp"), (nc.gpsimd, "pool")))

        XT = sb("XT", [128, KD, T])
        AH = sb("AH", [128, KD, T], FR)
        AL = sb("AL", [128, KD, T], FR)
        RAW = sb("RAW", [128, NRAW, 2048])
        WH = sb("WH", [128, NSPL, 2048], FR)
        WL = sb("WL", [128, NSPL, 2048], FR)
        VEC = sb("VEC", [128, NVEC])
        ONES = sb("ONES", [128, 128])
        IDENT = sb("IDENT", [128, 128])
        SQ = sb("SQ", [128, 2, T])
        R = sb("R", [128, T])
        TMP = sb("TMP", [128, 2, T])
        banks = [ctx.enter_context(nc.psum_tensor(f"PS{i}", [128, 512], F32)) for i in range(8)]
        mbank = Pool(banks[0:4])
        abank = Pool(banks[4:8])

        raw_sem = [sem(f"s_raw{i}") for i in range(NRAW)]
        s_out = sem("s_out")
        nload = [0]

        def load(dst, src, after=(), q=sp):
            s = sem(f"s_ld{nload[0]}")
            nload[0] += 1
            q.dma(lambda e: e.dma_start(dst, src), s, after)
            return (s, 16)

        def vec(name, i=0, p0=0, p1=128):
            o = VOFF[name] + i
            return VEC[p0:p1, o:o + 1]

        t_vec = load(VEC[:, :], d["vecs"][:, :])
        x4 = d["xt"].rearrange("p (k t) -> p k t", k=KD)
        t_xts = [load(XT[:, 4 * i:4 * i + 4, :], x4[:, 4 * i:4 * i + 4, :]) for i in range(4)]
        t_ones = load(ONES[:, :], d["ones"][:, :], q=act)
        t_ident = load(IDENT[:, :], d["ident"][:, :], q=act)

        order = []
        winA = d["w_in"]
        for i in [8] + list(range(8)) + list(range(9, 13)):
            order.append(winA[i])
        for h in range(12):
            for j in range(3):
                order.append(winA[13 + 12 * j + h])
        order += [d["w_out"][i] for i in range(16)]
        order += [d["w_query"][i] for i in range(16)]
        for p0, n in PARTS:
            order += [d["peer_down"][j] for j in range(p0, p0 + n)]
            order += [d["peer_up"].rearrange("(i j) c -> j i c", j=128)[j] for j in range(p0, p0 + n)]
        for l in range(2):
            w2 = d["w_in_2"]
            if l == 0:
                for g in range(4):
                    order += [w2[8 * g + i] for i in range(8)]
                    for half in range(2):
                        order += [w2[32 + 8 * g + 4 * half + i] for i in range(4)]
                        order += [d["pool_w"][4 * g + 2 * half + i] for i in range(2)]
            else:
                for g in range(8):
                    order += [w2[64 + 4 * g + i] for i in range(4)]
                    order += [w2[96 + 4 * g + i] for i in range(4)]
                    order += [d["lru_w"][g]]
            order += [d["w_out_2"][32 * l + i] for i in range(32)]
            order += [d["w_ple"][2 * l + i] for i in range(2)]
            order += [d["w_gate"][16 * l + i] for i in range(16)]
        NCH = len(order)

        t_hi, t_lo, t_used = {}, {}, {}
        st = {"fetched": 0, "split": 0, "used": 0}

        def fetch(c):
            after = [t_hi[c - NRAW], t_lo[c - NRAW]] if c >= NRAW else []
            s = c % NRAW
            sp.dma(lambda e: e.dma_start(RAW[:, s, :], order[c]), raw_sem[s], after)

        def split(c):
            r, s = c % NRAW, c % NSPL
            here = (raw_sem[r], 16 * (c // NRAW + 1))
            freed = [t_used[c - NSPL]] if c >= NSPL else []
            t_hi[c] = act.put(lambda e: e.activation(WH[:, s, :], RAW[:, r, :], ACT.Copy), [here] + freed)
            t_lo[c] = dve.put(lambda e: e.tensor_tensor(WL[:, s, :], RAW[:, r, :], WH[:, s, :].bitcast(F32),
                                                        ALU.subtract), [here, t_hi[c]] + freed)

        def ahead(c):
            while st["split"] < min(NCH, c + NSPL):
                while st["fetched"] < min(NCH, st["split"] + NRAW):
                    fetch(st["fetched"])
                    st["fetched"] += 1
                split(st["split"])
                st["split"] += 1

        bg = []

        def step(n=1):
            for _ in range(n):
                if not bg:
                    return
                if next(bg[0], "end") == "end":
                    bg.pop(0)

        def drain(gen=None):
            while bg and (gen is None or gen in bg):
                step()

        def chunk(jobs, steps=1):
            c = st["used"]
            ahead(c)
            s = c % NSPL
            n = len(jobs)
            tick = None
            for j, (ps, b, xh, xl, first, last, after, mark) in enumerate(jobs):
                wh, wl = WH[:, s, b * 128:b * 128 + 128], WL[:, s, b * 128:b * 128 + 128]
                w = list(after) + [t_lo[c]]
                fin = mark or j == n - 1
                pe.put(lambda e, ps=ps, wh=wh, xh=xh, first=first: e.matmul(
                    ps, wh, xh, start=first, stop=False, skip_group_check=True), w, inc=False)
                pe.put(lambda e, ps=ps, wh=wh, xl=xl: e.matmul(
                    ps, wh, xl, start=False, stop=False, skip_group_check=True), inc=False)
                tick = pe.put(lambda e, ps=ps, wl=wl, xh=xh, last=last: e.matmul(
                    ps, wl, xh, start=False, stop=last, skip_group_check=True), inc=fin)
                if mark:
                    mark.append(tick)
            t_used[c] = tick
            st["used"] = c + 1
            step(steps)
            return tick

        def tile_k(src, ticks, nk=KD, steps=1):
            bank, freed = mbank.take()
            ps = bank[:, 0:T]
            hi, lo = src
            for c0 in range(0, nk, 16):
                jobs = []
                for b in range(min(16, nk)):
                    k = c0 + b
                    jobs.append((ps, b, hi[:, k, :], lo[:, k, :], k == 0, k == nk - 1,
                                 (freed if k == 0 else []) + list(ticks.get(k, [])), None))
                t = chunk(jobs, steps)
            return bank, ps, t

        t_a = {}
        A = (AH, AL)

        def prep(k, src, g, after, freed=()):
            th = act.put(lambda e: e.activation(AH[:, k, :], src, ACT.Copy, scale=g), list(after) + list(freed))
            tl = dve.put(lambda e: e.scalar_tensor_tensor(AL[:, k, :], src, g, AH[:, k, :].bitcast(F32),
                                                          ALU.mult, ALU.subtract), [th] + list(after) + list(freed))
            t_a[k] = [th, tl]
            return tl

        sq = {"n": 0, "used": {}, "bank": None, "late": []}

        def square(src, after, n, total):
            i = sq["n"]
            sq["n"] += 1
            s = i % 2
            freed = [sq["used"][i - 2]] if i - 2 in sq["used"] else []
            t = act.put(lambda e: e.activation(SQ[:, s, :], src, ACT.Square), list(after) + freed)
            if n == 0:
                sq["bank"], sq["freed"] = abank.take()
            bank, extra = sq["bank"], (sq["freed"] if n == 0 else [])
            def go():
                sq["used"][i] = pe.put(lambda e: e.matmul(bank[:, 0:T], ONES[:, :], SQ[:, s, :], start=(n == 0),
                                                          stop=(n == total - 1)), [t, t_ones] + extra)
            sq["late"].append(go)
            if len(sq["late"]) > 1:
                sq["late"].pop(0)()
            return t

        r_read = []

        def norm_stat(n):
            while sq["late"]:
                sq["late"].pop(0)()
            bank = sq["bank"]
            done = sq["used"][sq["n"] - 1]
            t1 = act.put(lambda e: e.activation(R[:, :], bank[:, 0:T], ACT.Ln, bias=vec("eps"), scale=1.0 / n),
                         [done, t_vec] + list(r_read))
            abank.give(bank, [t1])
            t2 = act.put(lambda e: e.activation(R[:, :], R[:, :], ACT.Exp, scale=-0.5), [t1])
            r_read.clear()
            return t2

        s1 = ExitStack()
        MH = sb("MH", [128, KD, T], FR, s1)
        ML = sb("ML", [128, KD, T], FR, s1)
        sB = ExitStack()
        C1 = sb("C1", [128, 2, T], c=sB)
        MB = sb("MB", [128, 2, T], c=sB)
        GM = sb("GM", [128, 2, 128], c=sB)
        RC = sb("RC", [32, 2, T], c=sB)
        RP = sb("RP", [32, 32], c=sB)
        SCM = sb("SCM", [128, T], c=sB)
        UPW = sb("UPW", [32, 512], c=sB)
        GD = sb("GD", [32, T], c=sB)
        GQ = sb("GQ", [128, 2, T], c=sB)
        GK = sb("GK", [128, 2, T], c=sB)
        GV = sb("GV", [128, 4, T], c=sB)
        GR = sb("GR", [128, 4, T], c=sB)
        QKV = sb("QKV", [128, 3, 3, T], c=sB)
        t_c1 = load(C1[:, :, :], d["c_cnt"].rearrange("p (a t) -> p a t", a=2), q=act)
        t_mb = load(MB[:, :, :], d["c_bias"].rearrange("p (a t) -> p a t", a=2), q=act)
        t_gm = load(GM[:, :, :], d["c_gmask"].rearrange("p (a t) -> p a t", a=2), q=act)
        t_rc = load(RC[:, :, :], d["c_rope"].rearrange("p (a t) -> p a t", a=2), q=act)
        t_rp = load(RP[:, :], d["c_rot"][:, :], q=act)
        t_scm = load(SCM[:, :], d["c_scan"][:, :], q=act)
        t_up = load(UPW[:, :], d["gla_up"][:, :], q=act)
        act.put(lambda e: e.preload_act_table_set(SETS["logexp"]), inc=False)

        for k in range(KD):
            square(XT[:, k, :], [t_xts[k // 4]], k, KD)
            prep(k, XT[:, k, :], vec("norm1_g", k), [t_xts[k // 4], t_vec])
        t_r = norm_stat(D)

        def evac_r(dst, bank, ps, t, p1=128, after=()):
            tt = dve.put(lambda e: e.tensor_tensor(dst, ps[0:p1], R[0:p1, :], ALU.mult), [t, t_r] + list(after))
            mbank.give(bank, [tt])
            r_read[:] = [tt]
            return tt

        bank, ps, t = tile_k(A, t_a)
        t_gd = evac_r(GD[:, :], bank, ps, t, 32)
        t_g = {}
        for name, dst, n in (("q", GQ, 2), ("k", GK, 2), ("v", GV, 4), ("r", GR, 4)):
            for i in range(n):
                bank, ps, t = tile_k(A, t_a)
                t_g[name, i] = evac_r(dst[:, i, :], bank, ps, t)

        sG = ExitStack()
        BB, LS, E1, E2 = (XT[:, 4 * i:4 * i + 4, :] for i in range(4))
        KS = LS
        BL = sb("BL", [128, 4, 4], c=sG)
        DC = sb("DC", [128, 4, 4], c=sG)
        VN = sb("VN", [128, 4, 2, 128], c=sG)
        KN = sb("KN", [128, 4, 2, 128], c=sG)
        SS = sb("SS", [128, 4, 3, 128], c=sG)
        SM = TMP[:, :, :].rearrange("p s (a c) -> p s a c", a=2)
        sG_end, t_xt2 = [], []

        def gla():
            bz, fz = abank.take()
            bz2, fz2 = abank.take()
            for n in range(4):
                ps = (bz, bz2)[n // 2][:, (n % 2) * T:(n % 2) * T + T]
                t = pe.put(lambda e, n=n, ps=ps: e.matmul(ps, UPW[:, n * 128:n * 128 + 128], GD[:, :], start=True,
                                                          stop=True, skip_group_check=True),
                           [t_gd, t_up] + fz + fz2)
            yield
            for n in range(4):
                ps = (bz, bz2)[n // 2][:, (n % 2) * T:(n % 2) * T + T]
                tz = dve.put(lambda e, n=n, ps=ps: e.tensor_scalar(BB[:, n, :], ps, vec("gla_bias", n), None, ALU.add),
                             [t, t_vec])
            abank.give(bz, [tz])
            abank.give(bz2, [tz])
            t1 = act.put(lambda e: e.activation(LS[:, :, :], BB[:, :, :], ACT.Abs), [tz])
            t1 = act.put(lambda e: e.activation(E1[:, :, :], LS[:, :, :], ACT.Exp, scale=-1.0), [t1])
            t1 = act.put(lambda e: e.activation(E2[:, :, :], E1[:, :, :], ACT.Ln, bias=vec("one")), [t1])
            t2 = dve.put(lambda e: e.scalar_tensor_tensor(BB[:, :, :], BB[:, :, :], 0.0, E2[:, :, :], ALU.min,
                                                          ALU.subtract), [t1])
            t2 = dve.put(lambda e: e.tensor_scalar(LS[:, :, :], BB[:, :, :], 1.0 / 16.0, None, ALU.mult), [t2])
            yield
            for n in range(4):
                t3 = dve.put(lambda e, n=n: e.tensor_tensor_scan(BB[:, n, :], SCM[:, :], LS[:, n, :], 0.0, ALU.mult,
                                                                 ALU.add), [t2, t_scm])
            B4 = BB[:, :, :].rearrange("p n (c j) -> p n c j", c=4)
            t3 = dve.put(lambda e: e.tensor_copy(BL[:, :, :], B4[:, :, :, 63]), [t3])
            yield
            for n in (2, 3):
                t4 = dve.put(lambda e, n=n: e.tensor_tensor(LS[:, n, :], LS[:, n, :], BB[:, n, :], ALU.subtract), [t3])
            for n in (2, 3):
                for c in range(4):
                    cs = slice(64 * c, 64 * c + 64)
                    t5 = dve.put(lambda e, n=n, c=c, cs=cs: e.tensor_scalar(
                        BB[:, n, cs], LS[:, n, cs], BL[:, n, c:c + 1], None, ALU.add), [t4])
            yield
            t6 = act.put(lambda e: e.activation(E1[:, :, :], BB[:, :, :], ACT.Exp), [t5])
            t6 = act.put(lambda e: e.activation(E2[:, :, :], BB[:, :, :], ACT.Exp, scale=-1.0), [t5])
            t6d = act.put(lambda e: e.activation(DC[:, :, :], BL[:, :, :], ACT.Exp), [t3])
            for n in range(4):
                for c in range(4):
                    cs = slice(64 * c, 64 * c + 64)
                    t7 = act.put(lambda e, n=n, c=c, cs=cs: e.activation(
                        KS[:, n, cs], BB[:, n, cs], ACT.Exp, scale=-1.0, bias=BL[:, n, c:c + 1]), [t5])
                if n % 2:
                    yield
            for n in range(4):
                i = n % 2
                t8 = dve.put(lambda e, n=n, i=i: e.scalar_tensor_tensor(
                    E1[:, n, :], GQ[:, i, :], 0.125, E1[:, n, :], ALU.mult, ALU.mult), [t6, t_g["q", i]])
                t9 = dve.put(lambda e, n=n, i=i: e.tensor_tensor(E2[:, n, :], GK[:, i, :], E2[:, n, :], ALU.mult),
                             [t6, t_g["k", i]])
                t10 = dve.put(lambda e, n=n, i=i: e.tensor_tensor(KS[:, n, :], GK[:, i, :], KS[:, n, :], ALU.mult),
                              [t7])
            yield
            for src, dst, tk in ((GV, VN, t_g["v", 3]), (KS, KN, t10)):
                for half in range(2):
                    b, f = abank.take()
                    for m in range(2):
                        n = 2 * half + m
                        for tb in range(2):
                            t = pe.put(lambda e, b=b, m=m, tb=tb, n=n, src=src: e.transpose(
                                b[:, (2 * m + tb) * 128:(2 * m + tb) * 128 + 128],
                                src[:, n, tb * 128:tb * 128 + 128], IDENT[:, :]), [tk, t_ident] + f)
                    tc = act.put(lambda e, b=b, half=half, dst=dst: e.activation(
                        dst[:, 2 * half:2 * half + 2, :, :], b[:, :].rearrange("p (m s c) -> p m s c", m=2, s=2),
                        ACT.Copy), [t])
                    abank.give(b, [tc])
                yield
            t_s = {}
            for step_i in range(3):
                for n in range(4):
                    c = step_i if n < 2 else 3 - step_i
                    i = n % 2
                    tb, p0 = c // 2, 64 * (c % 2)
                    b, f = abank.take()
                    for hh in range(2):
                        t = pe.put(lambda e, b=b, hh=hh, n=n, tb=tb, p0=p0, i=i: e.matmul(
                            b[64 * hh:64 * hh + 64, 0:128], KN[p0:p0 + 64, n, tb, 64 * hh:64 * hh + 64],
                            VN[p0:p0 + 64, 2 * i + hh, tb, :], start=True, stop=True, skip_group_check=True),
                            [tc] + f)
                    if step_i == 0:
                        t_s[n, 0] = dve.put(lambda e, b=b, n=n: e.tensor_copy(SS[:, n, 0, :], b[:, 0:128]), [t])
                    else:
                        t_s[n, step_i] = dve.put(lambda e, b=b, n=n, k=step_i, c=c: e.scalar_tensor_tensor(
                            SS[:, n, k, :], SS[:, n, k - 1, :], DC[:, n, c:c + 1], b[:, 0:128], ALU.mult, ALU.add),
                            [t, t_s[n, step_i - 1], t6d])
                    abank.give(b, [t_s[n, step_i]])
                yield
            sm_free = [[], []]
            for h in range(4):
                i, hp = h // 2, 64 * (h % 2)
                bo, fo = abank.take()
                first = True
                for tb in range(2):
                    b, f = abank.take()
                    for dr in range(2):
                        n = 2 * dr + i
                        t = pe.put(lambda e, b=b, dr=dr, n=n, tb=tb, hp=hp: e.matmul(
                            b[:, dr * 128:dr * 128 + 128], E2[hp:hp + 64, n, tb * 128:tb * 128 + 128],
                            E1[hp:hp + 64, n, tb * 128:tb * 128 + 128], start=True, stop=True,
                            skip_group_check=True), [t8, t9] + f)
                    tm = dve.put(lambda e, b=b, tb=tb: e.tensor_tensor(
                        SM[:, tb, :, :], b[:, 0:256].rearrange("p (a c) -> p a c", a=2), GM[:, :, :], ALU.mult),
                        [t, t_gm] + sm_free[tb])
                    abank.give(b, [tm])
                    tm = dve.put(lambda e, tb=tb: e.tensor_tensor(SM[:, tb, 0, :], SM[:, tb, 0, :], SM[:, tb, 1, :],
                                                                  ALU.add), [tm])
                    yield
                    t = pe.put(lambda e, bo=bo, h=h, tb=tb, first=first: e.matmul(
                        bo[:, tb * 128:tb * 128 + 128], VN[:, h, tb, :], SM[:, tb, 0, :], start=first, stop=False,
                        skip_group_check=True), [tm] + fo)
                    sm_free[tb] = [t]
                    first = False
                for dr in range(2):
                    n = 2 * dr + i
                    for k in range(3):
                        c = k + 1 if dr == 0 else 2 - k
                        t = pe.put(lambda e, bo=bo, n=n, k=k, c=c, hp=hp: e.matmul(
                            bo[:, 64 * c:64 * c + 64], SS[hp:hp + 64, n, k, :], E1[hp:hp + 64, n, 64 * c:64 * c + 64],
                            start=False, stop=False, skip_group_check=True), [t_s[n, k]])
                OT = GV[:, h, :]
                to = act.put(lambda e, bo=bo, OT=OT: e.activation(OT, bo[:, 0:T], ACT.Copy), [t])
                ts = act.put(lambda e, bo=bo, i=i, h=h: e.activation(BB[:, h, :], bo[:, 0:T], ACT.Square), [t])
                abank.give(bo, [to, ts])
                yield
                b, f = abank.take()
                t = pe.put(lambda e, b=b, h=h: e.matmul(b[:, 0:T], ONES[:, :], BB[:, h, :], start=True, stop=True),
                           [ts] + f)
                t1 = act.put(lambda e, b=b, h=h: e.activation(BB[:, h, :], b[:, 0:T], ACT.Ln, bias=vec("eps"),
                                                              scale=1.0 / 128), [t])
                abank.give(b, [t1])
                t1 = act.put(lambda e, h=h: e.activation(BB[:, h, :], BB[:, h, :], ACT.Exp, scale=-0.5), [t1])
                t2 = act.put(lambda e, h=h: e.activation(KS[:, h, :], GR[:, h, :], ACT.Exp, scale=-1.0),
                             [t_g["r", h], tc])
                t3 = dve.put(lambda e, h=h: e.tensor_scalar(KS[:, h, :], KS[:, h, :], 1.0, None, ALU.add), [t2])
                t3 = dve.put(lambda e, h=h: e.reciprocal(KS[:, h, :], KS[:, h, :]), [t3])
                t3 = dve.put(lambda e, h=h: e.tensor_tensor(GR[:, h, :], GR[:, h, :], KS[:, h, :], ALU.mult), [t3])
                yield
                t4 = dve.put(lambda e, h=h, OT=OT: e.scalar_tensor_tensor(
                    OT, OT, vec("gla_out_g", h), BB[:, h, :], ALU.mult, ALU.mult), [to, t1])
                t4 = dve.put(lambda e, h=h, OT=OT: e.tensor_tensor(OT, OT, GR[:, h, :], ALU.mult), [t4, t3])
                th = act.put(lambda e, h=h, OT=OT: e.activation(MH[:, h, :], OT, ACT.Copy), [t4])
                tl = dve.put(lambda e, h=h, OT=OT: e.tensor_tensor(ML[:, h, :], OT, MH[:, h, :].bitcast(F32),
                                                                   ALU.subtract), [th])
                t_m[h] = [th, tl]
                yield
            sG_end[:] = [(pe.sem, pe.count), (act.sem, act.count), (dve.sem, dve.count)]
            t_xt2[:] = [load(XT[:, :, :], d["xt"].rearrange("p (k t) -> p k t", k=KD), sG_end, q=act)]

        t_m = {}
        gen_gla = gla()
        bg.append(gen_gla)
        sG.close()
        sA = ExitStack()
        ASQ = sb("ASQ", [128, 2, T], c=sA)
        ALG = TMP[:, :, :].rearrange("p a t -> p (a t)")
        ARR = sb("ARR", [128, 2, T], c=sA)
        AT1 = sb("AT1", [32, 2, T], c=sA)
        ASM = sb("ASM", [128, 2, T], c=sA)
        AP_ = sb("AP_", [128, 2, T], c=sA)
        APT = sb("APT", [128, 2, T], c=sA)
        AVN = sb("AVN", [128, 2, 128], c=sA)
        ANM = sb("ANM", [128, 2], c=sA)
        ADN = sb("ADN", [128, 2], c=sA)
        ARD = sb("ARD", [128, 2], c=sA)
        av = {"pt": [], "vn": [], "p": []}

        def attn(h, tq):
            s = h % 3
            qk = QKV[:, s, 0:2, :]
            qkf = qk.rearrange("p a t -> p (a t)")
            pre = list(sG_end)
            t = act.put(lambda e: e.activation(ASQ[:, :, :], qk, ACT.Square), [tq[0], tq[1]] + pre)
            bv, fv = abank.take()
            for kt in range(2):
                tv = pe.put(lambda e, kt=kt: e.transpose(bv[:, kt * 128:kt * 128 + 128],
                                                         QKV[:, s, 2, kt * 128:kt * 128 + 128], IDENT[:, :]),
                            [tq[2]] + fv)
            b, f = abank.take()
            t = pe.put(lambda e: e.matmul(b[:, :], ONES[:, :], ASQ[:, :, :].rearrange("p a t -> p (a t)"),
                                          start=True, stop=True), [t] + f)
            tvn = act.put(lambda e: e.activation(AVN[:, :, :], bv[:, 0:256].rearrange("p (a c) -> p a c", a=2),
                                                 ACT.Copy), [tv] + av["vn"] + pre)
            abank.give(bv, [tvn])
            t = act.put(lambda e: e.activation(ALG, b[:, :], ACT.Ln, bias=vec("eps"), scale=1.0 / 128), [t] + pre)
            abank.give(b, [t])
            t = act.put(lambda e: e.activation(ARR[:, :, :].rearrange("p a t -> p (a t)"), ALG, ACT.Exp,
                                               scale=-0.5), [t])
            yield
            for a, g in ((0, "q_norm_g"), (1, "k_norm_g")):
                tn = dve.put(lambda e, a=a, g=g: e.scalar_tensor_tensor(
                    QKV[:, s, a, :], QKV[:, s, a, :], vec(g), ARR[:, a, :], ALU.mult, ALU.mult), [t])
            b, f = abank.take()
            t = pe.put(lambda e: e.matmul(b[0:32, :], RP[:, :], qkf[0:32], start=True, stop=True), [tn, t_rp] + f)
            yield
            t1 = dve.put(lambda e: e.tensor_tensor(
                AT1[:, :, :], b[0:32, :].rearrange("p (a t) -> p a t", a=2),
                RC[:, 1, :].unsqueeze(1).broadcast_to([32, 2, T]), ALU.mult), [t, t_rc] + pre)
            abank.give(b, [t1])
            t2 = dve.put(lambda e: e.tensor_tensor(
                qk[0:32], qk[0:32], RC[:, 0, :].unsqueeze(1).broadcast_to([32, 2, T]), ALU.mult), [t])
            t2 = dve.put(lambda e: e.tensor_tensor(qk[0:32], qk[0:32], AT1[:, :, :], ALU.add), [t1, t2])
            b, f = abank.take()
            for qt in range(2):
                t = pe.put(lambda e, qt=qt: e.matmul(b[:, qt * T:qt * T + T], QKV[:, s, 0, qt * 128:qt * 128 + 128],
                                                     QKV[:, s, 1, :], start=True, stop=True, skip_group_check=True),
                           [t2] + f)
            t_qk = t
            yield
            t = dve.put(lambda e: e.scalar_tensor_tensor(
                ASM[:, :, :].rearrange("p a t -> p (a t)"), b[:, :], float(128 ** -0.5),
                MB[:, :, :].rearrange("p a t -> p (a t)"), ALU.mult, ALU.add), [t_qk, t_mb] + pre)
            abank.give(b, [t])
            t = dve.put(lambda e: e.tensor_reduce(ANM[:, :], ASM[:, :, :], AX.X, ALU.max, negate=True), [t] + pre)
            for qt in range(2):
                t1 = act.put(lambda e, qt=qt: e.activation(AP_[:, qt, :], ASM[:, qt, :], ACT.Exp,
                                                           bias=ANM[:, qt:qt + 1]), [t] + av["p"] + pre)
            for qt in range(2):
                t2 = dve.put(lambda e, qt=qt: e.tensor_tensor_reduce(
                    AP_[:, qt, :], AP_[:, qt, :], C1[:, qt, :], 1.0, 0.0, ALU.mult, ALU.add, ADN[:, qt:qt + 1]),
                    [t1, t_c1])
            t2 = dve.put(lambda e: e.reciprocal(ARD[:, :], ADN[:, :]), [t2])
            for qt in range(2):
                t3 = dve.put(lambda e, qt=qt: e.tensor_scalar(AP_[:, qt, :], AP_[:, qt, :], ARD[:, qt:qt + 1], None,
                                                              ALU.mult), [t2])
            yield
            b, f = abank.take()
            for kt in range(2):
                for qt in range(2):
                    t = pe.put(lambda e, kt=kt, qt=qt: e.transpose(
                        b[:, kt * T + qt * 128:kt * T + qt * 128 + 128], AP_[:, qt, kt * 128:kt * 128 + 128],
                        IDENT[:, :]), [t3] + f)
            av["p"] = [t]
            t = act.put(lambda e: e.activation(APT[:, :, :].rearrange("p a t -> p (a t)"), b[:, :], ACT.Copy),
                        [t] + av["pt"] + pre)
            abank.give(b, [t])
            yield
            b, f = abank.take()
            for kt in range(2):
                to = pe.put(lambda e, kt=kt: e.matmul(b[:, 0:T], AVN[:, kt, :], APT[:, kt, :], start=(kt == 0),
                                                      stop=(kt == 1)), [t, tvn] + f)
            av["pt"] = [to]
            av["vn"] = [to]
            th = act.put(lambda e: e.activation(MH[:, 4 + h, :], b[:, 0:T], ACT.Copy), [to])
            tl = dve.put(lambda e: e.tensor_tensor(ML[:, 4 + h, :], b[:, 0:T], MH[:, 4 + h, :].bitcast(F32),
                                                   ALU.subtract), [th])
            abank.give(b, [tl])
            t_m[4 + h] = [th, tl]
            qkv_free[s] = [t_qk, tv]
            yield

        qkv_free = [[], [], []]
        gens = []
        for h in range(12):
            if h >= 3:
                drain(gens[h - 3])
            tq = []
            for j in range(3):
                bank, ps, t = tile_k(A, t_a, steps=2 if h < 9 else 3)
                tq.append(evac_r(QKV[:, h % 3, j, :], bank, ps, t, after=qkv_free[h % 3]))
            gens.append(attn(h, tq))
            bg.append(gens[h])
        drain()
        end_b1 = [(pe.sem, pe.count), (act.sem, act.count), (dve.sem, dve.count)]
        sA.close()
        sB.close()

        a_free = [t_used[st["used"] - 1]]

        def out_tiles(n_tiles, src, ticks, nk, evac):
            for n in range(n_tiles):
                bank, ps, t = tile_k(src, ticks, nk)
                evac(n, bank, ps, t)

        def resid(n, bank, ps, t):
            tx = dve.put(lambda e: e.tensor_tensor(XT[:, n, :], XT[:, n, :], ps, ALU.add), [t] + t_xt2)
            mbank.give(bank, [tx])
            square(XT[:, n, :], [tx], n, KD)
            prep(n, XT[:, n, :], vec("norm2_g", n), [tx], a_free)

        out_tiles(16, (MH, ML), t_m, 16, resid)
        t_r = norm_stat(D)
        end_m = [(pe.sem, pe.count), (act.sem, act.count), (dve.sem, dve.count)]
        s1.close()

        sP = ExitStack()
        NP = max(n for _, n in PARTS)
        GA = sb("GA", [128, NP, T], c=sP)
        I1T = sb("I1T", [128, T], c=sP)
        I2T = sb("I2T", [128, T], c=sP)
        GTT = sb("GTT", [128, T], c=sP)
        IOTA = sb("IOTA", [128, 128], c=sP)
        t_iota = load(IOTA[:, :], d["c_iota"][:, :], end_b1 + end_m, q=act)
        sQ = ExitStack()
        QY = GA[:, 48:64, :]
        SK = GA[:, 24:32, :].rearrange("p n t -> p (n t)").rearrange("p (c k) -> p c k", c=16)
        SC = GA[:, 32:48, :].rearrange("p n t -> p (n t)").rearrange("p (a c k) -> p a c k", a=2, c=16)
        TV = sb("TV", [128, 2, 16, 16], c=sQ)
        TI = sb("TI", [128, 16, 16], U32, c=sQ)
        TF = sb("TF", [128, 2, 16, 16], c=sQ)
        BV = sb("BV", [128, 2, 8, 16], c=sQ)
        BPI = sb("BPI", [128, 128], U32, c=sQ)
        BPX = sb("BPX", [128, 2, 128], U32, c=sQ)
        BPF = sb("BPF", [128, 2, 128], c=sQ)
        CD = sb("CD", [128, 16, 16], c=sQ)
        EQ = GA[:, 48:56, :].rearrange("p n t -> p (n t)").rearrange("p (c k) -> p c k", k=16)
        IX = sb("IX", [128, 3, 128], c=sQ)
        ES = sb("ES", [128, 16], c=sQ)
        t_sk = load(SK[:, :, :], d["sub_keys"].rearrange("p (c k) -> p c k", c=16), end_b1 + end_m, q=act)
        t_q = {}

        def evac_q(n, bank, ps, t):
            t_q[n] = evac_r(QY[:, n, :], bank, ps, t, after=end_b1 + end_m)

        out_tiles(16, A, t_a, 16, evac_q)
        qy_done = []
        sc_done = []

        def topk():
            t_sc = {}
            for q in range(4):
                for a in range(2):
                    b, f = abank.take()
                    for c in range(4):
                        hc = 4 * q + c
                        t = pe.put(lambda e, b=b, c=c, hc=hc, a=a: e.matmul(
                            b[:, c * 128:c * 128 + 128], QY[:, hc, a * 128:a * 128 + 128], SK[:, hc, :], start=True,
                            stop=True, skip_group_check=True), [t_q[hc], t_sk] + f)
                    qy_done[:] = [t]
                    tc = act.put(lambda e, b=b, q=q, a=a: e.activation(
                        SC[:, a, 4 * q:4 * q + 4, :], b[:, :].rearrange("p (c k) -> p c k", c=4), ACT.Copy), [t])
                    abank.give(b, [tc])
                    for c in range(4):
                        t_sc[a, 4 * q + c] = tc
                yield
            st["qy"] = True
            t_ix = []
            for a in range(2):
                for hc in range(16):
                    v = SC[:, a, hc, :]
                    m1, m2 = TV[:, a, hc, 0:8], TV[:, a, hc, 8:16]
                    i1, i2 = TI[:, hc, 0:8], TI[:, hc, 8:16]
                    t = dve.put(lambda e, v=v, m1=m1: e.max(m1, v), [t_sc[a, hc]])
                    t = dve.put(lambda e, v=v, m1=m1, i1=i1: e.max_index(i1, m1, v), [t] + t_ix)
                    t = dve.put(lambda e, v=v, m1=m1: e.match_replace(v, m1, v, NEG), [t])
                    t = dve.put(lambda e, v=v, m2=m2: e.max(m2, v), [t])
                    t = dve.put(lambda e, v=v, m2=m2, i2=i2: e.max_index(i2, m2, v), [t])
                    yield
                t = dve.put(lambda e, a=a: e.tensor_copy(TF[:, a, :, :], TI[:, :, :]), [t])
                t_tf = t
                for h in range(8):
                    t = dve.put(lambda e, a=a, h=h: e.tensor_tensor(
                        CD[:, :, :], TV[:, a, 2 * h, :].unsqueeze(2).broadcast_to([128, 16, 16]),
                        TV[:, a, 2 * h + 1, :].unsqueeze(1).broadcast_to([128, 16, 16]), ALU.add), [t])
                    v = CD[:, :, :].rearrange("p a b -> p (a b)")
                    m1, m2 = BV[:, a, h, 0:8], BV[:, a, h, 8:16]
                    i1, i2 = BPI[:, 16 * h:16 * h + 8], BPI[:, 16 * h + 8:16 * h + 16]
                    t = dve.put(lambda e, v=v, m1=m1: e.max(m1, v), [t])
                    t = dve.put(lambda e, v=v, m1=m1, i1=i1: e.max_index(i1, m1, v), [t])
                    t = dve.put(lambda e, v=v, m1=m1: e.match_replace(v, m1, v, NEG), [t])
                    t = dve.put(lambda e, v=v, m2=m2: e.max(m2, v), [t])
                    t = dve.put(lambda e, v=v, m2=m2, i2=i2: e.max_index(i2, m2, v), [t])
                    yield
                t = dve.put(lambda e: e.tensor_single_scalar(BPX[:, 0, :], BPI[:, :], 4, ALU.logical_shift_right), [t])
                t = dve.put(lambda e: e.tensor_single_scalar(BPX[:, 1, :], BPI[:, :], 15, ALU.bitwise_and), [t])
                t = dve.put(lambda e: e.tensor_copy(BPF[:, :, :], BPX[:, :, :]), [t])
                for c in range(2):
                    t = dve.put(lambda e, c=c: e.tensor_tensor(
                        EQ[:, :, :], BPF[:, c, :].unsqueeze(2).broadcast_to([128, 128, 16]),
                        IOTA[:, 0:16].unsqueeze(1).broadcast_to([128, 128, 16]), ALU.is_equal), [t, t_iota] + qy_done)
                    yield
                    for h in range(8):
                        t2 = dve.put(lambda e, c=c, a=a, h=h: e.tensor_tensor(
                            EQ[:, 16 * h:16 * h + 16, :], EQ[:, 16 * h:16 * h + 16, :],
                            TF[:, a, 2 * h + c, :].unsqueeze(1).broadcast_to([128, 16, 16]), ALU.mult), [t, t_tf])
                    t = t2
                    yield
                    t = dve.put(lambda e, c=c: e.tensor_reduce(IX[:, c, :], EQ[:, :, :], AX.X, ALU.add), [t] + t_ix)
                    yield
                bv = BV[:, a, :, :]
                G3 = IX[:, 2, :].rearrange("p (h k) -> p h k", h=8)
                t = dve.put(lambda e, bv=bv, G3=G3, a=a: e.tensor_tensor(
                    G3, bv, BV[:, a, :, 0:1].broadcast_to([128, 8, 16]), ALU.subtract), [t] + t_ix)
                t = act.put(lambda e: e.activation(IX[:, 2, :], IX[:, 2, :], ACT.Exp), [t])
                t = dve.put(lambda e, G3=G3: e.tensor_reduce(ES[:, 0:8], G3, AX.X, ALU.add), [t])
                t = dve.put(lambda e: e.reciprocal(ES[:, 8:16], ES[:, 0:8]), [t])
                t = dve.put(lambda e, G3=G3: e.tensor_tensor(
                    G3, G3, ES[:, 8:16].unsqueeze(2).broadcast_to([128, 8, 16]), ALU.mult), [t])
                yield
                b, f = abank.take()
                for c in range(3):
                    tp = pe.put(lambda e, b=b, c=c: e.transpose(b[:, c * 128:c * 128 + 128], IX[:, c, :], IDENT[:, :]),
                                [t] + f)
                t_ix = [tp]
                for c, dst in enumerate((I1T, I2T, GTT)):
                    t_idx[a, c] = act.put(lambda e, b=b, c=c, dst=dst, a=a: e.activation(
                        dst[:, a * 128:a * 128 + 128], b[:, c * 128:c * 128 + 128], ACT.Copy), [tp])
                abank.give(b, [t_idx[a, 2]])
                yield

        t_idx = {}
        gen_topk = topk()
        bg.append(gen_topk)
        tmp_free = [[], []]
        ga_free = {}
        c_free = [[], []]
        sO = ExitStack()
        late = {}

        for pi, (p0, n) in enumerate(PARTS):
            t_act = {}
            for jj in range(n):
                bank, ps, t = tile_k(A, t_a, steps=2)
                s = jj % 2
                tt = dve.put(lambda e, s=s, ps=ps: e.tensor_tensor(TMP[:, s, :], ps, R[:, :], ALU.mult),
                             [t, t_r] + tmp_free[s])
                mbank.give(bank, [tt])
                r_read[:] = [tt]
                if pi == 0 and jj == 32:
                    drain(gen_topk)
                    sc_done = [(dve.sem, dve.count), (act.sem, act.count)]
                extra = ga_free.get(jj, []) + (end_b1 + end_m if pi == 0 else [])
                if pi == 0 and jj >= 24:
                    assert st["qy"]
                    extra += qy_done
                if pi == 0 and jj >= 32:
                    extra += sc_done
                ta = act.put(lambda e, s=s, jj=jj: e.activation(GA[:, jj, :], TMP[:, s, :], ACT.Gelu_apprx_tanh),
                             [tt] + extra)
                tmp_free[s] = [ta]
                t_act[jj] = ta
            if pi == 0:
                drain(gen_topk)
                end_q = [(pe.sem, pe.count), (act.sem, act.count), (dve.sem, dve.count)]
                sQ.close()
                NB = 8
                OA = sb("OA", [128, 2, NB, 128], c=sO)
                OB = sb("OB", [128, 2, NB, NP], c=sO)
                sO.close()
                sO = ExitStack()
                CH = sb("CH", [128, 2, T], FR, c=sO)
                CL = sb("CL", [128, 2, T], FR, c=sO)
                ob_free = [list(end_q), list(end_q)]
            for q in range(T // NB):
                s = q % 2
                b, f = abank.take()
                for k in range(NB):
                    tok = q * NB + k
                    a = tok // 128
                    ti = [t_idx[a, 0], t_idx[a, 1], t_idx[a, 2]]
                    tA = dve.put(lambda e, s=s, k=k, tok=tok: e.tensor_scalar(
                        OA[:, s, k, :], IOTA[:, :], I1T[:, tok:tok + 1], GTT[:, tok:tok + 1], ALU.is_equal,
                        ALU.mult), ti + ob_free[s])
                    tB = pool.put(lambda e, s=s, k=k, tok=tok, p0=p0, n=n: e.tensor_scalar(
                        OB[:, s, k, 0:n], IOTA[:, p0:p0 + n], I2T[:, tok:tok + 1], None, ALU.is_equal),
                        ti + ob_free[s] + [t_iota])
                    t = pe.put(lambda e, b=b, s=s, k=k, n=n: e.matmul(
                        b[:, k * n:k * n + n], OA[:, s, k, :], OB[:, s, k, 0:n], start=True, stop=True,
                        skip_group_check=True), [tA, tB] + f)
                ob_free[s] = [t]
                G = GA[:, 0:n, q * NB:q * NB + NB].rearrange("p j t -> p t j")
                tm = dve.put(lambda e, G=G, b=b, n=n: e.tensor_tensor(
                    G, G, b[:, 0:NB * n].rearrange("p (t j) -> p t j", j=n), ALU.mult), [t, t_act[n - 1]])
                abank.give(b, [tm])
            c_free = [[t, tm], [t, tm]]
            taken = [mbank.take() for _ in range(4)] + [abank.take() for _ in range(4)]
            freed = [x for _, f in taken for x in f]
            for jj in range(n):
                s = jj % 2
                th = act.put(lambda e, s=s, jj=jj: e.activation(CH[:, s, :], GA[:, jj, :], ACT.Copy),
                             [tm] + c_free[s])
                tl = dve.put(lambda e, s=s, jj=jj: e.tensor_tensor(CL[:, s, :], GA[:, jj, :],
                                                                   CH[:, s, :].bitcast(F32), ALU.subtract),
                             [th] + c_free[s])
                ga_free[jj] = [th, tl]
                marks = [[] for _ in range(16)]
                jobs = []
                for dt in range(16):
                    ps = taken[dt // 2][0][:, (dt % 2) * T:(dt % 2) * T + T]
                    jobs.append((ps, dt, CH[:, s, :], CL[:, s, :], jj == 0 and dt % 2 == 0, jj == n - 1,
                                 [th, tl] + (freed if jj == 0 else []), None))
                t = chunk(jobs)
                c_free[s] = [t]
            ob_free = [[t], [t]]
            t_x = {}
            for dt in range(16):
                ps = taken[dt // 2][0][:, (dt % 2) * T:(dt % 2) * T + T]
                t_x[dt] = dve.put(lambda e, dt=dt, ps=ps: e.tensor_tensor(XT[:, dt, :], XT[:, dt, :], ps, ALU.add),
                                  [t])
                if dt % 2:
                    (mbank if dt < 8 else abank).give(taken[dt // 2][0], [t_x[dt]])
        end_p = [(pe.sem, pe.count), (act.sem, act.count), (dve.sem, dve.count), (pool.sem, pool.count)]
        a_free = [t_used[st["used"] - 1]]
        sO.close()
        sP.close()

        s2 = ExitStack()
        PH = sb("PH", [128, 2, T], FR, c=s2)
        PL = sb("PL", [128, 2, T], FR, c=s2)
        INV = sb("INV", [128, 4, 16], c=s2)
        SP8 = sb("SP8", [128, 3, 32], c=s2)
        t_inv = load(INV[:, :, :], d["c_inv"].rearrange("p (g t) -> p g t", g=4), end_p)
        act.put(lambda e: e.preload_act_table_set(SETS["logexp"]), inc=False)
        Lv = VEC[:, VOFF["lru_L_2"]:VOFF["lru_L_2"] + 32]
        E_, Y_, M_ = SP8[:, 0, :], SP8[:, 1, :], SP8[:, 2, :]
        t = act.put(lambda e: e.activation(Y_, Lv, ACT.Abs), end_p)
        t = act.put(lambda e: e.activation(E_, Y_, ACT.Exp, scale=-1.0), [t])
        t = dve.put(lambda e: e.tensor_scalar(Y_, E_, 1.0, None, ALU.add), [t])
        t1 = act.put(lambda e: e.activation(M_, Y_, ACT.Ln), [t] + end_p)
        t2 = dve.put(lambda e: e.scalar_tensor_tensor(E_, Y_, -1.0, E_, ALU.add, ALU.subtract), [t1])
        t2 = dve.put(lambda e: e.reciprocal(Y_, Y_), [t2])
        t2 = dve.put(lambda e: e.tensor_tensor(E_, E_, Y_, ALU.mult), [t2])
        t2 = dve.put(lambda e: e.tensor_tensor(M_, M_, E_, ALU.subtract), [t2])
        t2 = dve.put(lambda e: e.tensor_scalar(Y_, Lv, -1.0, 0.0, ALU.mult, ALU.max), [t2])
        t2 = dve.put(lambda e: e.tensor_tensor(Y_, Y_, M_, ALU.add), [t2])
        t2 = dve.put(lambda e: e.tensor_scalar(M_, Y_, -8.0, None, ALU.mult), [t2])
        t_sp = dve.put(lambda e: e.tensor_scalar(Y_, Y_, 8.0, None, ALU.mult), [t2])

        for k in range(KD):
            square(XT[:, k, :], [t_x[k]], k, KD)
            prep(k, XT[:, k, :], vec("g_pre_2", k), [t_x[k]], a_free)
        t_r = norm_stat(D)

        def marks_now():
            return [(pe.sem, pe.count), (act.sem, act.count), (dve.sem, dve.count)]

        prev = list(end_p)
        for l in range(2):
            sY = ExitStack()
            YH = sb(f"YH{l}", [128, 32, T], FR, c=sY)
            YL = sb(f"YL{l}", [128, 32, T], FR, c=sY)
            s3 = ExitStack()
            PT = sb(f"PT{l}", [128, 2, T], c=s3)
            t_pt = load(PT[:, :, :], d["p_2"].rearrange("p (l k t) -> p l k t", l=2, k=2)[:, l], prev)
            th = act.put(lambda e, PT=PT: e.activation(PH[:, :, :], PT[:, :, :], ACT.Copy), [t_pt] + prev)
            t_p2 = dve.put(lambda e, PT=PT: e.tensor_tensor(PL[:, :, :], PT[:, :, :], PH[:, :, :].bitcast(F32),
                                                            ALU.subtract), [th] + prev)
            s3.close()
            prev = prev + [t_p2]
            sU = ExitStack()
            t_y = {}
            if l == 0:
                DH = sb("DH", [128, 8, T], FR, c=sU)
                DL = sb("DL", [128, 8, T], FR, c=sU)
                ZS = sb("ZS", [128, 4, T], c=sU)
                UP = sb("UP", [128, 3, 16 + T], c=sU)
                t = dve.put(lambda e: e.memset(UP[:, :, 0:16], 0.0), prev)
                t_up0 = t
                d_free = []
                for g in range(4):
                    w = 2 << g
                    t_d = {}
                    for i in range(8):
                        bank, ps, t = tile_k(A, t_a)
                        U = UP[:, 0, 16:16 + T]
                        t = dve.put(lambda e, ps=ps, U=U: e.tensor_tensor(U, ps, R[:, :], ALU.mult), [t, t_r, t_up0])
                        mbank.give(bank, [t])
                        src = 0
                        for k in range(g + 1):
                            dst = 1 + k % 2
                            sh = 1 << k
                            t = dve.put(lambda e, src=src, dst=dst, sh=sh: e.tensor_tensor(
                                UP[:, dst, 16:16 + T], UP[:, src, 16:16 + T], UP[:, src, 16 - sh:16 + T - sh],
                                ALU.add), [t])
                            src = dst
                        s = i % 2
                        t2 = dve.put(lambda e, src=src, s=s, w=w: e.scalar_tensor_tensor(
                            TMP[:, s, :], UP[:, src, 16:16 + T], 1.0 / w, UP[:, 0, 16:16 + T], ALU.mult,
                            ALU.subtract), [t] + tmp_free[s])
                        t = dve.put(lambda e, src=src, g=g: e.tensor_tensor(
                            UP[:, src, 16:32], UP[:, src, 16:32], INV[:, g, :], ALU.mult), [t2, t_inv])
                        t = dve.put(lambda e, src=src, s=s: e.tensor_tensor(
                            TMP[:, s, 0:16], UP[:, src, 16:32], UP[:, 0, 16:32], ALU.subtract), [t])
                        th = act.put(lambda e, s=s, i=i: e.activation(DH[:, i, :], TMP[:, s, :], ACT.Copy),
                                     [t] + d_free + prev)
                        tl = dve.put(lambda e, s=s, i=i: e.tensor_tensor(DL[:, i, :], TMP[:, s, :],
                                                                        DH[:, i, :].bitcast(F32), ALU.subtract),
                                     [th])
                        tmp_free[s] = [th]
                        t_d[i] = [th, tl]
                    t_z = {}
                    for half in range(2):
                      for i in range(4 * half, 4 * half + 4):
                          bank, ps, t = tile_k(A, t_a)
                          t = dve.put(lambda e, ps=ps, i=i: e.tensor_tensor(ZS[:, i % 4, :], ps, R[:, :], ALU.mult),
                                      [t, t_r])
                          mbank.give(bank, [t])
                          r_read[:] = [t]
                          t_z[i] = act.put(lambda e, i=i: e.activation(ZS[:, i % 4, :], ZS[:, i % 4, :], ACT.Silu), [t])
                      for c in range(2 * half, 2 * half + 2):
                          jobs = []
                          held = []
                          for o in range(2):
                              bank, freed = mbank.take()
                              mark = [None]
                              held.append((bank, mark))
                              for k in range(8):
                                  jobs.append((bank[:, 0:T], o * 8 + k, DH[:, k, :], DL[:, k, :], k == 0, k == 7,
                                               freed + t_d[k], mark if k == 7 else None))
                          d_free = [chunk(jobs)]
                          for o in range(2):
                              i = 2 * c + o
                              n = 8 * g + i
                              bank, mark = held[o]
                              ps = bank[:, 0:T]
                              s = i % 2
                              t = dve.put(lambda e, ps=ps, s=s, n=n: e.tensor_scalar(
                                  TMP[:, s, :], ps, vec("pool_b_2", n), vec("pool_scale_2", n), ALU.add, ALU.mult),
                                  [mark[-1]] + tmp_free[s])
                              mbank.give(bank, [t])
                              t = dve.put(lambda e, s=s, i=i: e.tensor_tensor(TMP[:, s, :], TMP[:, s, :], ZS[:, i % 4, :],
                                                                             ALU.mult), [t, t_z[i]])
                              th = act.put(lambda e, s=s, n=n, YH=YH: e.activation(YH[:, n, :], TMP[:, s, :], ACT.Copy),
                                           [t] + prev)
                              tl = dve.put(lambda e, s=s, n=n, YH=YH, YL=YL: e.tensor_tensor(
                                  YL[:, n, :], TMP[:, s, :], YH[:, n, :].bitcast(F32), ALU.subtract), [th])
                              tmp_free[s] = [th]
                              t_y[n] = [th, tl]
            else:
                UP = sb("UQ", [128, 4 + T], c=sU)
                UC = sb("UC", [128, 4, T], c=sU)
                ZB = sb("ZB", [128, 4, T], c=sU)
                RG = sb("RG", [128, 4, T], c=sU)
                IG = sb("IG", [128, 4, T], c=sU)
                t = dve.put(lambda e: e.memset(UP[:, 0:4], 0.0), prev)
                for g in range(8):
                    UH, UL = YH[:, 4 * g:4 * g + 4, :], YL[:, 4 * g:4 * g + 4, :]
                    t_d = {}
                    for i in range(4):
                        n = 4 * g + i
                        bank, ps, t = tile_k(A, t_a)
                        t = dve.put(lambda e, ps=ps: e.tensor_tensor(UP[:, 4:4 + T], ps, R[:, :], ALU.mult),
                                    [t, t_r, (dve.sem, dve.count)])
                        mbank.give(bank, [t])
                        t = dve.put(lambda e, i=i, n=n: e.tensor_scalar(
                            UC[:, i, :], UP[:, 4:4 + T], vec("conv_w_2", 96 + n), vec("conv_b_2", n), ALU.mult,
                            ALU.add), [t])
                        for k in (2, 1, 0):
                            t = dve.put(lambda e, i=i, n=n, k=k: e.scalar_tensor_tensor(
                                UC[:, i, :], UP[:, 1 + k:1 + k + T], vec("conv_w_2", 32 * k + n), UC[:, i, :],
                                ALU.mult, ALU.add), [t])
                        th = act.put(lambda e, i=i, UH=UH: e.activation(UH[:, i, :], UC[:, i, :], ACT.Copy),
                                     [t] + prev)
                        tl = dve.put(lambda e, i=i, UH=UH, UL=UL: e.tensor_tensor(UL[:, i, :], UC[:, i, :],
                                                                    UH[:, i, :].bitcast(F32), ALU.subtract), [th])
                        t_d[i] = [th, tl]
                    for i in range(4):
                        bank, ps, t = tile_k(A, t_a)
                        t_zz = dve.put(lambda e, ps=ps, i=i: e.tensor_tensor(ZB[:, i, :], ps, R[:, :], ALU.mult),
                                       [t, t_r])
                        mbank.give(bank, [t_zz])
                        r_read[:] = [t_zz]
                        s = i % 2
                        ts = act.put(lambda e, i=i, s=s: e.activation(TMP[:, s, :], ZB[:, i, :], ACT.Sigmoid),
                                     [t_zz] + tmp_free[s])
                        tz = dve.put(lambda e, i=i, s=s: e.tensor_tensor(ZB[:, i, :], ZB[:, i, :], TMP[:, s, :],
                                                                         ALU.mult), [ts])
                        tmp_free[s] = [tz]
                    jobs = []
                    held = []
                    for hh in range(2):
                        for ax in range(2):
                            bank, freed = mbank.take()
                            held.append(bank)
                            for o in range(2):
                                for k in range(2):
                                    jobs.append((bank[:, o * T:o * T + T], ((hh * 2 + ax) * 2 + k) * 2 + o,
                                                 UH[:, 2 * hh + k, :], UL[:, 2 * hh + k, :], k == 0 and o == 0,
                                                 k == 1, freed + t_d[2 * hh + k], None))
                    t = chunk(jobs)
                    tg = t
                    for hh in range(2):
                        for ax, dst, bn in ((0, RG, "lru_ba_2"), (1, IG, "lru_bx_2")):
                            bank = held[2 * hh + ax]
                            for o in range(2):
                                i = 2 * hh + o
                                ts = act.put(lambda e, bank=bank, o=o, i=i, dst=dst, bn=bn, g=g: e.activation(
                                    dst[:, i, :], bank[:, o * T:o * T + T], ACT.Sigmoid, bias=vec(bn, 4 * g + i)),
                                    [tg, (dve.sem, dve.count)])
                            mbank.give(bank, [ts])
                    t1 = dve.put(lambda e: e.tensor_tensor(UC[:, :, :], UC[:, :, :], IG[:, :, :], ALU.mult), [ts])
                    for i in range(4):
                        n = 4 * g + i
                        t2 = act.put(lambda e, i=i, n=n: e.activation(IG[:, i, :], RG[:, i, :], ACT.Tanh,
                                                                      scale=SP8[:, 1, n:n + 1]), [ts, t_sp, t1])
                    for i in range(4):
                        n = 4 * g + i
                        t4 = act.put(lambda e, i=i, n=n: e.activation(RG[:, i, :], RG[:, i, :], ACT.Exp,
                                                                      scale=SP8[:, 2, n:n + 1]), [t2])
                    for q in range(2):
                        t5 = dve.put(lambda e, q=q: e.tensor_tensor(
                            TMP[:, :, :], RG[:, 2 * q:2 * q + 2, :], RG[:, 2 * q:2 * q + 2, :], ALU.mult),
                            [t4] + tmp_free[0] + tmp_free[1])
                        t5 = dve.put(lambda e, q=q: e.scalar_tensor_tensor(
                            IG[:, 2 * q:2 * q + 2, :], TMP[:, :, :], 1.0, IG[:, 2 * q:2 * q + 2, :], ALU.add,
                            ALU.mult), [t5])
                        tmp_free[0] = tmp_free[1] = [t5]
                    t5 = dve.put(lambda e: e.tensor_scalar(IG[:, :, :], IG[:, :, :], 0.0, None, ALU.max), [t5])
                    t6 = act.put(lambda e: e.activation(IG[:, :, :], IG[:, :, :], ACT.Sqrt), [t5])
                    t7 = dve.put(lambda e: e.tensor_tensor(UC[:, :, :], UC[:, :, :], IG[:, :, :], ALU.mult), [t6])
                    for i in range(4):
                        t8 = dve.put(lambda e, i=i: e.tensor_tensor_scan(IG[:, i, :], RG[:, i, :], UC[:, i, :], 0.0,
                                                                         ALU.mult, ALU.add), [t7, t4])
                    t9 = dve.put(lambda e: e.tensor_tensor(ZB[:, :, :], ZB[:, :, :], IG[:, :, :], ALU.mult), [t8])
                    n0 = 4 * g
                    th = act.put(lambda e, n0=n0, YH=YH: e.activation(YH[:, n0:n0 + 4, :], ZB[:, :, :], ACT.Copy),
                                 [t9, tg] + prev)
                    tl = dve.put(lambda e, n0=n0, YH=YH, YL=YL: e.tensor_tensor(
                        YL[:, n0:n0 + 4, :], ZB[:, :, :], YH[:, n0:n0 + 4, :].bitcast(F32), ALU.subtract), [th])
                    for i in range(4):
                        t_y[n0 + i] = [th, tl]
            a_free = [t_used[st["used"] - 1]]
            end_u = marks_now()
            sU.close()
            sO2 = ExitStack()
            OO = sb(f"OO{l}", [128, 16, T], c=sO2)

            t_o = {}

            def evac_o(n, bank, ps, t, OO=OO, end_u=end_u):
                t_o[n] = act.put(lambda e: e.activation(OO[:, n, :], ps, ACT.Copy), [t] + end_u)
                ts = square(ps, [t], n, KD)
                mbank.give(bank, [t_o[n], ts])

            out_tiles(16, (YH, YL), t_y, 32, evac_o)
            end_y = marks_now()
            t_ro = norm_stat(D)
            sO2.close()
            sY.close()
            sE = ExitStack()
            EE = sb(f"EE{l}", [128, 16, T], c=sE)
            t_e = {}
            for c in range(2):
                jobs = []
                held = []
                for o in range(8):
                    if o % 2 == 0:
                        bank, freed = mbank.take()
                        held.append((bank, [None]))
                    for k in range(2):
                        jobs.append((bank[:, (o % 2) * T:(o % 2) * T + T], o * 2 + k, PH[:, k, :], PL[:, k, :],
                                     k == 0 and o % 2 == 0, k == 1, freed + [t_p2],
                                     held[-1][1] if (o % 2 and k == 1) else None))
                chunk(jobs)
                for q, (bank, mark) in enumerate(held):
                    te = act.put(lambda e, c=c, q=q, bank=bank, EE=EE: e.activation(
                        EE[:, 8 * c + 2 * q:8 * c + 2 * q + 2, :], bank[:, :].rearrange("p (a t) -> p a t", a=2),
                        ACT.Copy), [mark[-1]] + end_y)
                    t_e[8 * c + 2 * q] = t_e[8 * c + 2 * q + 1] = te
                    mbank.give(bank, [te])
            for k in range(KD):
                t = dve.put(lambda e, k=k, OO=OO, l=l: e.scalar_tensor_tensor(
                    OO[:, k, :], OO[:, k, :], vec("g_post_2", 16 * l + k), R[:, :], ALU.mult, ALU.mult),
                    [t_ro, t_o[k]])
                r_read[:] = [t]
                t = dve.put(lambda e, k=k, OO=OO: e.tensor_tensor(XT[:, k, :], XT[:, k, :], OO[:, k, :], ALU.add), [t])
                square(XT[:, k, :], [t], k, KD)
                prep(k, XT[:, k, :], vec("g_ple_in_2", 16 * l + k), [t], a_free)
            t_r = norm_stat(D)
            t_eg = {}

            def evac_g(n, bank, ps, t, EE=EE, t_r=t_r):
                s = n % 2
                t1 = dve.put(lambda e: e.tensor_tensor(TMP[:, s, :], ps, R[:, :], ALU.mult), [t, t_r] + tmp_free[s])
                mbank.give(bank, [t1])
                r_read[:] = [t1]
                t1 = act.put(lambda e: e.activation(TMP[:, s, :], TMP[:, s, :], ACT.Sigmoid), [t1])
                t1 = dve.put(lambda e: e.tensor_tensor(EE[:, n, :], EE[:, n, :], TMP[:, s, :], ALU.mult),
                             [t1, t_e[n]])
                tmp_free[s] = [t1]
                t_eg[n] = t1
                square(EE[:, n, :], [t1], n, KD)

            out_tiles(16, A, t_a, 16, evac_g)
            a_free = [t_used[st["used"] - 1]]
            t_rg = norm_stat(D)
            for k in range(KD):
                t = dve.put(lambda e, k=k, EE=EE, l=l: e.scalar_tensor_tensor(
                    EE[:, k, :], EE[:, k, :], vec("g_ple_out_2", 16 * l + k), R[:, :], ALU.mult, ALU.mult), [t_rg])
                r_read[:] = [t]
                t = dve.put(lambda e, k=k, EE=EE: e.tensor_tensor(XT[:, k, :], XT[:, k, :], EE[:, k, :], ALU.add), [t])
                if l == 0:
                    square(XT[:, k, :], [t], k, KD)
                    prep(k, XT[:, k, :], vec("g_pre_2", 16 + k), [t], a_free)
                elif k % 4 == 3:
                    q = k // 4
                    sp.dma(lambda e, q=q: e.dma_start(
                        out.rearrange("p (k t) -> p k t", k=KD)[:, 4 * q:4 * q + 4, :], XT[:, 4 * q:4 * q + 4, :]),
                        s_out, [t])
            if l == 0:
                t_r = norm_stat(D)
            prev = marks_now()
            sE.close()
        sp.wait([(s_out, 64)])
        s2.close()
        assert st["used"] == NCH, (st["used"], NCH)
        assert not sq["late"]


def _panels(np, w, kt=16):
    k, n = w.shape
    a = w.reshape(k // (kt * 128), kt, 128, n // 128, 128).transpose(3, 0, 2, 1, 4)
    return a.reshape(-1, 128, kt * 128)


def _layout(np, x):
    f = np.float32
    o = {}

    def col(v):
        v = np.asarray(v).reshape(-1)
        return v.reshape(-1, 128).T

    def tok(v):
        t, n = v.shape
        return v.T.reshape(n // 128, 128, t).transpose(1, 0, 2)

    cols = {}
    for name, _ in VECS:
        if name == "gla_bias":
            cols[name] = np.concatenate([col(x["gla_bias_f"]), col(x["gla_bias_b"])], axis=1)
        elif name == "eps":
            cols[name] = np.full((128, 1), 1e-6, f)
        elif name == "one":
            cols[name] = np.ones((128, 1), f)
        else:
            cols[name] = col(x[name])
    o["vecs"] = np.concatenate([cols[n] for n, _ in VECS], axis=1)
    o["xt"] = tok(x["x"][0]).reshape(128, -1)
    o["ones"] = np.ones((128, 128), f)
    o["ident"] = np.eye(128, dtype=f)
    w = x["w_in"][0]
    o["w_in"] = np.concatenate([_panels(np, w[:, 0:1024]), _panels(np, w[:, 1024:1152]),
                                _panels(np, w[:, 1056:1568]), _panels(np, w[:, 1568:])], axis=0)
    z = np.zeros((16, 256), f)
    o["gla_up"] = np.concatenate([np.concatenate([x["gla_up_f"][0], z], axis=1),
                                  np.concatenate([z, x["gla_up_b"][0]], axis=1)], axis=0)
    o["w_out"] = _panels(np, x["w_out"][0])
    o["w_query"] = _panels(np, x["peer_w_query"][0])
    o["sub_keys"] = x["peer_sub_keys"][0].reshape(16, 128, 128).transpose(2, 0, 1).reshape(128, 2048)
    o["peer_down"] = x["peer_down"][0].reshape(128, 128, 16, 128).transpose(1, 3, 2, 0).reshape(128, 128, 2048)
    o["peer_up"] = x["peer_up"][0]
    o["w_in_2"] = np.concatenate([_panels(np, x["w_in_2"][l]) for l in range(2)], axis=0)
    o["w_out_2"] = np.concatenate([_panels(np, x["w_out_2"][l]) for l in range(2)], axis=0)
    o["w_gate"] = np.concatenate([_panels(np, x["w_ple_gate_2"][l]) for l in range(2)], axis=0)
    pw = x["pool_w_2"][0].reshape(4, 8, 128, 4, 2, 128).transpose(0, 3, 2, 4, 1, 5)
    o["pool_w"] = pw.reshape(16, 128, 2048)
    pl = x["w_ple_2"].reshape(2, 2, 128, 2, 8, 128).transpose(0, 3, 2, 4, 1, 5)
    o["w_ple"] = pl.reshape(4, 128, 2048)
    lw = np.stack([x["lru_wa_2"][0], x["lru_wx_2"][0]], axis=1)
    lw = lw.reshape(8, 2, 2, 2, 128, 2, 128).transpose(0, 4, 1, 2, 3, 5, 6)
    o["lru_w"] = lw.reshape(8, 128, 2048)
    o["p_2"] = np.stack([tok(x["p_2"][l, 0]) for l in range(2)], axis=1).reshape(128, 1024)
    i = np.arange(256)
    rel = i[:, None] - i[None, :]
    cnt = (np.abs(rel) <= 64).astype(f) + (rel % 4 == 0).astype(f) + (rel % 16 == 0).astype(f)
    bias = np.where(cnt > 0, 0.0, -1e30).astype(f)
    o["c_cnt"] = cnt.reshape(2, 128, 256).transpose(1, 0, 2).reshape(128, 512)
    o["c_bias"] = bias.reshape(2, 128, 256).transpose(1, 0, 2).reshape(128, 512)
    j = np.arange(128)
    same = (j[:, None] // 64) == (j[None, :] // 64)
    mf = (same & (j[:, None] <= j[None, :])).astype(f)
    mb = (same & (j[:, None] > j[None, :])).astype(f)
    o["c_gmask"] = np.concatenate([mf, mb], axis=1)
    inv = np.float32(500000.0) ** (-np.arange(16, dtype=f) / f(16))
    ang = inv.astype(f)[:, None] * np.arange(256, dtype=f)[None, :]
    c, s = np.cos(ang).astype(f), np.sin(ang).astype(f)
    c2, s2 = np.concatenate([c, c], 0), np.concatenate([-s, s], 0)
    o["c_rope"] = np.concatenate([c2, s2], axis=1)
    rot = np.zeros((32, 32), f)
    rot[np.arange(16) + 16, np.arange(16)] = 1.0
    rot[np.arange(16), np.arange(16) + 16] = 1.0
    o["c_rot"] = rot
    o["c_scan"] = np.tile((i % 64 != 0).astype(f), (128, 1))
    o["c_iota"] = np.tile(j.astype(f), (128, 1))
    o["c_inv"] = np.tile(np.concatenate([1.0 / np.minimum(i[:16] + 1, w) for w in (2, 4, 8, 16)]).astype(f), (128, 1))
    return {k: np.ascontiguousarray(v) for k, v in o.items()}


def kernel(**inputs):
    import numpy as np
    import concourse.bacc as bacc
    from concourse.bass_utils import run_bass_kernel_spmd as run

    arrays = _layout(np, {k: np.asarray(v) for k, v in inputs.items()})
    nc = bacc.Bacc("TRN2", target_bir_lowering=False, num_devices=1, dynamic_dma_scratch_size=1024)
    d = {k: nc.dram_tensor("in_" + k, a.shape, mybir.dt.from_np(a.dtype), kind="ExternalInput").ap()
         for k, a in arrays.items()}
    out = nc.dram_tensor("out_0", (128, 4096), F32, kind="ExternalOutput").ap()
    build(nc, d, out)
    r = run(nc, [{"in_" + k: a for k, a in arrays.items()}], core_ids=[0])
    y = r.results[0]["out_0"].reshape(128, 16, 256).transpose(2, 1, 0).reshape(1, 256, 2048)
    return np.ascontiguousarray(y)
```

```python
from contextlib import ExitStack

import concourse.bass as bass
from concourse import mybir

F32 = mybir.dt.float32
FR = mybir.dt.float32r
U32 = mybir.dt.uint32
ALU = mybir.AluOpType
ACT = mybir.ActivationFunctionType
AX = mybir.AxisListType

T = 256
D = 2048
KD = 16
NRAW = 3
NSPL = 3
PARTS = [(0, 40), (40, 32), (72, 40), (112, 16)]
TAIL = 8
NEG = -3.0e38

VECS = [
    ("norm1_g", 16), ("norm2_g", 16), ("gla_bias", 4), ("gla_out_g", 4), ("q_norm_g", 1), ("k_norm_g", 1),
    ("g_pre_2", 32), ("g_post_2", 32), ("g_ple_in_2", 32), ("g_ple_out_2", 32),
    ("pool_b_2", 32), ("pool_scale_2", 32), ("conv_w_2", 128), ("conv_b_2", 32),
    ("lru_ba_2", 32), ("lru_bx_2", 32), ("lru_L_2", 32), ("eps", 1), ("one", 1),
]
VOFF = {}
_n = 0
for _k, _w in VECS:
    VOFF[_k] = _n
    _n += _w
NVEC = _n

SETS = {"logexp": "natural_log_exp_and_others", "gelu": "gelu_apprx_tanh_and_others",
        "sigmoid": "sigmoid_and_others"}


class Queue:

    def __init__(self, eng, sem):
        self.eng, self.sem = eng, sem
        self.count = 0
        self.seen = {}

    def wait(self, after):
        for sem, val in after:
            if self.seen.get(id(sem), 0) < val:
                self.seen[id(sem)] = val
                self.eng.wait_ge(sem, val)

    def put(self, fn, after=(), inc=True):
        self.wait(after)
        ins = fn(self.eng)
        if inc:
            ins.then_inc(self.sem, 1)
            self.count += 1
        return (self.sem, self.count)

    def dma(self, fn, sem, after=()):
        self.wait(after)
        fn(self.eng).then_inc(sem, 16)


class Pool:

    def __init__(self, places):
        self.free = [(p, []) for p in places]

    def take(self):
        assert self.free, "no place free"
        return self.free.pop(0)

    def give(self, place, ticks):
        self.free.append((place, list(ticks)))


def build(nc, d, out, stop=None):
    ctx = ExitStack()
    with ctx:
        def sb(name, shape, dt=F32, c=ctx):
            return c.enter_context(nc.sbuf_tensor(name, shape, dt))

        def sem(name):
            return ctx.enter_context(nc.semaphore(name))

        pe, act, dve, sp, pool = (
            Queue(e, sem("s_" + n)) for e, n in ((nc.tensor, "pe"), (nc.scalar, "act"), (nc.vector, "dve"),
                                                 (nc.sync, "sp"), (nc.gpsimd, "pool")))

        XT = sb("XT", [128, KD, T])
        AH = sb("AH", [128, KD, T], FR)
        AL = sb("AL", [128, KD, T], FR)
        RAW = sb("RAW", [128, NRAW, 2048])
        WH = sb("WH", [128, NSPL, 2048], FR)
        WL = sb("WL", [128, NSPL, 2048], FR)
        VEC = sb("VEC", [128, NVEC])
        ONES = sb("ONES", [128, 128])
        IDENT = sb("IDENT", [128, 128])
        SQ = sb("SQ", [128, 2, T])
        R = sb("R", [128, T])
        TMP = sb("TMP", [128, 2, T])
        banks = [ctx.enter_context(nc.psum_tensor(f"PS{i}", [128, 512], F32)) for i in range(8)]
        mbank = Pool(banks[0:4])
        abank = Pool(banks[4:8])

        raw_sem = [sem(f"s_raw{i}") for i in range(NRAW)]
        s_out = sem("s_out")
        nload = [0]

        def load(dst, src, after=(), q=sp):
            s = sem(f"s_ld{nload[0]}")
            nload[0] += 1
            q.dma(lambda e: e.dma_start(dst, src), s, after)
            return (s, 16)

        def vec(name, i=0, p0=0, p1=128):
            o = VOFF[name] + i
            return VEC[p0:p1, o:o + 1]

        t_vec = load(VEC[:, :], d["vecs"][:, :])
        x4 = d["xt"].rearrange("p (k t) -> p k t", k=KD)
        t_xts = [load(XT[:, 4 * i:4 * i + 4, :], x4[:, 4 * i:4 * i + 4, :]) for i in range(4)]
        t_ones = load(ONES[:, :], d["ones"][:, :], q=act)
        t_ident = load(IDENT[:, :], d["ident"][:, :], q=act)

        order = []
        winA = d["w_in"]
        for i in [8] + list(range(8)) + list(range(9, 13)):
            order.append(winA[i])
        for h in range(12):
            for j in range(3):
                order.append(winA[13 + 12 * j + h])
        order += [d["w_out"][i] for i in range(16)]
        order += [d["w_query"][i] for i in range(16)]
        down, up = d["peer_down"], d["peer_up"].rearrange("(i j) c -> i j c", j=128)

        def down_part(p):
            return [down[j] for j in range(PARTS[p][0], sum(PARTS[p]))]

        def up_part(p):
            p0, n = PARTS[p]
            return ([up[:, j, 0:1792] for j in range(p0, p0 + n)]
                    + [up[:, j:j + TAIL, 1792:2048] for j in range(p0, p0 + n, TAIL)])

        order += down_part(0) + down_part(1) + up_part(0) + down_part(2) + up_part(1) + down_part(3)
        order += up_part(2) + up_part(3)
        for l in range(2):
            w2 = d["w_in_2"]
            if l == 0:
                for g in range(4):
                    order += [w2[8 * g + i] for i in range(8)]
                    for half in range(2):
                        order += [w2[32 + 8 * g + 4 * half + i] for i in range(4)]
                        order += [d["pool_w"][4 * g + 2 * half + i] for i in range(2)]
            else:
                for g in range(8):
                    order += [w2[64 + 4 * g + i] for i in range(4)]
                    order += [w2[96 + 4 * g + i] for i in range(4)]
                    order += [d["lru_w"][g]]
            order += [d["w_out_2"][32 * l + 2 * i + c] for c in range(2) for i in range(4)]
            order += [d["w_out_2"][32 * l + i] for i in range(8, 32)]
            order += [d["w_ple"][2 * l + i] for i in range(2)]
            order += [d["w_gate"][16 * l + i] for i in range(16)]
        NCH = len(order)

        t_hi, t_lo, t_used = {}, {}, {}
        st = {"fetched": 0, "hi": 0, "lo": 0, "used": 0, "steps": 0}

        def width(c):
            n = 1
            for x in order[c].shape[1:]:
                n *= x
            return n

        def fetch(c):
            after = [t_hi[c - NRAW], t_lo[c - NRAW]] if c >= NRAW else []
            dst = RAW[:, c % NRAW, 0:width(c)]
            if len(order[c].shape) == 3:
                dst = dst.rearrange("p (a n) -> p a n", a=order[c].shape[1])
            sp.dma(lambda e: e.dma_start(dst, order[c]), raw_sem[c % NRAW], after)

        def split_hi(c):
            r, s, n = c % NRAW, c % NSPL, width(c)
            after = [(raw_sem[r], 16 * (c // NRAW + 1))] + ([t_used[c - NSPL]] if c >= NSPL else [])
            t_hi[c] = act.put(lambda e: e.activation(WH[:, s, 0:n], RAW[:, r, 0:n], ACT.Copy), after)

        def split_lo(c):
            r, s, n = c % NRAW, c % NSPL, width(c)
            after = [(raw_sem[r], 16 * (c // NRAW + 1)), t_hi[c]] + ([t_used[c - NSPL]] if c >= NSPL else [])
            t_lo[c] = dve.put(lambda e: e.tensor_tensor(WL[:, s, 0:n], RAW[:, r, 0:n], WH[:, s, 0:n].bitcast(F32),
                                                        ALU.subtract), after)

        def fetch_to(c):
            while st["fetched"] < min(NCH, c):
                fetch(st["fetched"])
                st["fetched"] += 1

        def hi_to(c):
            while st["hi"] < min(NCH, c):
                fetch_to(st["hi"] + 1)
                split_hi(st["hi"])
                st["hi"] += 1

        def lo_to(c):
            while st["lo"] < min(NCH, c):
                split_lo(st["lo"])
                st["lo"] += 1
                fetch_to(st["lo"] + NRAW)

        bg = []

        def step(n=1):
            for _ in range(n):
                if not bg:
                    return
                if next(bg[0], "end") == "end":
                    bg.pop(0)

        def drain(gen=None):
            while bg and (gen is None or gen in bg):
                step()

        def chunk(jobs, steps=1):
            c = st["used"]
            step(st["steps"])
            st["steps"] = steps
            if c == 0:
                fetch_to(NRAW)
            for n in range(st["lo"], c + NSPL):
                hi_to(n + 1)
                lo_to(n + 1)
            s = c % NSPL
            n = len(jobs)
            tick = None
            for j, (ps, b, xh, xl, first, last, after, mark) in enumerate(jobs):
                wh, wl = WH[:, s, b * 128:b * 128 + 128], WL[:, s, b * 128:b * 128 + 128]
                w = list(after() if callable(after) else after) + [t_lo[c]]
                fin = mark is not None or j == n - 1
                pe.put(lambda e, ps=ps, wh=wh, xh=xh, first=first: e.matmul(
                    ps, wh, xh, start=first, stop=False, skip_group_check=True), w, inc=False)
                pe.put(lambda e, ps=ps, wh=wh, xl=xl: e.matmul(
                    ps, wh, xl, start=False, stop=False, skip_group_check=True), inc=False)
                tick = pe.put(lambda e, ps=ps, wl=wl, xh=xh, last=last: e.matmul(
                    ps, wl, xh, start=False, stop=last, skip_group_check=True), inc=fin)
                if mark is not None:
                    mark(tick)
            t_used[c] = tick
            st["used"] = c + 1
            hi_to(c + NSPL + 1)
            return tick

        def tile_k(src, ticks, nk=KD, steps=1):
            bank, freed = mbank.take()
            ps = bank[:, 0:T]
            hi, lo = src
            for c0 in range(0, nk, 16):
                jobs = []
                for b in range(min(16, nk)):
                    k = c0 + b
                    jobs.append((ps, b, hi[:, k, :], lo[:, k, :], k == 0, k == nk - 1,
                                 (freed if k == 0 else []) + list(ticks.get(k, [])), None))
                t = chunk(jobs, steps)
            return bank, ps, t

        t_a = {}
        A = (AH, AL)

        def prep(k, src, g, after, freed=()):
            th = dve.put(lambda e: e.tensor_scalar(AH[:, k, :], src, g, None, ALU.mult), list(after) + list(freed))
            tl = dve.put(lambda e: e.scalar_tensor_tensor(AL[:, k, :], src, g, AH[:, k, :].bitcast(F32),
                                                          ALU.mult, ALU.subtract), [th] + list(after) + list(freed))
            t_a[k] = [th, tl]
            return tl

        sq = {"n": 0, "used": {}, "bank": None, "late": []}

        def square(src, after, n, total):
            i = sq["n"]
            sq["n"] += 1
            s = i % 2
            freed = [sq["used"][i - 2]] if i - 2 in sq["used"] else []
            t = act.put(lambda e: e.activation(SQ[:, s, :], src, ACT.Square), list(after) + freed)
            if n == 0:
                sq["bank"], sq["freed"] = abank.take()
            bank, extra = sq["bank"], (sq["freed"] if n == 0 else [])
            def go():
                sq["used"][i] = pe.put(lambda e: e.matmul(bank[:, 0:T], ONES[:, :], SQ[:, s, :], start=(n == 0),
                                                          stop=(n == total - 1)), [t, t_ones] + extra)
            sq["late"].append(go)
            if len(sq["late"]) > 1:
                sq["late"].pop(0)()
            return t

        r_read = []

        def norm_stat(n):
            while sq["late"]:
                sq["late"].pop(0)()
            bank = sq["bank"]
            done = sq["used"][sq["n"] - 1]
            t1 = act.put(lambda e: e.activation(R[:, :], bank[:, 0:T], ACT.Ln, bias=vec("eps"), scale=1.0 / n),
                         [done, t_vec] + list(r_read))
            abank.give(bank, [t1])
            t2 = act.put(lambda e: e.activation(R[:, :], R[:, :], ACT.Exp, scale=-0.5), [t1])
            r_read.clear()
            return t2

        s1 = ExitStack()
        MH = sb("MH", [128, KD, T], FR, s1)
        ML = sb("ML", [128, KD, T], FR, s1)
        sB = ExitStack()
        MB = sb("MB", [128, 2, T], c=sB)
        GM = sb("GM", [128, 2, 128], c=sB)
        RC = sb("RC", [32, 2, T], c=sB)
        RP = sb("RP", [32, 32], c=sB)
        SCM = sb("SCM", [128, T], c=sB)
        UPW = sb("UPW", [32, 512], c=sB)
        GD = sb("GD", [32, T], c=sB)
        GQ = sb("GQ", [128, 2, T], c=sB)
        GK = sb("GK", [128, 2, T], c=sB)
        GV = sb("GV", [128, 4, T], c=sB)
        GR = sb("GR", [128, 4, T], c=sB)
        QKV = sb("QKV", [128, 3, 3, T], c=sB)
        t_mb = load(MB[:, :, :], d["c_bias"].rearrange("p (a t) -> p a t", a=2), q=act)
        t_gm = load(GM[:, :, :], d["c_gmask"].rearrange("p (a t) -> p a t", a=2), q=act)
        t_rc = load(RC[:, :, :], d["c_rope"].rearrange("p (a t) -> p a t", a=2), q=act)
        t_rp = load(RP[:, :], d["c_rot"][:, :], q=act)
        t_scm = load(SCM[:, :], d["c_scan"][:, :], q=act)
        t_up = load(UPW[:, :], d["gla_up"][:, :], q=act)
        act.put(lambda e: e.preload_act_table_set(SETS["logexp"]), inc=False)

        for k in range(KD):
            square(XT[:, k, :], [t_xts[k // 4]], k, KD)
            prep(k, XT[:, k, :], vec("norm1_g", k), [t_xts[k // 4], t_vec])
        t_r = norm_stat(D)

        def evac_r(dst, bank, ps, t, p1=128, after=()):
            tt = dve.put(lambda e: e.tensor_tensor(dst, ps[0:p1], R[0:p1, :], ALU.mult), [t, t_r] + list(after))
            mbank.give(bank, [tt])
            r_read[:] = [tt]
            return tt

        bank, ps, t = tile_k(A, t_a)
        t_gd = evac_r(GD[:, :], bank, ps, t, 32)
        t_g = {}
        for name, dst, n in (("q", GQ, 2), ("k", GK, 2), ("v", GV, 4), ("r", GR, 4)):
            for i in range(n):
                bank, ps, t = tile_k(A, t_a)
                t_g[name, i] = evac_r(dst[:, i, :], bank, ps, t)

        sG = ExitStack()
        BB, LS, E1, E2 = (XT[:, 4 * i:4 * i + 4, :] for i in range(4))
        KS = LS
        BL = sb("BL", [128, 4, 4], c=sG)
        DC = sb("DC", [128, 4, 4], c=sG)
        VN = sb("VN", [128, 4, 2, 128], c=sG)
        KN = sb("KN", [128, 4, 2, 128], c=sG)
        SS = sb("SS", [128, 4, 3, 128], c=sG)
        SM = TMP[:, :, :].rearrange("p s (a c) -> p s a c", a=2)
        sG_end, t_xt2 = [], []

        def gla():
            bz, fz = abank.take()
            bz2, fz2 = abank.take()
            for n in range(4):
                ps = (bz, bz2)[n // 2][:, (n % 2) * T:(n % 2) * T + T]
                t = pe.put(lambda e, n=n, ps=ps: e.matmul(ps, UPW[:, n * 128:n * 128 + 128], GD[:, :], start=True,
                                                          stop=True, skip_group_check=True),
                           [t_gd, t_up] + fz + fz2)
            yield
            for n in range(4):
                ps = (bz, bz2)[n // 2][:, (n % 2) * T:(n % 2) * T + T]
                tz = dve.put(lambda e, n=n, ps=ps: e.tensor_scalar(BB[:, n, :], ps, vec("gla_bias", n), None, ALU.add),
                             [t, t_vec])
            abank.give(bz, [tz])
            abank.give(bz2, [tz])
            t1 = act.put(lambda e: e.activation(LS[:, :, :], BB[:, :, :], ACT.Abs), [tz])
            t1 = act.put(lambda e: e.activation(E1[:, :, :], LS[:, :, :], ACT.Exp, scale=-1.0), [t1])
            t1 = act.put(lambda e: e.activation(E2[:, :, :], E1[:, :, :], ACT.Ln, bias=vec("one")), [t1])
            t2 = dve.put(lambda e: e.scalar_tensor_tensor(BB[:, :, :], BB[:, :, :], 0.0, E2[:, :, :], ALU.min,
                                                          ALU.subtract), [t1])
            t2 = dve.put(lambda e: e.tensor_scalar(LS[:, :, :], BB[:, :, :], 1.0 / 16.0, None, ALU.mult), [t2])
            yield
            for n in range(4):
                t3 = dve.put(lambda e, n=n: e.tensor_tensor_scan(BB[:, n, :], SCM[:, :], LS[:, n, :], 0.0, ALU.mult,
                                                                 ALU.add), [t2, t_scm])
            B4 = BB[:, :, :].rearrange("p n (c j) -> p n c j", c=4)
            t3 = dve.put(lambda e: e.tensor_copy(BL[:, :, :], B4[:, :, :, 63]), [t3])
            yield
            for n in (2, 3):
                t4 = dve.put(lambda e, n=n: e.tensor_tensor(LS[:, n, :], LS[:, n, :], BB[:, n, :], ALU.subtract), [t3])
            for n in (2, 3):
                for c in range(4):
                    cs = slice(64 * c, 64 * c + 64)
                    t5 = dve.put(lambda e, n=n, c=c, cs=cs: e.tensor_scalar(
                        BB[:, n, cs], LS[:, n, cs], BL[:, n, c:c + 1], None, ALU.add), [t4])
            yield
            t6 = act.put(lambda e: e.activation(E1[:, :, :], BB[:, :, :], ACT.Exp), [t5])
            t6 = act.put(lambda e: e.activation(E2[:, :, :], BB[:, :, :], ACT.Exp, scale=-1.0), [t5])
            t6d = act.put(lambda e: e.activation(DC[:, :, :], BL[:, :, :], ACT.Exp), [t3])
            for n in range(4):
                for c in range(4):
                    cs = slice(64 * c, 64 * c + 64)
                    t7 = act.put(lambda e, n=n, c=c, cs=cs: e.activation(
                        KS[:, n, cs], BB[:, n, cs], ACT.Exp, scale=-1.0, bias=BL[:, n, c:c + 1]), [t5])
                if n % 2:
                    yield
            for n in range(4):
                i = n % 2
                t8 = dve.put(lambda e, n=n, i=i: e.scalar_tensor_tensor(
                    E1[:, n, :], GQ[:, i, :], 0.125, E1[:, n, :], ALU.mult, ALU.mult), [t6, t_g["q", i]])
                t9 = dve.put(lambda e, n=n, i=i: e.tensor_tensor(E2[:, n, :], GK[:, i, :], E2[:, n, :], ALU.mult),
                             [t6, t_g["k", i]])
                t10 = dve.put(lambda e, n=n, i=i: e.tensor_tensor(KS[:, n, :], GK[:, i, :], KS[:, n, :], ALU.mult),
                              [t7])
            yield
            for src, dst, tk in ((GV, VN, t_g["v", 3]), (KS, KN, t10)):
                for half in range(2):
                    b, f = abank.take()
                    for m in range(2):
                        n = 2 * half + m
                        for tb in range(2):
                            t = pe.put(lambda e, b=b, m=m, tb=tb, n=n, src=src: e.transpose(
                                b[:, (2 * m + tb) * 128:(2 * m + tb) * 128 + 128],
                                src[:, n, tb * 128:tb * 128 + 128], IDENT[:, :]), [tk, t_ident] + f)
                    tc = act.put(lambda e, b=b, half=half, dst=dst: e.activation(
                        dst[:, 2 * half:2 * half + 2, :, :], b[:, :].rearrange("p (m s c) -> p m s c", m=2, s=2),
                        ACT.Copy), [t])
                    abank.give(b, [tc])
                yield
            t_s = {}
            for step_i in range(3):
                for n in range(4):
                    c = step_i if n < 2 else 3 - step_i
                    i = n % 2
                    tb, p0 = c // 2, 64 * (c % 2)
                    b, f = abank.take()
                    for hh in range(2):
                        t = pe.put(lambda e, b=b, hh=hh, n=n, tb=tb, p0=p0, i=i: e.matmul(
                            b[64 * hh:64 * hh + 64, 0:128], KN[p0:p0 + 64, n, tb, 64 * hh:64 * hh + 64],
                            VN[p0:p0 + 64, 2 * i + hh, tb, :], start=True, stop=True, skip_group_check=True),
                            [tc] + f)
                    if step_i == 0:
                        t_s[n, 0] = dve.put(lambda e, b=b, n=n: e.tensor_copy(SS[:, n, 0, :], b[:, 0:128]), [t])
                    else:
                        t_s[n, step_i] = dve.put(lambda e, b=b, n=n, k=step_i, c=c: e.scalar_tensor_tensor(
                            SS[:, n, k, :], SS[:, n, k - 1, :], DC[:, n, c:c + 1], b[:, 0:128], ALU.mult, ALU.add),
                            [t, t_s[n, step_i - 1], t6d])
                    abank.give(b, [t_s[n, step_i]])
                yield
            sm_free = [[], []]
            for h in range(4):
                i, hp = h // 2, 64 * (h % 2)
                bo, fo = abank.take()
                first = True
                for tb in range(2):
                    b, f = abank.take()
                    for dr in range(2):
                        n = 2 * dr + i
                        t = pe.put(lambda e, b=b, dr=dr, n=n, tb=tb, hp=hp: e.matmul(
                            b[:, dr * 128:dr * 128 + 128], E2[hp:hp + 64, n, tb * 128:tb * 128 + 128],
                            E1[hp:hp + 64, n, tb * 128:tb * 128 + 128], start=True, stop=True,
                            skip_group_check=True), [t8, t9] + f)
                    tm = dve.put(lambda e, b=b, tb=tb: e.tensor_tensor(
                        SM[:, tb, :, :], b[:, 0:256].rearrange("p (a c) -> p a c", a=2), GM[:, :, :], ALU.mult),
                        [t, t_gm] + sm_free[tb])
                    abank.give(b, [tm])
                    tm = dve.put(lambda e, tb=tb: e.tensor_tensor(SM[:, tb, 0, :], SM[:, tb, 0, :], SM[:, tb, 1, :],
                                                                  ALU.add), [tm])
                    yield
                    t = pe.put(lambda e, bo=bo, h=h, tb=tb, first=first: e.matmul(
                        bo[:, tb * 128:tb * 128 + 128], VN[:, h, tb, :], SM[:, tb, 0, :], start=first, stop=False,
                        skip_group_check=True), [tm] + fo)
                    sm_free[tb] = [t]
                    first = False
                for dr in range(2):
                    n = 2 * dr + i
                    for k in range(3):
                        c = k + 1 if dr == 0 else 2 - k
                        t = pe.put(lambda e, bo=bo, n=n, k=k, c=c, hp=hp: e.matmul(
                            bo[:, 64 * c:64 * c + 64], SS[hp:hp + 64, n, k, :], E1[hp:hp + 64, n, 64 * c:64 * c + 64],
                            start=False, stop=False, skip_group_check=True), [t_s[n, k]])
                OT = GV[:, h, :]
                to = act.put(lambda e, bo=bo, OT=OT: e.activation(OT, bo[:, 0:T], ACT.Copy), [t])
                ts = act.put(lambda e, bo=bo, i=i, h=h: e.activation(BB[:, h, :], bo[:, 0:T], ACT.Square), [t])
                abank.give(bo, [to, ts])
                yield
                b, f = abank.take()
                t = pe.put(lambda e, b=b, h=h: e.matmul(b[:, 0:T], ONES[:, :], BB[:, h, :], start=True, stop=True),
                           [ts] + f)
                t1 = act.put(lambda e, b=b, h=h: e.activation(BB[:, h, :], b[:, 0:T], ACT.Ln, bias=vec("eps"),
                                                              scale=1.0 / 128), [t])
                abank.give(b, [t1])
                t1 = act.put(lambda e, h=h: e.activation(BB[:, h, :], BB[:, h, :], ACT.Exp, scale=-0.5), [t1])
                t2 = act.put(lambda e, h=h: e.activation(KS[:, h, :], GR[:, h, :], ACT.Exp, scale=-1.0),
                             [t_g["r", h], tc])
                t3 = dve.put(lambda e, h=h: e.tensor_scalar(KS[:, h, :], KS[:, h, :], 1.0, None, ALU.add), [t2])
                t3 = dve.put(lambda e, h=h: e.reciprocal(KS[:, h, :], KS[:, h, :]), [t3])
                t3 = dve.put(lambda e, h=h: e.tensor_tensor(GR[:, h, :], GR[:, h, :], KS[:, h, :], ALU.mult), [t3])
                yield
                t4 = dve.put(lambda e, h=h, OT=OT: e.scalar_tensor_tensor(
                    OT, OT, vec("gla_out_g", h), BB[:, h, :], ALU.mult, ALU.mult), [to, t1])
                t4 = dve.put(lambda e, h=h, OT=OT: e.tensor_tensor(OT, OT, GR[:, h, :], ALU.mult), [t4, t3])
                th = dve.put(lambda e, h=h, OT=OT: e.tensor_copy(MH[:, h, :], OT), [t4])
                tl = dve.put(lambda e, h=h, OT=OT: e.tensor_tensor(ML[:, h, :], OT, MH[:, h, :].bitcast(F32),
                                                                   ALU.subtract), [th])
                t_m[h] = [th, tl]
                yield
            sG_end[:] = [(pe.sem, pe.count), (act.sem, act.count), (dve.sem, dve.count)]
            t_xt2[:] = [load(XT[:, :, :], d["xt"].rearrange("p (k t) -> p k t", k=KD), sG_end, q=act)]

        t_m = {}
        gen_gla = gla()
        bg.append(gen_gla)
        sG.close()
        sA = ExitStack()
        ASQ = sb("ASQ", [128, 2, T], c=sA)
        ALG = TMP[:, :, :].rearrange("p a t -> p (a t)")
        ARR = sb("ARR", [128, 2, T], c=sA)
        AT1 = sb("AT1", [32, 2, T], c=sA)
        ASM = sb("ASM", [128, 2, T], c=sA)
        AP_ = sb("AP_", [128, 2, T], c=sA)
        APT = sb("APT", [128, 2, T], c=sA)
        AVN = sb("AVN", [128, 2, 128], c=sA)
        ANM = sb("ANM", [128, 2], c=sA)
        ADN = sb("ADN", [128, 2], c=sA)
        ARD = sb("ARD", [128, 2], c=sA)
        av = {"pt": [], "vn": [], "p": []}

        def attn(h, tq):
            s = h % 3
            qk = QKV[:, s, 0:2, :]
            qkf = qk.rearrange("p a t -> p (a t)")
            pre = list(sG_end)
            t = act.put(lambda e: e.activation(ASQ[:, :, :], qk, ACT.Square), [tq[0], tq[1]] + pre)
            bv, fv = abank.take()
            for kt in range(2):
                tv = pe.put(lambda e, kt=kt: e.transpose(bv[:, kt * 128:kt * 128 + 128],
                                                         QKV[:, s, 2, kt * 128:kt * 128 + 128], IDENT[:, :]),
                            [tq[2]] + fv)
            b, f = abank.take()
            t = pe.put(lambda e: e.matmul(b[:, :], ONES[:, :], ASQ[:, :, :].rearrange("p a t -> p (a t)"),
                                          start=True, stop=True), [t] + f)
            tvn = act.put(lambda e: e.activation(AVN[:, :, :], bv[:, 0:256].rearrange("p (a c) -> p a c", a=2),
                                                 ACT.Copy), [tv] + av["vn"] + pre)
            abank.give(bv, [tvn])
            t = act.put(lambda e: e.activation(ALG, b[:, :], ACT.Ln, bias=vec("eps"), scale=1.0 / 128), [t] + pre)
            abank.give(b, [t])
            t = act.put(lambda e: e.activation(ARR[:, :, :].rearrange("p a t -> p (a t)"), ALG, ACT.Exp,
                                               scale=-0.5), [t])
            yield
            for a, g in ((0, "q_norm_g"), (1, "k_norm_g")):
                tn = dve.put(lambda e, a=a, g=g: e.scalar_tensor_tensor(
                    QKV[:, s, a, :], QKV[:, s, a, :], vec(g), ARR[:, a, :], ALU.mult, ALU.mult), [t])
            b, f = abank.take()
            t = pe.put(lambda e: e.matmul(b[0:32, :], RP[:, :], qkf[0:32], start=True, stop=True), [tn, t_rp] + f)
            yield
            t1 = dve.put(lambda e: e.tensor_tensor(
                AT1[:, :, :], b[0:32, :].rearrange("p (a t) -> p a t", a=2),
                RC[:, 1, :].unsqueeze(1).broadcast_to([32, 2, T]), ALU.mult), [t, t_rc] + pre)
            abank.give(b, [t1])
            t2 = dve.put(lambda e: e.tensor_tensor(
                qk[0:32], qk[0:32], RC[:, 0, :].unsqueeze(1).broadcast_to([32, 2, T]), ALU.mult), [t])
            t2 = dve.put(lambda e: e.tensor_tensor(qk[0:32], qk[0:32], AT1[:, :, :], ALU.add), [t1, t2])
            b, f = abank.take()
            for qt in range(2):
                t = pe.put(lambda e, qt=qt: e.matmul(b[:, qt * T:qt * T + T], QKV[:, s, 0, qt * 128:qt * 128 + 128],
                                                     QKV[:, s, 1, :], start=True, stop=True, skip_group_check=True),
                           [t2] + f)
            t_qk = t
            yield
            t = dve.put(lambda e: e.scalar_tensor_tensor(
                ASM[:, :, :].rearrange("p a t -> p (a t)"), b[:, :], float(128 ** -0.5),
                MB[:, :, :].rearrange("p a t -> p (a t)"), ALU.mult, ALU.add), [t_qk, t_mb] + pre)
            abank.give(b, [t])
            t = dve.put(lambda e: e.tensor_reduce(ANM[:, :], ASM[:, :, :], AX.X, ALU.max, negate=True), [t] + pre)
            for qt in range(2):
                t2 = act.put(lambda e, qt=qt: e.activation(AP_[:, qt, :], ASM[:, qt, :], ACT.Exp,
                                                           bias=ANM[:, qt:qt + 1], accum_out=ADN[:, qt:qt + 1]),
                             [t] + av["p"] + pre)
            yield
            t2 = dve.put(lambda e: e.reciprocal(ARD[:, :], ADN[:, :]), [t2])
            for qt in range(2):
                t3 = dve.put(lambda e, qt=qt: e.tensor_scalar(AP_[:, qt, :], AP_[:, qt, :], ARD[:, qt:qt + 1], None,
                                                              ALU.mult), [t2])
            yield
            b, f = abank.take()
            for kt in range(2):
                for qt in range(2):
                    t = pe.put(lambda e, kt=kt, qt=qt: e.transpose(
                        b[:, kt * T + qt * 128:kt * T + qt * 128 + 128], AP_[:, qt, kt * 128:kt * 128 + 128],
                        IDENT[:, :]), [t3] + f)
            av["p"] = [t]
            t = act.put(lambda e: e.activation(APT[:, :, :].rearrange("p a t -> p (a t)"), b[:, :], ACT.Copy),
                        [t] + av["pt"] + pre)
            abank.give(b, [t])
            yield
            b, f = abank.take()
            for kt in range(2):
                to = pe.put(lambda e, kt=kt: e.matmul(b[:, 0:T], AVN[:, kt, :], APT[:, kt, :], start=(kt == 0),
                                                      stop=(kt == 1)), [t, tvn] + f)
            av["pt"] = [to]
            av["vn"] = [to]
            th = dve.put(lambda e: e.tensor_copy(MH[:, 4 + h, :], b[:, 0:T]), [to])
            tl = dve.put(lambda e: e.tensor_tensor(ML[:, 4 + h, :], b[:, 0:T], MH[:, 4 + h, :].bitcast(F32),
                                                   ALU.subtract), [th])
            abank.give(b, [tl])
            t_m[4 + h] = [th, tl]
            qkv_free[s] = [t_qk, tv]
            yield

        qkv_free = [[], [], []]
        gens = []
        for h in range(12):
            if h >= 3:
                drain(gens[h - 3])
            tq = []
            for j in range(3):
                bank, ps, t = tile_k(A, t_a, steps=2 if h < 9 else 3)
                tq.append(evac_r(QKV[:, h % 3, j, :], bank, ps, t, after=qkv_free[h % 3]))
            gens.append(attn(h, tq))
            bg.append(gens[h])
        drain()
        end_b1 = [(pe.sem, pe.count), (act.sem, act.count), (dve.sem, dve.count)]
        sA.close()
        sB.close()

        a_free = [t_used[st["used"] - 1]]

        def out_tiles(n_tiles, src, ticks, nk, evac):
            n0 = 0
            if nk == 32:
                hi, lo = src
                held = [mbank.take() for _ in range(4)]
                done = {}
                for c in range(2):
                    if c:
                        drain()
                    for n in range(4):
                        bank, freed = held[n]
                        done[n] = chunk([(bank[:, 0:T], b, hi[:, 16 * c + b, :], lo[:, 16 * c + b, :],
                                          c == 0 and b == 0, c == 1 and b == 15,
                                          (freed if c == b == 0 else []) + ticks[16 * c + b], None)
                                         for b in range(16)], 2)
                        if c:
                            evac(n, held[n][0], held[n][0][:, 0:T], done[n])
                n0 = 4
            for n in range(n0, n_tiles):
                bank, ps, t = tile_k(src, ticks, nk)
                evac(n, bank, ps, t)

        def resid(n, bank, ps, t):
            tx = dve.put(lambda e: e.tensor_tensor(XT[:, n, :], XT[:, n, :], ps, ALU.add), [t] + t_xt2)
            mbank.give(bank, [tx])
            square(XT[:, n, :], [tx], n, KD)
            prep(n, XT[:, n, :], vec("norm2_g", n), [tx], a_free)

        out_tiles(16, (MH, ML), t_m, 16, resid)
        t_r = norm_stat(D)
        end_m = [(pe.sem, pe.count), (act.sem, act.count), (dve.sem, dve.count)]
        s1.close()

        sP = ExitStack()
        NX = max(PARTS[0][1], PARTS[2][1])
        NY = max(PARTS[1][1], PARTS[3][1])
        GA = sb("GA", [128, NX + NY, T], c=sP)
        I1T = sb("I1T", [128, T], c=sP)
        I2T = sb("I2T", [128, T], c=sP)
        GTT = sb("GTT", [128, T], c=sP)
        IOTA = sb("IOTA", [128, 128], c=sP)
        t_iota = load(IOTA[:, :], d["c_iota"][:, :], end_b1 + end_m, q=act)
        sQ = ExitStack()
        QY = GA[:, 56:72, :]
        SK = GA[:, 32:40, :].rearrange("p n t -> p (n t)").rearrange("p (c k) -> p c k", c=16)
        SC = GA[:, 40:56, :].rearrange("p n t -> p (n t)").rearrange("p (a c k) -> p a c k", a=2, c=16)
        TV = sb("TV", [128, 2, 16, 16], c=sQ)
        TI = sb("TI", [128, 16, 16], U32, c=sQ)
        TF = sb("TF", [128, 2, 16, 16], c=sQ)
        BV = sb("BV", [128, 2, 8, 16], c=sQ)
        BPI = sb("BPI", [128, 128], U32, c=sQ)
        BPX = sb("BPX", [128, 2, 128], U32, c=sQ)
        BPF = sb("BPF", [128, 2, 128], c=sQ)
        CD = sb("CD", [128, 16, 16], c=sQ)
        EQ = GA[:, 56:64, :].rearrange("p n t -> p (n t)").rearrange("p (c k) -> p c k", k=16)
        IX = sb("IX", [128, 3, 128], c=sQ)
        ES = sb("ES", [128, 16], c=sQ)
        t_sk = load(SK[:, :, :], d["sub_keys"].rearrange("p (c k) -> p c k", c=16), end_b1 + end_m, q=act)
        t_q = {}

        def evac_q(n, bank, ps, t):
            t_q[n] = evac_r(QY[:, n, :], bank, ps, t, after=end_b1 + end_m)

        out_tiles(16, A, t_a, 16, evac_q)
        qy_done = []
        sc_done = []

        def topk():
            t_sc = {}
            for q in range(4):
                for a in range(2):
                    b, f = abank.take()
                    for c in range(4):
                        hc = 4 * q + c
                        t = pe.put(lambda e, b=b, c=c, hc=hc, a=a: e.matmul(
                            b[:, c * 128:c * 128 + 128], QY[:, hc, a * 128:a * 128 + 128], SK[:, hc, :], start=True,
                            stop=True, skip_group_check=True), [t_q[hc], t_sk] + f)
                    qy_done[:] = [t]
                    tc = act.put(lambda e, b=b, q=q, a=a: e.activation(
                        SC[:, a, 4 * q:4 * q + 4, :], b[:, :].rearrange("p (c k) -> p c k", c=4), ACT.Copy), [t])
                    abank.give(b, [tc])
                    for c in range(4):
                        t_sc[a, 4 * q + c] = tc
                yield
            st["qy"] = True
            t_ix = []
            for a in range(2):
                for hc in range(16):
                    v = SC[:, a, hc, :]
                    m1, m2 = TV[:, a, hc, 0:8], TV[:, a, hc, 8:16]
                    i1, i2 = TI[:, hc, 0:8], TI[:, hc, 8:16]
                    t = dve.put(lambda e, v=v, m1=m1: e.max(m1, v), [t_sc[a, hc]])
                    t = dve.put(lambda e, v=v, m1=m1, i1=i1: e.max_index(i1, m1, v), [t] + t_ix)
                    t = dve.put(lambda e, v=v, m1=m1: e.match_replace(v, m1, v, NEG), [t])
                    t = dve.put(lambda e, v=v, m2=m2: e.max(m2, v), [t])
                    t = dve.put(lambda e, v=v, m2=m2, i2=i2: e.max_index(i2, m2, v), [t])
                    yield
                t = dve.put(lambda e, a=a: e.tensor_copy(TF[:, a, :, :], TI[:, :, :]), [t])
                t_tf = t
                for h in range(8):
                    t = dve.put(lambda e, a=a, h=h: e.tensor_tensor(
                        CD[:, :, :], TV[:, a, 2 * h, :].unsqueeze(2).broadcast_to([128, 16, 16]),
                        TV[:, a, 2 * h + 1, :].unsqueeze(1).broadcast_to([128, 16, 16]), ALU.add), [t])
                    v = CD[:, :, :].rearrange("p a b -> p (a b)")
                    m1, m2 = BV[:, a, h, 0:8], BV[:, a, h, 8:16]
                    i1, i2 = BPI[:, 16 * h:16 * h + 8], BPI[:, 16 * h + 8:16 * h + 16]
                    t = dve.put(lambda e, v=v, m1=m1: e.max(m1, v), [t])
                    t = dve.put(lambda e, v=v, m1=m1, i1=i1: e.max_index(i1, m1, v), [t])
                    t = dve.put(lambda e, v=v, m1=m1: e.match_replace(v, m1, v, NEG), [t])
                    t = dve.put(lambda e, v=v, m2=m2: e.max(m2, v), [t])
                    t = dve.put(lambda e, v=v, m2=m2, i2=i2: e.max_index(i2, m2, v), [t])
                    yield
                t = dve.put(lambda e: e.tensor_single_scalar(BPX[:, 0, :], BPI[:, :], 4, ALU.logical_shift_right), [t])
                t = dve.put(lambda e: e.tensor_single_scalar(BPX[:, 1, :], BPI[:, :], 15, ALU.bitwise_and), [t])
                t = dve.put(lambda e: e.tensor_copy(BPF[:, :, :], BPX[:, :, :]), [t])
                for c in range(2):
                    t = dve.put(lambda e, c=c: e.tensor_tensor(
                        EQ[:, :, :], BPF[:, c, :].unsqueeze(2).broadcast_to([128, 128, 16]),
                        IOTA[:, 0:16].unsqueeze(1).broadcast_to([128, 128, 16]), ALU.is_equal), [t, t_iota] + qy_done)
                    yield
                    for h in range(8):
                        t2 = dve.put(lambda e, c=c, a=a, h=h: e.tensor_tensor(
                            EQ[:, 16 * h:16 * h + 16, :], EQ[:, 16 * h:16 * h + 16, :],
                            TF[:, a, 2 * h + c, :].unsqueeze(1).broadcast_to([128, 16, 16]), ALU.mult), [t, t_tf])
                    t = t2
                    yield
                    t = dve.put(lambda e, c=c: e.tensor_reduce(IX[:, c, :], EQ[:, :, :], AX.X, ALU.add), [t] + t_ix)
                    yield
                bv = BV[:, a, :, :]
                G3 = IX[:, 2, :].rearrange("p (h k) -> p h k", h=8)
                t = dve.put(lambda e, bv=bv, G3=G3, a=a: e.tensor_tensor(
                    G3, bv, BV[:, a, :, 0:1].broadcast_to([128, 8, 16]), ALU.subtract), [t] + t_ix)
                t = act.put(lambda e: e.activation(IX[:, 2, :], IX[:, 2, :], ACT.Exp), [t])
                t = dve.put(lambda e, G3=G3: e.tensor_reduce(ES[:, 0:8], G3, AX.X, ALU.add), [t])
                t = dve.put(lambda e: e.reciprocal(ES[:, 8:16], ES[:, 0:8]), [t])
                t = dve.put(lambda e, G3=G3: e.tensor_tensor(
                    G3, G3, ES[:, 8:16].unsqueeze(2).broadcast_to([128, 8, 16]), ALU.mult), [t])
                yield
                b, f = abank.take()
                for c in range(3):
                    tp = pe.put(lambda e, b=b, c=c: e.transpose(b[:, c * 128:c * 128 + 128], IX[:, c, :], IDENT[:, :]),
                                [t] + f)
                t_ix = [tp]
                for c, dst in enumerate((I1T, I2T, GTT)):
                    t_idx[a, c] = act.put(lambda e, b=b, c=c, dst=dst, a=a: e.activation(
                        dst[:, a * 128:a * 128 + 128], b[:, c * 128:c * 128 + 128], ACT.Copy), [tp])
                abank.give(b, [t_idx[a, 2]])
                yield

        t_idx = {}
        gen_topk = topk()
        bg.append(gen_topk)
        tmp_free = [[], []]
        place = [0, NX, 0, NX]
        ga_free = {}
        t_act = [{} for _ in PARTS]
        t_g = {}
        NB = 8

        def phase_a(p, steps, pre=()):
            for jj in range(PARTS[p][1]):
                slot = place[p] + jj
                bank, ps, t = tile_k(A, t_a, steps=steps)
                s = jj % 2
                tt = dve.put(lambda e: e.tensor_tensor(TMP[:, s, :], ps, R[:, :], ALU.mult),
                             [t, t_r] + tmp_free[s])
                mbank.give(bank, [tt])
                r_read[:] = [tt]
                extra = ga_free.get(slot, []) + list(pre)
                if p == 0 and slot >= 32:
                    assert st["qy"]
                    extra += qy_done
                ta = act.put(lambda e: e.activation(GA[:, slot, :], TMP[:, s, :], ACT.Gelu_apprx_tanh),
                             [tt] + extra)
                tmp_free[s] = [ta]
                t_act[p][jj] = ta

        def gates(p):
            p0, n = PARTS[p]
            nq = T // NB
            t_hot = {}

            def hot(q):
                s = q % 2
                a = q * NB // 128
                after = [t_idx[a, 0], t_idx[a, 1], t_idx[a, 2], t_iota] + ob_free[s]
                for k in range(NB):
                    tok = q * NB + k
                    dve.put(lambda e: e.tensor_scalar(
                        OA[:, s, k, :], IOTA[:, :], I1T[:, tok:tok + 1], GTT[:, tok:tok + 1], ALU.is_equal,
                        ALU.mult), after, inc=False)
                t_hot[q] = dve.put(lambda e: e.tensor_tensor(
                    OB[:, s, :, 0:n], IOTA[:, p0:p0 + n].unsqueeze(1).broadcast_to([128, NB, n]),
                    I2T[:, q * NB:q * NB + NB].unsqueeze(2).broadcast_to([128, NB, n]), ALU.is_equal), after)

            def times(q, b, t):
                G = GA[:, place[p]:place[p] + n, q * NB:q * NB + NB].rearrange("p j t -> p t j")
                t_g[p] = dve.put(lambda e: e.tensor_tensor(
                    G, G, b[:, 0:NB * n].rearrange("p (t j) -> p t j", j=n), ALU.mult), [t, t_act[p][n - 1]])
                abank.give(b, [t_g[p]])

            hot(0)
            yield
            held = None
            for q in range(nq):
                if held:
                    times(q - 1, *held)
                s = q % 2
                b, f = abank.take()
                for k in range(NB):
                    t = pe.put(lambda e: e.matmul(b[:, k * n:k * n + n], OA[:, s, k, :], OB[:, s, k, 0:n], start=True,
                                                  stop=True, skip_group_check=True), [t_hot[q]] + f, inc=k == NB - 1)
                ob_free[s] = [t]
                held = (b, t)
                if q + 1 < nq:
                    hot(q + 1)
                yield
            times(nq - 1, *held)

        def coef(p, jj, s):
            slot = place[p] + jj
            th = dve.put(lambda e: e.tensor_copy(CH[:, s, :], GA[:, slot, :]), [t_g[p]] + c_free[s])
            tl = dve.put(lambda e: e.tensor_tensor(CL[:, s, :], GA[:, slot, :], CH[:, s, :].bitcast(F32),
                                                   ALU.subtract), [th])
            ga_free[slot] = [tl]
            return [tl]

        t_x = {}

        def phase_b(p, steps):
            n = PARTS[p][1]
            taken = [mbank.take() for _ in range(4)] + [abank.take() for _ in range(3)]
            freed = [x for _, f in taken for x in f]
            for jj in range(n):
                s = jj % 2
                tc = coef(p, jj, s)
                jobs = [(taken[dt // 2][0][:, (dt % 2) * T:(dt % 2) * T + T], dt, CH[:, s, :], CL[:, s, :],
                         jj == 0 and dt % 2 == 0, jj == n - 1, tc + (freed if jj == 0 else []), None)
                        for dt in range(14)]
                t = chunk(jobs, steps)
                c_free[s] = [t]
            for dt in range(14):
                bank = taken[dt // 2][0]
                t_x[dt] = dve.put(lambda e: e.tensor_tensor(
                    XT[:, dt, :], XT[:, dt, :], bank[:, (dt % 2) * T:(dt % 2) * T + T], ALU.add), [t])
                if dt % 2:
                    (mbank if dt < 8 else abank).give(bank, [t_x[dt]])
            bank, freed = mbank.take()
            for j0 in range(0, n, TAIL):
                jobs = []
                for j in range(TAIL):
                    jj = j0 + j
                    jobs.append((jj, [(bank[:, dt * T:dt * T + T], 2 * j + dt, CH[:, jj % 2, :], CL[:, jj % 2, :],
                                       jj == 0 and dt == 0, jj == n - 1) for dt in range(2)]))
                t = tail_chunk(p, jobs, freed)
            for dt in range(2):
                t_x[14 + dt] = dve.put(lambda e: e.tensor_tensor(
                    XT[:, 14 + dt, :], XT[:, 14 + dt, :], bank[:, dt * T:dt * T + T], ALU.add), [t])
            mbank.give(bank, [t_x[15]])

        def tail_chunk(p, jobs, freed):
            full = []
            tc = {}
            for i, (jj, two) in enumerate(jobs):
                mark = [None]
                full.append((jj, two, mark))
            def before(i):
                if i < len(full):
                    tc[i] = coef(p, full[i][0], full[i][0] % 2)
            before(0)
            before(1)
            flat = []
            for i, (jj, two, mark) in enumerate(full):
                for dt, (ps, b, xh, xl, first, last) in enumerate(two):
                    def after(i=i):
                        return tc[i] + freed
                    def then(tick, i=i, jj=jj):
                        c_free[jj % 2] = [tick]
                        before(i + 2)
                    flat.append((ps, b, xh, xl, first, last, after, then if dt else None))
            return chunk(flat, 1)

        phase_a(0, 2, end_b1 + end_m)
        drain(gen_topk)
        end_q = [(pe.sem, pe.count), (act.sem, act.count), (dve.sem, dve.count)]
        sQ.close()
        sO = ExitStack()
        OA = sb("OA", [128, 2, NB, 128], c=sO)
        OB = sb("OB", [128, 2, NB, NX], c=sO)
        CH = sb("CH", [128, 2, T], FR, c=sO)
        CL = sb("CL", [128, 2, T], FR, c=sO)
        ob_free = [list(end_q), list(end_q)]
        c_free = [list(end_q), list(end_q)]
        bg.append(gates(0))
        phase_a(1, 1, end_q)
        drain()
        bg.append(gates(1))
        phase_b(0, 1)
        drain()
        phase_a(2, 1)
        bg.append(gates(2))
        phase_b(1, 1)
        drain()
        phase_a(3, 1)
        bg.append(gates(3))
        phase_b(2, 1)
        drain()
        phase_b(3, 1)
        end_p = [(pe.sem, pe.count), (act.sem, act.count), (dve.sem, dve.count), (pool.sem, pool.count)]
        a_free = [t_used[st["used"] - 1]]
        sO.close()
        sP.close()

        s2 = ExitStack()
        PH = sb("PH", [128, 2, T], FR, c=s2)
        PL = sb("PL", [128, 2, T], FR, c=s2)
        INV = sb("INV", [128, 4, 16], c=s2)
        SP8 = sb("SP8", [128, 3, 32], c=s2)
        t_inv = load(INV[:, :, :], d["c_inv"].rearrange("p (g t) -> p g t", g=4), end_p)
        act.put(lambda e: e.preload_act_table_set(SETS["logexp"]), inc=False)
        Lv = VEC[:, VOFF["lru_L_2"]:VOFF["lru_L_2"] + 32]
        E_, Y_, M_ = SP8[:, 0, :], SP8[:, 1, :], SP8[:, 2, :]
        t = act.put(lambda e: e.activation(Y_, Lv, ACT.Abs), end_p)
        t = act.put(lambda e: e.activation(E_, Y_, ACT.Exp, scale=-1.0), [t])
        t = dve.put(lambda e: e.tensor_scalar(Y_, E_, 1.0, None, ALU.add), [t])
        t1 = act.put(lambda e: e.activation(M_, Y_, ACT.Ln), [t] + end_p)
        t2 = dve.put(lambda e: e.scalar_tensor_tensor(E_, Y_, -1.0, E_, ALU.add, ALU.subtract), [t1])
        t2 = dve.put(lambda e: e.reciprocal(Y_, Y_), [t2])
        t2 = dve.put(lambda e: e.tensor_tensor(E_, E_, Y_, ALU.mult), [t2])
        t2 = dve.put(lambda e: e.tensor_tensor(M_, M_, E_, ALU.subtract), [t2])
        t2 = dve.put(lambda e: e.tensor_scalar(Y_, Lv, -1.0, 0.0, ALU.mult, ALU.max), [t2])
        t2 = dve.put(lambda e: e.tensor_tensor(Y_, Y_, M_, ALU.add), [t2])
        t2 = dve.put(lambda e: e.tensor_scalar(M_, Y_, -8.0, None, ALU.mult), [t2])
        t_sp = dve.put(lambda e: e.tensor_scalar(Y_, Y_, 8.0, None, ALU.mult), [t2])

        for k in range(KD):
            square(XT[:, k, :], [t_x[k]], k, KD)
            prep(k, XT[:, k, :], vec("g_pre_2", k), [t_x[k]], a_free)
        t_r = norm_stat(D)

        def marks_now():
            return [(pe.sem, pe.count), (act.sem, act.count), (dve.sem, dve.count)]

        prev = list(end_p)
        for l in range(2):
            sY = ExitStack()
            YH = sb(f"YH{l}", [128, 32, T], FR, c=sY)
            YL = sb(f"YL{l}", [128, 32, T], FR, c=sY)
            s3 = ExitStack()
            PT = sb(f"PT{l}", [128, 2, T], c=s3)
            t_pt = load(PT[:, :, :], d["p_2"].rearrange("p (l k t) -> p l k t", l=2, k=2)[:, l], prev)
            th = act.put(lambda e, PT=PT: e.activation(PH[:, :, :], PT[:, :, :], ACT.Copy), [t_pt] + prev)
            t_p2 = dve.put(lambda e, PT=PT: e.tensor_tensor(PL[:, :, :], PT[:, :, :], PH[:, :, :].bitcast(F32),
                                                            ALU.subtract), [th] + prev)
            s3.close()
            prev = prev + [t_p2]
            sU = ExitStack()
            t_y = {}
            if l == 0:
                DH = sb("DH", [128, 8, T], FR, c=sU)
                DL = sb("DL", [128, 8, T], FR, c=sU)
                ZS = sb("ZS", [128, 4, T], c=sU)
                UP = sb("UP", [128, 3, 16 + T], c=sU)
                t = dve.put(lambda e: e.memset(UP[:, :, 0:16], 0.0), prev)
                t_up0 = t
                d_free = []
                for g in range(4):
                    w = 2 << g
                    t_d = {}
                    for i in range(8):
                        bank, ps, t = tile_k(A, t_a)
                        U = UP[:, 0, 16:16 + T]
                        t = dve.put(lambda e, ps=ps, U=U: e.tensor_tensor(U, ps, R[:, :], ALU.mult), [t, t_r, t_up0])
                        mbank.give(bank, [t])
                        src = 0
                        for k in range(g + 1):
                            dst = 1 + k % 2
                            sh = 1 << k
                            t = dve.put(lambda e, src=src, dst=dst, sh=sh: e.tensor_tensor(
                                UP[:, dst, 16:16 + T], UP[:, src, 16:16 + T], UP[:, src, 16 - sh:16 + T - sh],
                                ALU.add), [t])
                            src = dst
                        s = i % 2
                        t2 = dve.put(lambda e, src=src, s=s, w=w: e.scalar_tensor_tensor(
                            TMP[:, s, :], UP[:, src, 16:16 + T], 1.0 / w, UP[:, 0, 16:16 + T], ALU.mult,
                            ALU.subtract), [t] + tmp_free[s])
                        t = dve.put(lambda e, src=src, g=g: e.tensor_tensor(
                            UP[:, src, 16:32], UP[:, src, 16:32], INV[:, g, :], ALU.mult), [t2, t_inv])
                        t = dve.put(lambda e, src=src, s=s: e.tensor_tensor(
                            TMP[:, s, 0:16], UP[:, src, 16:32], UP[:, 0, 16:32], ALU.subtract), [t])
                        th = dve.put(lambda e: e.tensor_copy(DH[:, i, :], TMP[:, s, :]), [t] + d_free + prev)
                        tl = dve.put(lambda e, s=s, i=i: e.tensor_tensor(DL[:, i, :], TMP[:, s, :],
                                                                        DH[:, i, :].bitcast(F32), ALU.subtract),
                                     [th])
                        tmp_free[s] = [th]
                        t_d[i] = [th, tl]
                    t_z = {}
                    for half in range(2):
                      for i in range(4 * half, 4 * half + 4):
                          bank, ps, t = tile_k(A, t_a)
                          t = dve.put(lambda e, ps=ps, i=i: e.tensor_tensor(ZS[:, i % 4, :], ps, R[:, :], ALU.mult),
                                      [t, t_r])
                          mbank.give(bank, [t])
                          r_read[:] = [t]
                          t_z[i] = act.put(lambda e, i=i: e.activation(ZS[:, i % 4, :], ZS[:, i % 4, :], ACT.Silu), [t])
                      for c in range(2 * half, 2 * half + 2):
                          jobs = []
                          held = []
                          for o in range(2):
                              bank, freed = mbank.take()
                              mark = []
                              held.append((bank, mark))
                              for k in range(8):
                                  jobs.append((bank[:, 0:T], o * 8 + k, DH[:, k, :], DL[:, k, :], k == 0, k == 7,
                                               freed + t_d[k], mark.append if k == 7 else None))
                          d_free = [chunk(jobs)]
                          for o in range(2):
                              i = 2 * c + o
                              n = 8 * g + i
                              bank, mark = held[o]
                              ps = bank[:, 0:T]
                              s = i % 2
                              t = dve.put(lambda e, ps=ps, s=s, n=n: e.tensor_scalar(
                                  TMP[:, s, :], ps, vec("pool_b_2", n), vec("pool_scale_2", n), ALU.add, ALU.mult),
                                  [mark[-1]] + tmp_free[s])
                              mbank.give(bank, [t])
                              t = dve.put(lambda e, s=s, i=i: e.tensor_tensor(TMP[:, s, :], TMP[:, s, :], ZS[:, i % 4, :],
                                                                             ALU.mult), [t, t_z[i]])
                              th = dve.put(lambda e: e.tensor_copy(YH[:, n, :], TMP[:, s, :]), [t] + prev)
                              tl = dve.put(lambda e, s=s, n=n, YH=YH, YL=YL: e.tensor_tensor(
                                  YL[:, n, :], TMP[:, s, :], YH[:, n, :].bitcast(F32), ALU.subtract), [th])
                              tmp_free[s] = [th]
                              t_y[n] = [th, tl]
            else:
                UP = sb("UQ", [128, 4 + T], c=sU)
                UCS = sb("UCS", [128, 2, 4, T], c=sU)
                ZB = sb("ZB", [128, 4, T], c=sU)
                RG = sb("RG", [128, 4, T], c=sU)
                IG = sb("IG", [128, 4, T], c=sU)
                t_u0 = dve.put(lambda e: e.memset(UP[:, 0:4], 0.0), prev)
                rg_read, ig_read, uc_read, z_read = [], [], [[], []], []

                def recur(g, tg, held, t_z):
                    UC = UCS[:, g % 2]
                    for ax, dst, bn, rd in ((0, RG, "lru_ba_2", rg_read), (1, IG, "lru_bx_2", ig_read)):
                        for hh in range(2):
                            bank = held[2 * hh + ax]
                            for o in range(2):
                                i = 2 * hh + o
                                ts = act.put(lambda e: e.activation(
                                    dst[:, i, :], bank[:, o * T:o * T + T], ACT.Sigmoid, bias=vec(bn, 4 * g + i)),
                                    [tg] + rd + prev)
                            abank.give(bank, [ts])
                        yield
                    t1 = dve.put(lambda e: e.tensor_tensor(UC, UC, IG[:, :, :], ALU.mult), [ts])
                    for i in range(4):
                        n = 4 * g + i
                        t2 = act.put(lambda e: e.activation(IG[:, i, :], RG[:, i, :], ACT.Tanh,
                                                            scale=SP8[:, 1, n:n + 1]), [ts, t_sp, t1])
                    for i in range(4):
                        n = 4 * g + i
                        t4 = act.put(lambda e: e.activation(RG[:, i, :], RG[:, i, :], ACT.Exp,
                                                            scale=SP8[:, 2, n:n + 1]), [t2])
                    yield
                    for q in range(2):
                        t5 = dve.put(lambda e: e.tensor_tensor(
                            TMP[:, :, :], RG[:, 2 * q:2 * q + 2, :], RG[:, 2 * q:2 * q + 2, :], ALU.mult),
                            [t4] + tmp_free[0] + tmp_free[1])
                        t5 = dve.put(lambda e: e.scalar_tensor_tensor(
                            IG[:, 2 * q:2 * q + 2, :], TMP[:, :, :], 1.0, IG[:, 2 * q:2 * q + 2, :], ALU.add,
                            ALU.mult), [t5])
                        tmp_free[0] = tmp_free[1] = [t5]
                    t5 = dve.put(lambda e: e.tensor_scalar(IG[:, :, :], IG[:, :, :], 0.0, None, ALU.max), [t5])
                    t6 = act.put(lambda e: e.activation(IG[:, :, :], IG[:, :, :], ACT.Sqrt), [t5])
                    yield
                    t7 = dve.put(lambda e: e.tensor_tensor(UC, UC, IG[:, :, :], ALU.mult), [t6])
                    for i in range(4):
                        t8 = dve.put(lambda e: e.tensor_tensor_scan(IG[:, i, :], RG[:, i, :], UC[:, i, :], 0.0,
                                                                    ALU.mult, ALU.add), [t7, t4])
                    uc_read[g % 2] = rg_read[:] = [t8]
                    yield
                    t9 = dve.put(lambda e: e.tensor_tensor(ZB[:, :, :], ZB[:, :, :], IG[:, :, :], ALU.mult),
                                 [t8, t_z])
                    ig_read[:] = [t9]
                    n0 = 4 * g
                    th = dve.put(lambda e: e.tensor_copy(YH[:, n0:n0 + 4, :], ZB[:, :, :]), [t9, tg] + prev)
                    tl = dve.put(lambda e: e.tensor_tensor(
                        YL[:, n0:n0 + 4, :], ZB[:, :, :], YH[:, n0:n0 + 4, :].bitcast(F32), ALU.subtract), [th])
                    z_read[:] = [tl]
                    for i in range(4):
                        t_y[n0 + i] = [tl]
                    yield

                conv_prev = [t_u0]
                for g in range(8):
                    UH, UL = YH[:, 4 * g:4 * g + 4, :], YL[:, 4 * g:4 * g + 4, :]
                    UC = UCS[:, g % 2]
                    t_d = {}
                    for i in range(4):
                        n = 4 * g + i
                        bank, ps, t = tile_k(A, t_a, steps=2)
                        t = dve.put(lambda e: e.tensor_tensor(UP[:, 4:4 + T], ps, R[:, :], ALU.mult),
                                    [t, t_r] + conv_prev)
                        mbank.give(bank, [t])
                        t = dve.put(lambda e: e.tensor_scalar(
                            UC[:, i, :], UP[:, 4:4 + T], vec("conv_w_2", 96 + n), vec("conv_b_2", n), ALU.mult,
                            ALU.add), [t] + uc_read[g % 2])
                        for k in (2, 1, 0):
                            t = dve.put(lambda e: e.scalar_tensor_tensor(
                                UC[:, i, :], UP[:, 1 + k:1 + k + T], vec("conv_w_2", 32 * k + n), UC[:, i, :],
                                ALU.mult, ALU.add), [t])
                        conv_prev = [t]
                        th = dve.put(lambda e: e.tensor_copy(UH[:, i, :], UC[:, i, :]), [t] + prev)
                        tl = dve.put(lambda e: e.tensor_tensor(UL[:, i, :], UC[:, i, :],
                                                               UH[:, i, :].bitcast(F32), ALU.subtract), [th])
                        t_d[i] = [tl]
                    drain()
                    zs = []

                    def z_mult():
                        i, ts = zs.pop(0)
                        tz = dve.put(lambda e: e.tensor_tensor(ZB[:, i, :], ZB[:, i, :], TMP[:, i % 2, :], ALU.mult),
                                     [ts])
                        tmp_free[i % 2] = [tz]
                        return tz

                    for i in range(4):
                        bank, ps, t = tile_k(A, t_a)
                        t_zz = dve.put(lambda e: e.tensor_tensor(ZB[:, i, :], ps, R[:, :], ALU.mult),
                                       [t, t_r] + z_read)
                        mbank.give(bank, [t_zz])
                        r_read[:] = [t_zz]
                        ts = act.put(lambda e: e.activation(TMP[:, i % 2, :], ZB[:, i, :], ACT.Sigmoid),
                                     [t_zz] + tmp_free[i % 2])
                        if zs:
                            z_mult()
                        zs.append((i, ts))
                    jobs = []
                    held = []
                    for hh in range(2):
                        for ax in range(2):
                            bank, freed = abank.take()
                            held.append(bank)
                            for o in range(2):
                                for k in range(2):
                                    jobs.append((bank[:, o * T:o * T + T], ((hh * 2 + ax) * 2 + k) * 2 + o,
                                                 UH[:, 2 * hh + k, :], UL[:, 2 * hh + k, :], k == 0 and o == 0,
                                                 k == 1, freed + t_d[2 * hh + k], None))
                    tg = chunk(jobs)
                    tz = z_mult()
                    bg.append(recur(g, tg, held, tz))
            a_free = [t_used[st["used"] - 1]]
            sU.close()
            sO2 = ExitStack()
            OO = sb(f"OO{l}", [128, 16, T], c=sO2)

            t_o = {}
            end_u = []

            def evac_o(n, bank, ps, t):
                if n == 0:
                    drain()
                    end_u[:] = marks_now()
                t_o[n] = act.put(lambda e: e.activation(OO[:, n, :], ps, ACT.Copy,
                                                        scale=vec("g_post_2", 16 * l + n)), [t] + end_u)
                ts = square(ps, [t], n, KD)
                mbank.give(bank, [t_o[n], ts])

            out_tiles(16, (YH, YL), t_y, 32, evac_o)
            end_y = marks_now()
            t_ro = norm_stat(D)
            sO2.close()
            sY.close()
            sE = ExitStack()
            EE = sb(f"EE{l}", [128, 16, T], c=sE)
            t_e = {}
            for c in range(2):
                jobs = []
                held = []
                for o in range(8):
                    if o % 2 == 0:
                        bank, freed = mbank.take()
                        held.append((bank, []))
                    for k in range(2):
                        jobs.append((bank[:, (o % 2) * T:(o % 2) * T + T], o * 2 + k, PH[:, k, :], PL[:, k, :],
                                     k == 0 and o % 2 == 0, k == 1, freed + [t_p2],
                                     held[-1][1].append if (o % 2 and k == 1) else None))
                chunk(jobs)
                for q, (bank, mark) in enumerate(held):
                    te = act.put(lambda e, c=c, q=q, bank=bank, EE=EE: e.activation(
                        EE[:, 8 * c + 2 * q:8 * c + 2 * q + 2, :], bank[:, :].rearrange("p (a t) -> p a t", a=2),
                        ACT.Copy), [mark[-1]] + end_y)
                    t_e[8 * c + 2 * q] = t_e[8 * c + 2 * q + 1] = te
                    mbank.give(bank, [te])
            for k in range(KD):
                t = dve.put(lambda e: e.tensor_tensor(OO[:, k, :], OO[:, k, :], R[:, :], ALU.mult),
                            [t_ro, t_o[k]])
                r_read[:] = [t]
                t = dve.put(lambda e, k=k, OO=OO: e.tensor_tensor(XT[:, k, :], XT[:, k, :], OO[:, k, :], ALU.add), [t])
                square(XT[:, k, :], [t], k, KD)
                prep(k, XT[:, k, :], vec("g_ple_in_2", 16 * l + k), [t], a_free)
            t_r = norm_stat(D)
            t_eg = {}

            def evac_g(n, bank, ps, t, EE=EE, t_r=t_r):
                s = n % 2
                t1 = dve.put(lambda e: e.tensor_tensor(TMP[:, s, :], ps, R[:, :], ALU.mult), [t, t_r] + tmp_free[s])
                mbank.give(bank, [t1])
                r_read[:] = [t1]
                t1 = act.put(lambda e: e.activation(TMP[:, s, :], TMP[:, s, :], ACT.Sigmoid), [t1])
                t1 = dve.put(lambda e: e.tensor_tensor(EE[:, n, :], EE[:, n, :], TMP[:, s, :], ALU.mult),
                             [t1, t_e[n]])
                tmp_free[s] = [t1]
                t_eg[n] = t1
                square(EE[:, n, :], [t1], n, KD)

            out_tiles(16, A, t_a, 16, evac_g)
            a_free = [t_used[st["used"] - 1]]
            t_rg = norm_stat(D)
            for k in range(KD):
                t = dve.put(lambda e, k=k, EE=EE, l=l: e.scalar_tensor_tensor(
                    EE[:, k, :], EE[:, k, :], vec("g_ple_out_2", 16 * l + k), R[:, :], ALU.mult, ALU.mult), [t_rg])
                r_read[:] = [t]
                t = dve.put(lambda e, k=k, EE=EE: e.tensor_tensor(XT[:, k, :], XT[:, k, :], EE[:, k, :], ALU.add), [t])
                if l == 0:
                    square(XT[:, k, :], [t], k, KD)
                    prep(k, XT[:, k, :], vec("g_pre_2", 16 + k), [t], a_free)
                elif k % 4 == 3:
                    q = k // 4
                    sp.dma(lambda e, q=q: e.dma_start(
                        out.rearrange("p (k t) -> p k t", k=KD)[:, 4 * q:4 * q + 4, :], XT[:, 4 * q:4 * q + 4, :]),
                        s_out, [t])
            if l == 0:
                t_r = norm_stat(D)
            prev = marks_now()
            sE.close()
        sp.wait([(s_out, 64)])
        s2.close()
        assert st["used"] == NCH, (st["used"], NCH)
        assert not sq["late"]


def _panels(np, w, kt=16):
    k, n = w.shape
    a = w.reshape(k // (kt * 128), kt, 128, n // 128, 128).transpose(3, 0, 2, 1, 4)
    return a.reshape(-1, 128, kt * 128)


def _layout(np, x):
    f = np.float32
    o = {}

    def col(v):
        v = np.asarray(v).reshape(-1)
        return v.reshape(-1, 128).T

    def tok(v):
        t, n = v.shape
        return v.T.reshape(n // 128, 128, t).transpose(1, 0, 2)

    cols = {}
    for name, _ in VECS:
        if name == "gla_bias":
            cols[name] = np.concatenate([col(x["gla_bias_f"]), col(x["gla_bias_b"])], axis=1)
        elif name == "eps":
            cols[name] = np.full((128, 1), 1e-6, f)
        elif name == "one":
            cols[name] = np.ones((128, 1), f)
        else:
            cols[name] = col(x[name])
    o["vecs"] = np.concatenate([cols[n] for n, _ in VECS], axis=1)
    o["xt"] = tok(x["x"][0]).reshape(128, -1)
    o["ones"] = np.ones((128, 128), f)
    o["ident"] = np.eye(128, dtype=f)
    w = x["w_in"][0]
    o["w_in"] = np.concatenate([_panels(np, w[:, 0:1024]), _panels(np, w[:, 1024:1152]),
                                _panels(np, w[:, 1056:1568]), _panels(np, w[:, 1568:])], axis=0)
    z = np.zeros((16, 256), f)
    o["gla_up"] = np.concatenate([np.concatenate([x["gla_up_f"][0], z], axis=1),
                                  np.concatenate([z, x["gla_up_b"][0]], axis=1)], axis=0)
    o["w_out"] = _panels(np, x["w_out"][0])
    o["w_query"] = _panels(np, x["peer_w_query"][0])
    o["sub_keys"] = x["peer_sub_keys"][0].reshape(16, 128, 128).transpose(2, 0, 1).reshape(128, 2048)
    o["peer_down"] = x["peer_down"][0].reshape(128, 128, 16, 128).transpose(1, 3, 2, 0).reshape(128, 128, 2048)
    o["peer_up"] = x["peer_up"][0]
    o["w_in_2"] = np.concatenate([_panels(np, x["w_in_2"][l]) for l in range(2)], axis=0)
    o["w_out_2"] = np.concatenate([_panels(np, x["w_out_2"][l]) for l in range(2)], axis=0)
    o["w_gate"] = np.concatenate([_panels(np, x["w_ple_gate_2"][l]) for l in range(2)], axis=0)
    pw = x["pool_w_2"][0].reshape(4, 8, 128, 4, 2, 128).transpose(0, 3, 2, 4, 1, 5)
    o["pool_w"] = pw.reshape(16, 128, 2048)
    pl = x["w_ple_2"].reshape(2, 2, 128, 2, 8, 128).transpose(0, 3, 2, 4, 1, 5)
    o["w_ple"] = pl.reshape(4, 128, 2048)
    lw = np.stack([x["lru_wa_2"][0], x["lru_wx_2"][0]], axis=1)
    lw = lw.reshape(8, 2, 2, 2, 128, 2, 128).transpose(0, 4, 1, 2, 3, 5, 6)
    o["lru_w"] = lw.reshape(8, 128, 2048)
    o["p_2"] = np.stack([tok(x["p_2"][l, 0]) for l in range(2)], axis=1).reshape(128, 1024)
    i = np.arange(256)
    rel = i[:, None] - i[None, :]
    cnt = (np.abs(rel) <= 64).astype(f) + (rel % 4 == 0).astype(f) + (rel % 16 == 0).astype(f)
    bias = np.where(cnt > 0, np.log(np.maximum(cnt, 1.0)), -1e30).astype(f)
    o["c_bias"] = bias.reshape(2, 128, 256).transpose(1, 0, 2).reshape(128, 512)
    j = np.arange(128)
    same = (j[:, None] // 64) == (j[None, :] // 64)
    mf = (same & (j[:, None] <= j[None, :])).astype(f)
    mb = (same & (j[:, None] > j[None, :])).astype(f)
    o["c_gmask"] = np.concatenate([mf, mb], axis=1)
    inv = np.float32(500000.0) ** (-np.arange(16, dtype=f) / f(16))
    ang = inv.astype(f)[:, None] * np.arange(256, dtype=f)[None, :]
    c, s = np.cos(ang).astype(f), np.sin(ang).astype(f)
    c2, s2 = np.concatenate([c, c], 0), np.concatenate([-s, s], 0)
    o["c_rope"] = np.concatenate([c2, s2], axis=1)
    rot = np.zeros((32, 32), f)
    rot[np.arange(16) + 16, np.arange(16)] = 1.0
    rot[np.arange(16), np.arange(16) + 16] = 1.0
    o["c_rot"] = rot
    o["c_scan"] = np.tile((i % 64 != 0).astype(f), (128, 1))
    o["c_iota"] = np.tile(j.astype(f), (128, 1))
    o["c_inv"] = np.tile(np.concatenate([1.0 / np.minimum(i[:16] + 1, w) for w in (2, 4, 8, 16)]).astype(f), (128, 1))
    return {k: np.ascontiguousarray(v) for k, v in o.items()}


def kernel(**inputs):
    import numpy as np
    import concourse.bacc as bacc
    from concourse.bass_utils import run_bass_kernel_spmd as run

    arrays = _layout(np, {k: np.asarray(v) for k, v in inputs.items()})
    nc = bacc.Bacc("TRN2", target_bir_lowering=False, num_devices=1, dynamic_dma_scratch_size=1024)
    d = {k: nc.dram_tensor("in_" + k, a.shape, mybir.dt.from_np(a.dtype), kind="ExternalInput").ap()
         for k, a in arrays.items()}
    out = nc.dram_tensor("out_0", (128, 4096), F32, kind="ExternalOutput").ap()
    build(nc, d, out)
    r = run(nc, [{"in_" + k: a for k, a in arrays.items()}], core_ids=[0])
    y = r.results[0]["out_0"].reshape(128, 16, 256).transpose(2, 1, 0).reshape(1, 256, 2048)
    return np.ascontiguousarray(y)
```

```python
from contextlib import ExitStack

import concourse.bass as bass
from concourse import mybir

F32 = mybir.dt.float32
FR = mybir.dt.float32r
U32 = mybir.dt.uint32
ALU = mybir.AluOpType
ACT = mybir.ActivationFunctionType
AX = mybir.AxisListType

T = 256
D = 2048
KD = 16
NRAW = 3
NSPL = 3
PARTS = [(0, 56), (56, 16), (72, 56)]
TAIL = 8
NEG = -3.0e38

VECS = [
    ("norm1_g", 16), ("norm2_g", 16), ("gla_bias", 4), ("gla_out_g", 4), ("q_norm_g", 1), ("k_norm_g", 1),
    ("g_pre_2", 32), ("g_post_2", 32), ("g_ple_in_2", 32), ("g_ple_out_2", 32),
    ("pool_b_2", 32), ("pool_scale_2", 32), ("conv_w_2", 128), ("conv_b_2", 32),
    ("lru_ba_2", 32), ("lru_bx_2", 32), ("lru_L_2", 32), ("eps", 1), ("one", 1),
]
VOFF = {}
_n = 0
for _k, _w in VECS:
    VOFF[_k] = _n
    _n += _w
NVEC = _n

SETS = {"logexp": "natural_log_exp_and_others", "gelu": "gelu_apprx_tanh_and_others",
        "sigmoid": "sigmoid_and_others"}


class Queue:

    def __init__(self, eng, sem):
        self.eng, self.sem = eng, sem
        self.count = 0
        self.seen = {}

    def wait(self, after):
        for sem, val in after:
            if self.seen.get(id(sem), 0) < val:
                self.seen[id(sem)] = val
                self.eng.wait_ge(sem, val)

    def put(self, fn, after=(), inc=True):
        self.wait(after)
        ins = fn(self.eng)
        if inc:
            ins.then_inc(self.sem, 1)
            self.count += 1
        return (self.sem, self.count)

    def dma(self, fn, sem, after=()):
        self.wait(after)
        fn(self.eng).then_inc(sem, 16)


class Pool:

    def __init__(self, places):
        self.free = [(p, []) for p in places]

    def take(self):
        assert self.free, "no place free"
        return self.free.pop(0)

    def give(self, place, ticks):
        self.free.append((place, list(ticks)))


class LazyTicks:

    def __init__(self, ticks, finish):
        self.ticks, self.finish = ticks, finish

    def get(self, k, default=()):
        while k not in self.ticks:
            self.finish()
        return self.ticks[k]

    __getitem__ = get


def build(nc, d, out):
    ctx = ExitStack()
    with ctx:
        def sb(name, shape, dt=F32, c=ctx):
            return c.enter_context(nc.sbuf_tensor(name, shape, dt))

        def sem(name):
            return ctx.enter_context(nc.semaphore(name))

        pe, act, dve, sp, pool = (
            Queue(e, sem("s_" + n)) for e, n in ((nc.tensor, "pe"), (nc.scalar, "act"), (nc.vector, "dve"),
                                                 (nc.sync, "sp"), (nc.gpsimd, "pool")))

        XT = sb("XT", [128, KD, T])
        AH = sb("AH", [128, KD, T], FR)
        AL = sb("AL", [128, KD, T], FR)
        RAW = sb("RAW", [128, NRAW, 2048])
        WH = sb("WH", [128, NSPL, 2048], FR)
        WL = sb("WL", [128, NSPL, 2048], FR)
        VEC = sb("VEC", [128, NVEC])
        ONES = sb("ONES", [128, 128])
        IDENT = sb("IDENT", [128, 128])
        SQ = sb("SQ", [128, 2, T])
        R = sb("R", [128, T])
        TMP = sb("TMP", [128, 2, T])
        banks = [ctx.enter_context(nc.psum_tensor(f"PS{i}", [128, 512], F32)) for i in range(8)]
        mbank = Pool(banks[0:4])
        abank = Pool(banks[4:8])

        raw_sem = [sem(f"s_raw{i}") for i in range(NRAW)]
        s_out = sem("s_out")
        nload = [0]

        def load(dst, src, after=(), q=sp):
            s = sem(f"s_ld{nload[0]}")
            nload[0] += 1
            q.dma(lambda e: e.dma_start(dst, src), s, after)
            return (s, 16)

        def vec(name, i=0, p0=0, p1=128):
            o = VOFF[name] + i
            return VEC[p0:p1, o:o + 1]

        t_vec = load(VEC[:, :], d["vecs"][:, :])
        x4 = d["xt"].rearrange("p (k t) -> p k t", k=KD)
        t_xts = [load(XT[:, 4 * i:4 * i + 4, :], x4[:, 4 * i:4 * i + 4, :]) for i in range(4)]
        t_ones = load(ONES[:, :], d["ones"][:, :], q=act)
        t_ident = load(IDENT[:, :], d["ident"][:, :], q=act)

        order = []
        winA = d["w_in"]
        for i in [8] + list(range(8)) + list(range(9, 13)):
            order.append(winA[i])
        for h in range(12):
            for j in range(3):
                order.append(winA[13 + 12 * j + h])
        order += [d["w_out"][i] for i in range(16)]
        order += [d["w_query"][i] for i in range(16)]
        down, up = d["peer_down"], d["peer_up"].rearrange("(i j) c -> i j c", j=128)

        def down_part(p):
            return [down[j] for j in range(PARTS[p][0], sum(PARTS[p]))]

        def up_part(p):
            p0, n = PARTS[p]
            return ([up[:, j, 0:1792] for j in range(p0, p0 + n)]
                    + [up[:, j:j + TAIL, 1792:2048] for j in range(p0, p0 + n, TAIL)])

        order += down_part(0) + down_part(1) + up_part(0) + down_part(2) + up_part(1) + up_part(2)
        for l in range(2):
            w2 = d["w_in_2"]
            if l == 0:
                for g in range(4):
                    order += [w2[8 * g + i] for i in range(8)]
                    for half in range(2):
                        order += [w2[32 + 8 * g + 4 * half + i] for i in range(4)]
                        order += [d["pool_w"][4 * g + 2 * half + i] for i in range(2)]
            else:
                for g in range(8):
                    order += [w2[64 + 4 * g + i] for i in range(4)]
                    order += [w2[96 + 4 * g + i] for i in range(4)]
                    order += [d["lru_w"][g]]
            order += [d["w_out_2"][32 * l + 2 * i + c] for c in range(2) for i in range(4)]
            order += [d["w_out_2"][32 * l + i] for i in range(8, 32)]
            order += [d["w_ple"][2 * l + i] for i in range(2)]
            order += [d["w_gate"][16 * l + i] for i in range(16)]
        NCH = len(order)

        t_hi, t_lo, t_used = {}, {}, {}
        st = {"fetched": 0, "hi": 0, "lo": 0, "used": 0}

        def width(c):
            n = 1
            for x in order[c].shape[1:]:
                n *= x
            return n

        def fetch(c):
            after = [t_hi[c - NRAW], t_lo[c - NRAW]] if c >= NRAW else []
            dst = RAW[:, c % NRAW, 0:width(c)]
            if len(order[c].shape) == 3:
                dst = dst.rearrange("p (a n) -> p a n", a=order[c].shape[1])
            sp.dma(lambda e: e.dma_start(dst, order[c]), raw_sem[c % NRAW], after)

        def split_hi(c):
            r, s, n = c % NRAW, c % NSPL, width(c)
            after = [(raw_sem[r], 16 * (c // NRAW + 1))] + ([t_used[c - NSPL]] if c >= NSPL else [])
            t_hi[c] = act.put(lambda e: e.activation(WH[:, s, 0:n], RAW[:, r, 0:n], ACT.Copy), after)

        def split_lo(c):
            r, s, n = c % NRAW, c % NSPL, width(c)
            after = [(raw_sem[r], 16 * (c // NRAW + 1)), t_hi[c]] + ([t_used[c - NSPL]] if c >= NSPL else [])
            t_lo[c] = dve.put(lambda e: e.tensor_tensor(WL[:, s, 0:n], RAW[:, r, 0:n], WH[:, s, 0:n].bitcast(F32),
                                                        ALU.subtract), after)

        def fetch_to(c):
            while st["fetched"] < min(NCH, c):
                fetch(st["fetched"])
                st["fetched"] += 1

        def hi_to(c):
            while st["hi"] < min(NCH, c):
                fetch_to(st["hi"] + 1)
                split_hi(st["hi"])
                st["hi"] += 1

        def lo_to(c):
            while st["lo"] < min(NCH, c):
                split_lo(st["lo"])
                st["lo"] += 1
                fetch_to(st["lo"] + NRAW)

        def split_piece(c, q):
            r, s, n = c % NRAW, c % NSPL, width(c) // 4
            cs = slice(q * n, q * n + n)
            after = [(raw_sem[r], 16 * (c // NRAW + 1)), t_used[c - NSPL]]
            if st["hi"] == c:
                th = act.put(lambda e: e.activation(WH[:, s, cs], RAW[:, r, cs], ACT.Copy), after)
            else:
                th = t_hi[c]
            tl = dve.put(lambda e: e.tensor_tensor(WL[:, s, cs], RAW[:, r, cs], WH[:, s, cs].bitcast(F32),
                                                   ALU.subtract), [th] + after)
            if q == 3:
                t_hi[c], t_lo[c] = th, tl
                st["hi"] = max(st["hi"], c + 1)
                st["lo"] = c + 1
                fetch_to(c + 1 + NRAW)

        bg = []
        turn = {"wide": 1, "n": 0}

        def step(n=1, pace=True):
            for _ in range(n):
                if not bg:
                    return
                turn["n"] += 1
                i = turn["n"] % turn["wide"]
                if i >= len(bg) and pace:
                    continue
                work = bg[min(i, len(bg) - 1)]
                if next(work, "end") == "end":
                    bg.remove(work)

        def drain(gen=None):
            while bg and (gen is None or gen in bg):
                step(pace=False)

        def run(m, jobs, steps=1, then=None, cut=False):
            c0 = st["used"]
            n = len(jobs)
            at = [n * i // steps for i in range(steps)] if steps else []
            step(at.count(0))
            if then:
                then()
            if not cut:
                for n in range(st["lo"], c0 + NSPL):
                    hi_to(n + 1)
                    lo_to(n + 1)
            assert st["lo"] >= c0 + m
            ends = {job[0]: j for j, job in enumerate(jobs)}
            tick = None
            for j, (ci, ps, b, xh, xl, first, last, after, mark) in enumerate(jobs):
                if j:
                    step(at.count(j))
                c = c0 + ci
                s = c % NSPL
                wh, wl = WH[:, s, b * 128:b * 128 + 128], WL[:, s, b * 128:b * 128 + 128]
                w = list(after() if callable(after) else after) + [t_lo[c]]
                fin = mark is not None or ends[ci] == j
                pe.put(lambda e: e.matmul(ps, wh, xh, start=first, stop=False, skip_group_check=True), w, inc=False)
                pe.put(lambda e: e.matmul(ps, wh, xl, start=False, stop=False, skip_group_check=True), inc=False)
                tick = pe.put(lambda e: e.matmul(ps, wl, xh, start=False, stop=last, skip_group_check=True), inc=fin)
                if mark is not None:
                    mark(tick)
                if cut and j % 4 == 1:
                    split_piece(c0 + 2, j // 4)
                if ends[ci] == j:
                    assert c == st["used"]
                    t_used[c] = tick
                    st["used"] = c + 1
                    if not cut:
                        hi_to(c + NSPL + 1)
            return tick

        def chunk(jobs, steps=1, then=None, cut=False):
            return run(1, [(0,) + tuple(job) for job in jobs], steps, then, cut)

        def together(m, src, ticks, late, steps=2):
            hi, lo = src
            held = [mbank.take() for _ in range(m)]
            done = {}

            def job(i, k):
                return (i, held[i][0][:, 0:T], k, hi[:, k, :], lo[:, k, :], k == 0, k == 15,
                        lambda: (held[i][1] if k == 0 else []) + list(ticks.get(k, [])),
                        (lambda tick: done.__setitem__(i, tick)) if k == 15 else None)

            jobs = [job(i, k) for i in range(m) for k in range(late)]
            jobs += [job(i, k) for k in range(late, 15) for i in range(m)] + [job(i, 15) for i in range(m)]
            run(m, jobs, steps)
            return [(i, held[i][0], held[i][0][:, 0:T], done[i]) for i in range(m)]

        def tile_k(src, ticks, nk=KD, steps=1):
            bank, freed = mbank.take()
            ps = bank[:, 0:T]
            hi, lo = src
            for c0 in range(0, nk, 16):
                jobs = []
                for b in range(min(16, nk)):
                    k = c0 + b
                    jobs.append((ps, b, hi[:, k, :], lo[:, k, :], k == 0, k == nk - 1,
                                 (freed if k == 0 else []) + list(ticks.get(k, [])), None))
                t = chunk(jobs, steps)
            return bank, ps, t

        def each_tile(n_tiles, src, ticks, nk=KD, late=None, steps=1):
            n0 = 0
            if late is not None:
                first = together(2 if late == 0 else 3, src, ticks, late, steps)
                drain()
                if late == 0:
                    first += [(n,) + tile_k(src, ticks, nk, 1) for n in (2, 3)]
                yield from first
                n0 = len(first)
                steps = 1
            if nk == 32:
                hi, lo = src
                held = [mbank.take() for _ in range(4)]
                for c in range(2):
                    if c:
                        drain()
                    for n in range(4):
                        bank, freed = held[n]
                        t = chunk([(bank[:, 0:T], b, hi[:, 16 * c + b, :], lo[:, 16 * c + b, :],
                                    c == 0 and b == 0, c == 1 and b == 15,
                                    (freed if c == b == 0 else []) + ticks[16 * c + b], None)
                                   for b in range(16)], 2)
                        if c:
                            yield n, bank, bank[:, 0:T], t
                n0 = 4
            for n in range(n0, n_tiles):
                yield (n,) + tile_k(src, ticks, nk, steps)

        def out_tiles(n_tiles, src, ticks, nk, evac, late=None, steps=1):
            for n, bank, ps, t in each_tile(n_tiles, src, ticks, nk, late, steps):
                evac(n, bank, ps, t)

        t_a = {}
        A = (AH, AL)

        def prep(k, src, g, after, freed=()):
            th = dve.put(lambda e: e.tensor_scalar(AH[:, k, :], src, g, None, ALU.mult), list(after) + list(freed))
            tl = dve.put(lambda e: e.scalar_tensor_tensor(AL[:, k, :], src, g, AH[:, k, :].bitcast(F32),
                                                          ALU.mult, ALU.subtract), [th] + list(after) + list(freed))
            t_a[k] = [th, tl]
            return tl

        def entering(update, gain, freed):
            for k in range(KD):
                after = update(k)
                square(XT[:, k, :], after, k, KD)
                prep(k, XT[:, k, :], gain(k), after, freed)
                yield
            norm_stat(D)

        LA = LazyTicks(t_a, lambda: step())

        def enter(update, gain, freed=()):
            t_a.clear()
            bg.append(entering(update, gain, list(freed)))
            step(2)

        sq = {"n": 0, "used": {}, "bank": None, "late": []}

        def square(src, after, n, total):
            i = sq["n"]
            sq["n"] += 1
            s = i % 2
            freed = [sq["used"][i - 2]] if i - 2 in sq["used"] else []
            t = act.put(lambda e: e.activation(SQ[:, s, :], src, ACT.Square), list(after) + freed)
            if n == 0:
                sq["bank"], sq["freed"] = abank.take()
            bank, extra = sq["bank"], (sq["freed"] if n == 0 else [])
            def go():
                sq["used"][i] = pe.put(lambda e: e.matmul(bank[:, 0:T], ONES[:, :], SQ[:, s, :], start=(n == 0),
                                                          stop=(n == total - 1)), [t, t_ones] + extra)
            sq["late"].append(go)
            if len(sq["late"]) > 1:
                sq["late"].pop(0)()
            return t

        r_read = []
        rr = {}

        def norm_stat(n):
            while sq["late"]:
                sq["late"].pop(0)()
            bank = sq["bank"]
            act.put(lambda e: e.preload_act_table_set(SETS["logexp"]), inc=False)
            done = sq["used"][sq["n"] - 1]
            t1 = act.put(lambda e: e.activation(R[:, :], bank[:, 0:T], ACT.Ln, bias=vec("eps"), scale=1.0 / n),
                         [done, t_vec] + list(r_read))
            abank.give(bank, [t1])
            t2 = act.put(lambda e: e.activation(R[:, :], R[:, :], ACT.Exp, scale=-0.5), [t1])
            r_read.clear()
            rr["t"] = t2
            return t2

        s1 = ExitStack()
        MH = sb("MH", [128, KD, T], FR, s1)
        ML = sb("ML", [128, KD, T], FR, s1)
        sB = ExitStack()
        MB = sb("MB", [128, 2, T], c=sB)
        GM = sb("GM", [128, 2, 128], c=sB)
        RC = sb("RC", [32, 2, T], c=sB)
        RP = sb("RP", [32, 32], c=sB)
        SCM = sb("SCM", [128, T], c=sB)
        UPW = sb("UPW", [32, 512], c=sB)
        GD = sb("GD", [32, T], c=sB)
        GQ = sb("GQ", [128, 2, T], c=sB)
        GK = sb("GK", [128, 2, T], c=sB)
        GV = sb("GV", [128, 4, T], c=sB)
        GR = sb("GR", [128, 4, T], c=sB)
        QKV = sb("QKV", [128, 3, 3, T], c=sB)
        t_mb = load(MB[:, :, :], d["c_bias"].rearrange("p (a t) -> p a t", a=2), q=act)
        t_gm = load(GM[:, :, :], d["c_gmask"].rearrange("p (a t) -> p a t", a=2), q=act)
        t_rc = load(RC[:, :, :], d["c_rope"].rearrange("p (a t) -> p a t", a=2), q=act)
        t_rp = load(RP[:, :], d["c_rot"][:, :], q=act)
        t_scm = load(SCM[:, :], d["c_scan"][:, :], q=act)
        t_up = load(UPW[:, :], d["gla_up"][:, :], q=act)
        act.put(lambda e: e.preload_act_table_set(SETS["logexp"]), inc=False)

        enter(lambda k: [t_xts[k // 4], t_vec], lambda k: vec("norm1_g", k))

        def evac_r(dst, bank, ps, t, p1=128, after=()):
            tt = dve.put(lambda e: e.tensor_tensor(dst, ps[0:p1], R[0:p1, :], ALU.mult), [t, rr["t"]] + list(after))
            mbank.give(bank, [tt])
            r_read[:] = [tt]
            return tt

        t_g = {}
        mine = [(n, dst, i) for n, dst, w in (("q", GQ, 2), ("k", GK, 2), ("v", GV, 4), ("r", GR, 4)) for i in range(w)]
        for n, bank, ps, t in each_tile(13, A, LA, late=0, steps=0):
            if n == 0:
                t_gd = evac_r(GD[:, :], bank, ps, t, 32)
            else:
                name, dst, i = mine[n - 1]
                t_g[name, i] = evac_r(dst[:, i, :], bank, ps, t)

        sG = ExitStack()
        BB, LS, E1, E2 = (XT[:, 4 * i:4 * i + 4, :] for i in range(4))
        KS = LS
        BL = sb("BL", [128, 4, 4], c=sG)
        DC = sb("DC", [128, 4, 4], c=sG)
        VN = sb("VN", [128, 4, 2, 128], c=sG)
        KN = sb("KN", [128, 4, 2, 128], c=sG)
        SS = sb("SS", [128, 4, 3, 128], c=sG)
        SM = TMP[:, :, :].rearrange("p s (a c) -> p s a c", a=2)
        sG_end, t_xt2 = [], []

        def gla():
            bz, fz = abank.take()
            bz2, fz2 = abank.take()
            for n in range(4):
                ps = (bz, bz2)[n // 2][:, (n % 2) * T:(n % 2) * T + T]
                t = pe.put(lambda e, n=n, ps=ps: e.matmul(ps, UPW[:, n * 128:n * 128 + 128], GD[:, :], start=True,
                                                          stop=True, skip_group_check=True),
                           [t_gd, t_up] + fz + fz2)
            yield
            for n in range(4):
                ps = (bz, bz2)[n // 2][:, (n % 2) * T:(n % 2) * T + T]
                tz = dve.put(lambda e, n=n, ps=ps: e.tensor_scalar(BB[:, n, :], ps, vec("gla_bias", n), None, ALU.add),
                             [t, t_vec])
            abank.give(bz, [tz])
            abank.give(bz2, [tz])
            t1 = act.put(lambda e: e.activation(LS[:, :, :], BB[:, :, :], ACT.Abs), [tz])
            t1 = act.put(lambda e: e.activation(E1[:, :, :], LS[:, :, :], ACT.Exp, scale=-1.0), [t1])
            t1 = act.put(lambda e: e.activation(E2[:, :, :], E1[:, :, :], ACT.Ln, bias=vec("one")), [t1])
            t2 = dve.put(lambda e: e.scalar_tensor_tensor(BB[:, :, :], BB[:, :, :], 0.0, E2[:, :, :], ALU.min,
                                                          ALU.subtract), [t1])
            t2 = dve.put(lambda e: e.tensor_scalar(LS[:, :, :], BB[:, :, :], 1.0 / 16.0, None, ALU.mult), [t2])
            yield
            for n in range(4):
                t3 = dve.put(lambda e, n=n: e.tensor_tensor_scan(BB[:, n, :], SCM[:, :], LS[:, n, :], 0.0, ALU.mult,
                                                                 ALU.add), [t2, t_scm])
            B4 = BB[:, :, :].rearrange("p n (c j) -> p n c j", c=4)
            t3 = dve.put(lambda e: e.tensor_copy(BL[:, :, :], B4[:, :, :, 63]), [t3])
            yield
            for n in (2, 3):
                t4 = dve.put(lambda e, n=n: e.tensor_tensor(LS[:, n, :], LS[:, n, :], BB[:, n, :], ALU.subtract), [t3])
            for n in (2, 3):
                for c in range(4):
                    cs = slice(64 * c, 64 * c + 64)
                    t5 = dve.put(lambda e, n=n, c=c, cs=cs: e.tensor_scalar(
                        BB[:, n, cs], LS[:, n, cs], BL[:, n, c:c + 1], None, ALU.add), [t4])
            yield
            t6 = act.put(lambda e: e.activation(E1[:, :, :], BB[:, :, :], ACT.Exp), [t5])
            t6 = act.put(lambda e: e.activation(E2[:, :, :], BB[:, :, :], ACT.Exp, scale=-1.0), [t5])
            t6d = act.put(lambda e: e.activation(DC[:, :, :], BL[:, :, :], ACT.Exp), [t3])
            yield
            t7 = dve.put(lambda e: e.tensor_tensor(
                KS[:, :, :].rearrange("p n (c j) -> p (n c) j", c=4),
                E2[:, :, :].rearrange("p n (c j) -> p (n c) j", c=4),
                DC[:, :, :].rearrange("p n c -> p (n c)").unsqueeze(2).broadcast_to([128, 16, 64]), ALU.mult),
                [t6, t6d])
            for n in range(4):
                i = n % 2
                t8 = dve.put(lambda e, n=n, i=i: e.scalar_tensor_tensor(
                    E1[:, n, :], GQ[:, i, :], 0.125, E1[:, n, :], ALU.mult, ALU.mult), [t6, t_g["q", i]])
                t9 = dve.put(lambda e, n=n, i=i: e.tensor_tensor(E2[:, n, :], GK[:, i, :], E2[:, n, :], ALU.mult),
                             [t6, t7, t_g["k", i]])
                t10 = dve.put(lambda e, n=n, i=i: e.tensor_tensor(KS[:, n, :], GK[:, i, :], KS[:, n, :], ALU.mult),
                              [t7])
                if n == 1:
                    yield
            yield
            for src, dst, tk in ((GV, VN, t_g["v", 3]), (KS, KN, t10)):
                for half in range(2):
                    b, f = abank.take()
                    for m in range(2):
                        n = 2 * half + m
                        for tb in range(2):
                            t = pe.put(lambda e, b=b, m=m, tb=tb, n=n, src=src: e.transpose(
                                b[:, (2 * m + tb) * 128:(2 * m + tb) * 128 + 128],
                                src[:, n, tb * 128:tb * 128 + 128], IDENT[:, :]), [tk, t_ident] + f)
                    tc = act.put(lambda e, b=b, half=half, dst=dst: e.activation(
                        dst[:, 2 * half:2 * half + 2, :, :], b[:, :].rearrange("p (m s c) -> p m s c", m=2, s=2),
                        ACT.Copy), [t])
                    abank.give(b, [tc])
                yield
            t_s = {}
            for step_i in range(3):
                for n in range(4):
                    c = step_i if n < 2 else 3 - step_i
                    i = n % 2
                    tb, p0 = c // 2, 64 * (c % 2)
                    b, f = abank.take()
                    for hh in range(2):
                        t = pe.put(lambda e, b=b, hh=hh, n=n, tb=tb, p0=p0, i=i: e.matmul(
                            b[64 * hh:64 * hh + 64, 0:128], KN[p0:p0 + 64, n, tb, 64 * hh:64 * hh + 64],
                            VN[p0:p0 + 64, 2 * i + hh, tb, :], start=True, stop=True, skip_group_check=True),
                            [tc] + f)
                    if step_i == 0:
                        t_s[n, 0] = dve.put(lambda e, b=b, n=n: e.tensor_copy(SS[:, n, 0, :], b[:, 0:128]), [t])
                    else:
                        t_s[n, step_i] = dve.put(lambda e, b=b, n=n, k=step_i, c=c: e.scalar_tensor_tensor(
                            SS[:, n, k, :], SS[:, n, k - 1, :], DC[:, n, c:c + 1], b[:, 0:128], ALU.mult, ALU.add),
                            [t, t_s[n, step_i - 1], t6d])
                    abank.give(b, [t_s[n, step_i]])
                yield
            sm_free = [[], []]
            for h in range(4):
                i, hp = h // 2, 64 * (h % 2)
                bo, fo = abank.take()
                first = True
                for tb in range(2):
                    b, f = abank.take()
                    for dr in range(2):
                        n = 2 * dr + i
                        t = pe.put(lambda e, b=b, dr=dr, n=n, tb=tb, hp=hp: e.matmul(
                            b[:, dr * 128:dr * 128 + 128], E2[hp:hp + 64, n, tb * 128:tb * 128 + 128],
                            E1[hp:hp + 64, n, tb * 128:tb * 128 + 128], start=True, stop=True,
                            skip_group_check=True), [t8, t9] + f)
                    tm = dve.put(lambda e, b=b, tb=tb: e.tensor_tensor(
                        SM[:, tb, :, :], b[:, 0:256].rearrange("p (a c) -> p a c", a=2), GM[:, :, :], ALU.mult),
                        [t, t_gm] + sm_free[tb])
                    abank.give(b, [tm])
                    tm = dve.put(lambda e, tb=tb: e.tensor_tensor(SM[:, tb, 0, :], SM[:, tb, 0, :], SM[:, tb, 1, :],
                                                                  ALU.add), [tm])
                    yield
                    t = pe.put(lambda e, bo=bo, h=h, tb=tb, first=first: e.matmul(
                        bo[:, tb * 128:tb * 128 + 128], VN[:, h, tb, :], SM[:, tb, 0, :], start=first, stop=False,
                        skip_group_check=True), [tm] + fo)
                    sm_free[tb] = [t]
                    first = False
                for dr in range(2):
                    n = 2 * dr + i
                    for k in range(3):
                        c = k + 1 if dr == 0 else 2 - k
                        t = pe.put(lambda e, bo=bo, n=n, k=k, c=c, hp=hp: e.matmul(
                            bo[:, 64 * c:64 * c + 64], SS[hp:hp + 64, n, k, :], E1[hp:hp + 64, n, 64 * c:64 * c + 64],
                            start=False, stop=False, skip_group_check=True), [t_s[n, k]])
                OT = GV[:, h, :]
                to = act.put(lambda e, bo=bo, OT=OT: e.activation(OT, bo[:, 0:T], ACT.Copy), [t])
                ts = act.put(lambda e, bo=bo, i=i, h=h: e.activation(BB[:, h, :], bo[:, 0:T], ACT.Square), [t])
                abank.give(bo, [to, ts])
                yield
                b, f = abank.take()
                t = pe.put(lambda e, b=b, h=h: e.matmul(b[:, 0:T], ONES[:, :], BB[:, h, :], start=True, stop=True),
                           [ts] + f)
                t1 = act.put(lambda e, b=b, h=h: e.activation(BB[:, h, :], b[:, 0:T], ACT.Ln, bias=vec("eps"),
                                                              scale=1.0 / 128), [t])
                abank.give(b, [t1])
                t1 = act.put(lambda e, h=h: e.activation(BB[:, h, :], BB[:, h, :], ACT.Exp, scale=-0.5), [t1])
                t2 = act.put(lambda e, h=h: e.activation(KS[:, h, :], GR[:, h, :], ACT.Exp, scale=-1.0),
                             [t_g["r", h], tc])
                t3 = dve.put(lambda e, h=h: e.tensor_scalar(KS[:, h, :], KS[:, h, :], 1.0, None, ALU.add), [t2])
                t3 = dve.put(lambda e, h=h: e.reciprocal(KS[:, h, :], KS[:, h, :]), [t3])
                t3 = dve.put(lambda e, h=h: e.tensor_tensor(GR[:, h, :], GR[:, h, :], KS[:, h, :], ALU.mult), [t3])
                yield
                t4 = dve.put(lambda e, h=h, OT=OT: e.scalar_tensor_tensor(
                    OT, OT, vec("gla_out_g", h), BB[:, h, :], ALU.mult, ALU.mult), [to, t1])
                t4 = dve.put(lambda e, h=h, OT=OT: e.tensor_tensor(OT, OT, GR[:, h, :], ALU.mult), [t4, t3])
                th = dve.put(lambda e, h=h, OT=OT: e.tensor_copy(MH[:, h, :], OT), [t4])
                tl = dve.put(lambda e, h=h, OT=OT: e.tensor_tensor(ML[:, h, :], OT, MH[:, h, :].bitcast(F32),
                                                                   ALU.subtract), [th])
                t_m[h] = [th, tl]
                yield
            sG_end[:] = [(pe.sem, pe.count), (act.sem, act.count), (dve.sem, dve.count)]
            t_xt2[:] = [load(XT[:, :, :], d["xt"].rearrange("p (k t) -> p k t", k=KD), sG_end, q=act)]

        t_m = {}
        gen_gla = gla()
        bg.append(gen_gla)
        turn["wide"] = 2
        sA = ExitStack()
        A1 = sb("A1", [128, 2, 2, T], c=sA)
        A2 = sb("A2", [128, 2, 2, T], c=sA)
        A3 = sb("A3", [128, 2, 2, T], c=sA)
        A4 = sb("A4", [128, 2, 2, 128], c=sA)
        A5 = sb("A5", [128, 2, 3, 2], c=sA)
        a_done = [[], []]

        def attn(h, tq):
            s = h % 3
            qk = QKV[:, s, 0:2, :]
            qkf = qk.rearrange("p a t -> p (a t)")
            w = h % 2
            ASQ = ASM = A1[:, w]
            ALG = ASQ.rearrange("p a t -> p (a t)")
            ARR = APT = A2[:, w]
            AP_ = A3[:, w]
            AT1 = A3[0:32, w]
            AVN = A4[:, w]
            ANM, ADN, ARD = A5[:, w, 0], A5[:, w, 1], A5[:, w, 2]
            pre = list(a_done[w])
            t = act.put(lambda e: e.activation(ASQ, qk, ACT.Square), [tq[0], tq[1]] + pre)
            yield
            bv, fv = abank.take()
            for kt in range(2):
                tv = pe.put(lambda e: e.transpose(bv[:, kt * 128:kt * 128 + 128],
                                                  QKV[:, s, 2, kt * 128:kt * 128 + 128], IDENT[:, :]), [tq[2]] + fv)
            b, f = abank.take()
            t = pe.put(lambda e: e.matmul(b[:, :], ONES[:, :], ASQ.rearrange("p a t -> p (a t)"),
                                          start=True, stop=True), [t] + f)
            yield
            t = act.put(lambda e: e.activation(ALG, b[:, :], ACT.Ln, bias=vec("eps"), scale=1.0 / 128), [t] + pre)
            abank.give(b, [t])
            t = act.put(lambda e: e.activation(ARR.rearrange("p a t -> p (a t)"), ALG, ACT.Exp,
                                               scale=-0.5), [t])
            tvn = act.put(lambda e: e.activation(AVN, bv[:, 0:256].rearrange("p (a c) -> p a c", a=2),
                                                 ACT.Copy), [tv] + pre)
            abank.give(bv, [tvn])
            yield
            for a, g in ((0, "q_norm_g"), (1, "k_norm_g")):
                tn = dve.put(lambda e: e.scalar_tensor_tensor(
                    QKV[:, s, a, :], QKV[:, s, a, :], vec(g), ARR[:, a, :], ALU.mult, ALU.mult), [t])
            yield
            yield
            b, f = abank.take()
            t = pe.put(lambda e: e.matmul(b[0:32, :], RP[:, :], qkf[0:32], start=True, stop=True), [tn, t_rp] + f)
            yield
            t1 = dve.put(lambda e: e.tensor_tensor(
                AT1, b[0:32, :].rearrange("p (a t) -> p a t", a=2),
                RC[:, 1, :].unsqueeze(1).broadcast_to([32, 2, T]), ALU.mult), [t, t_rc] + pre)
            abank.give(b, [t1])
            t2 = dve.put(lambda e: e.tensor_tensor(
                qk[0:32], qk[0:32], RC[:, 0, :].unsqueeze(1).broadcast_to([32, 2, T]), ALU.mult), [t])
            t2 = dve.put(lambda e: e.tensor_tensor(qk[0:32], qk[0:32], AT1, ALU.add), [t1, t2])
            yield
            yield
            b, f = abank.take()
            for qt in range(2):
                t = pe.put(lambda e: e.matmul(b[:, qt * T:qt * T + T], QKV[:, s, 0, qt * 128:qt * 128 + 128],
                                              QKV[:, s, 1, :], start=True, stop=True, skip_group_check=True),
                           [t2] + f)
            t_qk = t
            yield
            t = dve.put(lambda e: e.scalar_tensor_tensor(
                ASM.rearrange("p a t -> p (a t)"), b[:, :], float(128 ** -0.5),
                MB[:, :, :].rearrange("p a t -> p (a t)"), ALU.mult, ALU.add), [t_qk, t_mb] + pre)
            abank.give(b, [t])
            t = dve.put(lambda e: e.tensor_reduce(ANM, ASM, AX.X, ALU.max, negate=True), [t] + pre)
            for qt in range(2):
                t2 = act.put(lambda e: e.activation(AP_[:, qt, :], ASM[:, qt, :], ACT.Exp,
                                                    bias=ANM[:, qt:qt + 1], accum_out=ADN[:, qt:qt + 1]),
                             [t] + pre)
            yield
            yield
            t2 = dve.put(lambda e: e.reciprocal(ARD, ADN), [t2])
            for qt in range(2):
                t3 = dve.put(lambda e: e.tensor_scalar(AP_[:, qt, :], AP_[:, qt, :], ARD[:, qt:qt + 1], None,
                                                       ALU.mult), [t2])
            yield
            b, f = abank.take()
            for kt in range(2):
                for qt in range(2):
                    t = pe.put(lambda e: e.transpose(
                        b[:, kt * T + qt * 128:kt * T + qt * 128 + 128], AP_[:, qt, kt * 128:kt * 128 + 128],
                        IDENT[:, :]), [t3] + f)
            yield
            t = act.put(lambda e: e.activation(APT.rearrange("p a t -> p (a t)"), b[:, :], ACT.Copy),
                        [t] + pre)
            abank.give(b, [t])
            yield
            yield
            b, f = abank.take()
            for kt in range(2):
                to = pe.put(lambda e: e.matmul(b[:, 0:T], AVN[:, kt, :], APT[:, kt, :], start=(kt == 0),
                                               stop=(kt == 1)), [t, tvn] + f)
            a_done[w] = [to]
            yield
            th = dve.put(lambda e: e.tensor_copy(MH[:, 4 + h, :], b[:, 0:T]), [to])
            tl = dve.put(lambda e: e.tensor_tensor(ML[:, 4 + h, :], b[:, 0:T], MH[:, 4 + h, :].bitcast(F32),
                                                   ALU.subtract), [th])
            abank.give(b, [tl])
            t_m[4 + h] = [th, tl]
            qkv_free[s] = [t_qk, tv]
            yield

        qkv_free = [[], [], []]
        gens = []
        for h in range(12):
            if h >= 3:
                drain(gens[h - 3])
            tq = []
            for j in range(3):
                bank, ps, t = tile_k(A, t_a, steps=7)
                tq.append(evac_r(QKV[:, h % 3, j, :], bank, ps, t, after=qkv_free[h % 3]))
            gens.append(attn(h, tq))
            bg.append(gens[h])
        drain(gens[9])
        sA.close()
        sG.close()
        sB.close()

        a_free = [t_used[st["used"] - 1]]

        def resid(n, bank, ps, t):
            tx = dve.put(lambda e: e.tensor_tensor(XT[:, n, :], XT[:, n, :], ps, ALU.add), [t] + t_xt2)
            mbank.give(bank, [tx])
            square(XT[:, n, :], [tx], n, KD)
            prep(n, XT[:, n, :], vec("norm2_g", n), [tx], a_free)

        out_tiles(16, (MH, ML), LazyTicks(t_m, drain), 16, resid, 12, 26)
        norm_stat(D)
        turn["wide"] = 1
        end_m = end_b1 = [(pe.sem, pe.count), (act.sem, act.count), (dve.sem, dve.count)]
        s1.close()

        sP = ExitStack()
        NX = max(PARTS[0][1], PARTS[2][1])
        NY = PARTS[1][1]
        GA = sb("GA", [128, NX + NY, T], c=sP)
        I1T = sb("I1T", [128, T], c=sP)
        I2T = sb("I2T", [128, T], c=sP)
        GTT = sb("GTT", [128, T], c=sP)
        IOTA = sb("IOTA", [128, 128], c=sP)
        t_iota = load(IOTA[:, :], d["c_iota"][:, :], end_b1 + end_m, q=act)
        sQ = ExitStack()
        QY = GA[:, 40:56, :]
        SK = GA[:, 32:40, :].rearrange("p n t -> p (n t)").rearrange("p (c k) -> p c k", c=16)
        SC = GA[:, 56:72, :].rearrange("p n t -> p (n t)").rearrange("p (a c k) -> p a c k", a=2, c=16)
        TV = sb("TV", [128, 2, 16, 16], c=sQ)
        TI = sb("TI", [128, 16, 16], U32, c=sQ)
        TF = sb("TF", [128, 2, 16, 16], c=sQ)
        BV = sb("BV", [128, 2, 8, 16], c=sQ)
        BPI = sb("BPI", [128, 128], U32, c=sQ)
        BPX = sb("BPX", [128, 2, 128], U32, c=sQ)
        BPF = sb("BPF", [128, 2, 128], c=sQ)
        CD = sb("CD", [128, 16, 16], c=sQ)
        IX = sb("IX", [128, 3, 128], c=sQ)
        ES = sb("ES", [128, 16], c=sQ)
        t_sk = load(SK[:, :, :], d["sub_keys"].rearrange("p (c k) -> p c k", c=16), end_b1 + end_m, q=act)
        t_q = {}

        def evac_q(n, bank, ps, t):
            t_q[n] = evac_r(QY[:, n, :], bank, ps, t, after=end_b1 + end_m)

        out_tiles(16, A, t_a, 16, evac_q)
        qy_done = []
        sc_done = []

        def topk():
            t_sc = {}
            for q in range(4):
                for a in range(2):
                    b, f = abank.take()
                    for c in range(4):
                        hc = 4 * q + c
                        t = pe.put(lambda e, b=b, c=c, hc=hc, a=a: e.matmul(
                            b[:, c * 128:c * 128 + 128], QY[:, hc, a * 128:a * 128 + 128], SK[:, hc, :], start=True,
                            stop=True, skip_group_check=True), [t_q[hc], t_sk] + f)
                    qy_done[:] = [t]
                    tc = act.put(lambda e, b=b, q=q, a=a: e.activation(
                        SC[:, a, 4 * q:4 * q + 4, :], b[:, :].rearrange("p (c k) -> p c k", c=4), ACT.Copy), [t])
                    abank.give(b, [tc])
                    for c in range(4):
                        t_sc[a, 4 * q + c] = tc
                yield
            st["qy"] = True
            t_ix = []
            for a in range(2):
                EQ = SC[:, a].rearrange("p c k -> p (c k)").rearrange("p (c k) -> p c k", k=16)
                for hc in range(16):
                    v = SC[:, a, hc, :]
                    m1, m2 = TV[:, a, hc, 0:8], TV[:, a, hc, 8:16]
                    i1, i2 = TI[:, hc, 0:8], TI[:, hc, 8:16]
                    t = dve.put(lambda e, v=v, m1=m1: e.max(m1, v), [t_sc[a, hc]])
                    t = dve.put(lambda e, v=v, m1=m1, i1=i1: e.max_index(i1, m1, v), [t] + t_ix)
                    t = dve.put(lambda e, v=v, m1=m1: e.match_replace(v, m1, v, NEG), [t])
                    t = dve.put(lambda e, v=v, m2=m2: e.max(m2, v), [t])
                    t = dve.put(lambda e, v=v, m2=m2, i2=i2: e.max_index(i2, m2, v), [t])
                    yield
                t = dve.put(lambda e, a=a: e.tensor_copy(TF[:, a, :, :], TI[:, :, :]), [t])
                t_tf = t
                for h in range(8):
                    t = dve.put(lambda e, a=a, h=h: e.tensor_tensor(
                        CD[:, :, :], TV[:, a, 2 * h, :].unsqueeze(2).broadcast_to([128, 16, 16]),
                        TV[:, a, 2 * h + 1, :].unsqueeze(1).broadcast_to([128, 16, 16]), ALU.add), [t])
                    v = CD[:, :, :].rearrange("p a b -> p (a b)")
                    m1, m2 = BV[:, a, h, 0:8], BV[:, a, h, 8:16]
                    i1, i2 = BPI[:, 16 * h:16 * h + 8], BPI[:, 16 * h + 8:16 * h + 16]
                    t = dve.put(lambda e, v=v, m1=m1: e.max(m1, v), [t])
                    t = dve.put(lambda e, v=v, m1=m1, i1=i1: e.max_index(i1, m1, v), [t])
                    t = dve.put(lambda e, v=v, m1=m1: e.match_replace(v, m1, v, NEG), [t])
                    t = dve.put(lambda e, v=v, m2=m2: e.max(m2, v), [t])
                    t = dve.put(lambda e, v=v, m2=m2, i2=i2: e.max_index(i2, m2, v), [t])
                    yield
                t = dve.put(lambda e: e.tensor_single_scalar(BPX[:, 0, :], BPI[:, :], 4, ALU.logical_shift_right), [t])
                t = dve.put(lambda e: e.tensor_single_scalar(BPX[:, 1, :], BPI[:, :], 15, ALU.bitwise_and), [t])
                t = dve.put(lambda e: e.tensor_copy(BPF[:, :, :], BPX[:, :, :]), [t])
                for c in range(2):
                    t = dve.put(lambda e, c=c: e.tensor_tensor(
                        EQ[:, :, :], BPF[:, c, :].unsqueeze(2).broadcast_to([128, 128, 16]),
                        IOTA[:, 0:16].unsqueeze(1).broadcast_to([128, 128, 16]), ALU.is_equal), [t, t_iota] + qy_done)
                    yield
                    for h in range(8):
                        t2 = dve.put(lambda e, c=c, a=a, h=h: e.tensor_tensor(
                            EQ[:, 16 * h:16 * h + 16, :], EQ[:, 16 * h:16 * h + 16, :],
                            TF[:, a, 2 * h + c, :].unsqueeze(1).broadcast_to([128, 16, 16]), ALU.mult), [t, t_tf])
                    t = t2
                    yield
                    t = dve.put(lambda e, c=c: e.tensor_reduce(IX[:, c, :], EQ[:, :, :], AX.X, ALU.add), [t] + t_ix)
                    yield
                bv = BV[:, a, :, :]
                G3 = IX[:, 2, :].rearrange("p (h k) -> p h k", h=8)
                t = dve.put(lambda e, bv=bv, G3=G3, a=a: e.tensor_tensor(
                    G3, bv, BV[:, a, :, 0:1].broadcast_to([128, 8, 16]), ALU.subtract), [t] + t_ix)
                t = act.put(lambda e: e.activation(IX[:, 2, :], IX[:, 2, :], ACT.Exp), [t])
                t = dve.put(lambda e, G3=G3: e.tensor_reduce(ES[:, 0:8], G3, AX.X, ALU.add), [t])
                t = dve.put(lambda e: e.reciprocal(ES[:, 8:16], ES[:, 0:8]), [t])
                t = dve.put(lambda e, G3=G3: e.tensor_tensor(
                    G3, G3, ES[:, 8:16].unsqueeze(2).broadcast_to([128, 8, 16]), ALU.mult), [t])
                yield
                b, f = abank.take()
                for c in range(3):
                    tp = pe.put(lambda e, b=b, c=c: e.transpose(b[:, c * 128:c * 128 + 128], IX[:, c, :], IDENT[:, :]),
                                [t] + f)
                t_ix = [tp]
                for c, dst in enumerate((I1T, I2T, GTT)):
                    t_idx[a, c] = act.put(lambda e, b=b, c=c, dst=dst, a=a: e.activation(
                        dst[:, a * 128:a * 128 + 128], b[:, c * 128:c * 128 + 128], ACT.Copy), [tp])
                abank.give(b, [t_idx[a, 2]])
                yield

        t_idx = {}
        gen_topk = topk()
        bg.append(gen_topk)
        tmp_free = [[], []]
        place = [0, NX, 0]
        ga_free = {}
        t_act = [{} for _ in PARTS]
        t_g = {}
        NB = 8
        NC = 4

        def phase_a(p, steps, pre=()):
            for jj in range(PARTS[p][1]):
                slot = place[p] + jj
                bank, ps, t = tile_k(A, t_a, steps=steps(jj))
                s = jj % 2
                tt = dve.put(lambda e: e.tensor_tensor(TMP[:, s, :], ps, R[:, :], ALU.mult),
                             [t, rr["t"]] + tmp_free[s])
                mbank.give(bank, [tt])
                r_read[:] = [tt]
                extra = ga_free.get(slot, []) + list(pre)
                if p == 0 and slot >= 32:
                    assert st["qy"]
                    extra += qy_done
                ta = act.put(lambda e: e.activation(GA[:, slot, :], TMP[:, s, :], ACT.Gelu_apprx_tanh),
                             [tt] + extra)
                tmp_free[s] = [ta]
                t_act[p][jj] = ta

        def gates(p):
            p0, n = PARTS[p]
            nq = T // NB
            t_hot = {}

            def hot(q):
                s = q % 2
                a = q * NB // 128
                after = [t_idx[a, 0], t_idx[a, 1], t_idx[a, 2], t_iota] + ob_free[s]
                for k in range(NB):
                    tok = q * NB + k
                    dve.put(lambda e: e.tensor_scalar(
                        OA[:, s, k, :], IOTA[:, :], I1T[:, tok:tok + 1], GTT[:, tok:tok + 1], ALU.is_equal,
                        ALU.mult), after, inc=False)
                t_hot[q] = dve.put(lambda e: e.tensor_tensor(
                    OB[:, s, :, 0:n], IOTA[:, p0:p0 + n].unsqueeze(1).broadcast_to([128, NB, n]),
                    I2T[:, q * NB:q * NB + NB].unsqueeze(2).broadcast_to([128, NB, n]), ALU.is_equal), after)

            def times(q, b, t):
                G = GA[:, place[p]:place[p] + n, q * NB:q * NB + NB].rearrange("p j t -> p t j")
                t_g[p] = dve.put(lambda e: e.tensor_tensor(
                    G, G, b[:, 0:NB * n].rearrange("p (t j) -> p t j", j=n), ALU.mult), [t, t_act[p][n - 1]])
                abank.give(b, [t_g[p]])

            hot(0)
            yield
            held = None
            for q in range(nq):
                if held:
                    times(q - 1, *held)
                s = q % 2
                b, f = abank.take()
                for k in range(NB):
                    t = pe.put(lambda e: e.matmul(b[:, k * n:k * n + n], OA[:, s, k, :], OB[:, s, k, 0:n], start=True,
                                                  stop=True, skip_group_check=True), [t_hot[q]] + f, inc=k == NB - 1)
                ob_free[s] = [t]
                held = (b, t)
                if q + 1 < nq:
                    hot(q + 1)
                yield
            times(nq - 1, *held)

        def coef(p, jj, s):
            slot = place[p] + jj
            th = act.put(lambda e: e.activation(CH[:, s, :], GA[:, slot, :], ACT.Copy), [t_g[p]] + c_free[s])
            tl = dve.put(lambda e: e.tensor_tensor(CL[:, s, :], GA[:, slot, :], CH[:, s, :].bitcast(F32),
                                                   ALU.subtract), [th] + c_free[s])
            ga_free[slot] = [tl]
            return [tl]

        t_x = {}

        def phase_b(p, steps):
            n = PARTS[p][1]
            taken = [mbank.take() for _ in range(4)] + [abank.take() for _ in range(3)]
            freed = [x for _, f in taken for x in f]
            tc = {}

            def blocks_to(m):
                for i in range(len(tc), min(m, 2 * n)):
                    tc[i] = coef(p, i % n, i % NC)

            def used(i, tick):
                c_free[i % NC] = [tick]
                if i >= n:
                    blocks_to(i + NC + 1)

            blocks_to(3)
            for jj in range(n):
                s = jj % NC
                jobs = [(taken[dt // 2][0][:, (dt % 2) * T:(dt % 2) * T + T], dt, CH[:, s, :], CL[:, s, :],
                         jj == 0 and dt % 2 == 0, jj == n - 1, tc[jj] + (freed if jj == 0 else []), None)
                        for dt in range(14)]
                t = chunk(jobs, steps, lambda: blocks_to(jj + 3))
                used(jj, t)
            for dt in range(14):
                bank = taken[dt // 2][0]
                t_x[dt] = dve.put(lambda e: e.tensor_tensor(
                    XT[:, dt, :], XT[:, dt, :], bank[:, (dt % 2) * T:(dt % 2) * T + T], ALU.add), [t])
                if dt % 2:
                    (mbank if dt < 8 else abank).give(bank, [t_x[dt]])
            if p == len(PARTS) - 1:
                del t_x[14], t_x[15]
                enter(lambda k: [t_x[k]], lambda k: vec("g_pre_2", k), [t_used[st["used"] - 1]])
            bank, freed = mbank.take()
            blocks_to(n + NC)
            for j0 in range(0, n, TAIL):
                jobs = []
                for j in range(TAIL):
                    i = n + j0 + j
                    s = i % NC
                    for dt in range(2):
                        jobs.append((bank[:, dt * T:dt * T + T], 2 * j + dt, CH[:, s, :], CL[:, s, :],
                                     i == n and dt == 0, i == 2 * n - 1, lambda i=i: tc[i] + freed,
                                     (lambda tick, i=i: used(i, tick)) if dt else None))
                t = chunk(jobs, 2 if j0 + TAIL < n else 0, cut=True)
            for dt in (14, 15):
                t_x[dt] = dve.put(lambda e: e.tensor_tensor(
                    XT[:, dt, :], XT[:, dt, :], bank[:, (dt - 14) * T:(dt - 13) * T], ALU.add), [t])
            mbank.give(bank, [t_x[15]])

        phase_a(0, lambda jj: 2 if jj % 4 == 0 else 1, end_b1 + end_m)
        drain(gen_topk)
        end_q = [(pe.sem, pe.count), (act.sem, act.count), (dve.sem, dve.count)]
        sQ.close()
        sO = ExitStack()
        OA = sb("OA", [128, 2, NB, 128], c=sO)
        OB = sb("OB", [128, 2, NB, NX], c=sO)
        CH = sb("CH", [128, NC, T], FR, c=sO)
        CL = sb("CL", [128, NC, T], FR, c=sO)
        ob_free = [list(end_q), list(end_q)]
        c_free = [list(end_q) for _ in range(NC)]
        bg.append(gates(0))
        phase_a(1, lambda jj: 2, end_q)
        drain()
        bg.append(gates(1))
        phase_b(0, 1)
        drain()
        phase_a(2, lambda jj: 0)
        bg.append(gates(2))
        phase_b(1, 2)
        drain()
        phase_b(2, 1)
        end_p = [(pe.sem, pe.count), (act.sem, act.count), (dve.sem, dve.count), (pool.sem, pool.count)]
        sO.close()
        sP.close()

        s2 = ExitStack()
        PH = sb("PH", [128, 2, T], FR, c=s2)
        PL = sb("PL", [128, 2, T], FR, c=s2)
        SP8 = sb("SP8", [128, 3, 32], c=s2)
        act.put(lambda e: e.preload_act_table_set(SETS["logexp"]), inc=False)
        Lv = VEC[:, VOFF["lru_L_2"]:VOFF["lru_L_2"] + 32]
        E_, Y_, M_ = SP8[:, 0, :], SP8[:, 1, :], SP8[:, 2, :]
        t = act.put(lambda e: e.activation(Y_, Lv, ACT.Abs), end_p)
        t = act.put(lambda e: e.activation(E_, Y_, ACT.Exp, scale=-1.0), [t])
        t = dve.put(lambda e: e.tensor_scalar(Y_, E_, 1.0, None, ALU.add), [t])
        t1 = act.put(lambda e: e.activation(M_, Y_, ACT.Ln), [t] + end_p)
        t2 = dve.put(lambda e: e.scalar_tensor_tensor(E_, Y_, -1.0, E_, ALU.add, ALU.subtract), [t1])
        t2 = dve.put(lambda e: e.reciprocal(Y_, Y_), [t2])
        t2 = dve.put(lambda e: e.tensor_tensor(E_, E_, Y_, ALU.mult), [t2])
        t2 = dve.put(lambda e: e.tensor_tensor(M_, M_, E_, ALU.subtract), [t2])
        t2 = dve.put(lambda e: e.tensor_scalar(Y_, Lv, -1.0, 0.0, ALU.mult, ALU.max), [t2])
        t2 = dve.put(lambda e: e.tensor_tensor(Y_, Y_, M_, ALU.add), [t2])
        t2 = dve.put(lambda e: e.tensor_scalar(M_, Y_, -8.0, None, ALU.mult), [t2])
        t_sp = dve.put(lambda e: e.tensor_scalar(Y_, Y_, 8.0, None, ALU.mult), [t2])

        def marks_now():
            return [(pe.sem, pe.count), (act.sem, act.count), (dve.sem, dve.count)]

        PT = sb("PT", [128, 2, T], c=s2)
        prev, p_free = list(end_p), list(end_p)
        for l in range(2):
            t_pt = load(PT[:, :, :], d["p_2"].rearrange("p (l k t) -> p l k t", l=2, k=2)[:, l], p_free)
            sY = ExitStack()
            YH = sb(f"YH{l}", [128, 32, T], FR, c=sY)
            YL = sb(f"YL{l}", [128, 32, T], FR, c=sY)
            sU = ExitStack()
            t_y = {}
            if l == 0:
                DH = sb("DH", [128, 8, T], FR, c=sU)
                DL = sb("DL", [128, 8, T], FR, c=sU)
                ZS = sb("ZS", [128, 4, T], c=sU)
                INV = sb("INV", [128, 4, 16], c=sU)
                t_inv = load(INV[:, :, :], d["c_inv"].rearrange("p (g t) -> p g t", g=4), prev)
                UP = sb("UP", [128, 3, 16 + T], c=sU)
                t = dve.put(lambda e: e.memset(UP[:, :, 0:16], 0.0), prev)
                t_up0 = t
                d_free = []
                for g in range(4):
                    w = 2 << g
                    t_d = {}
                    for i, bank, ps, t in each_tile(8, A, LA, late=0 if g == 0 else None, steps=0 if g == 0 else 1):
                        U = UP[:, 0, 16:16 + T]
                        t = dve.put(lambda e, ps=ps, U=U: e.tensor_tensor(U, ps, R[:, :], ALU.mult), [t, rr["t"], t_up0])
                        mbank.give(bank, [t])
                        src = 0
                        for k in range(g + 1):
                            dst = 1 + k % 2
                            sh = 1 << k
                            t = dve.put(lambda e, src=src, dst=dst, sh=sh: e.tensor_tensor(
                                UP[:, dst, 16:16 + T], UP[:, src, 16:16 + T], UP[:, src, 16 - sh:16 + T - sh],
                                ALU.add), [t])
                            src = dst
                        s = i % 2
                        t2 = dve.put(lambda e, src=src, s=s, w=w: e.scalar_tensor_tensor(
                            TMP[:, s, :], UP[:, src, 16:16 + T], 1.0 / w, UP[:, 0, 16:16 + T], ALU.mult,
                            ALU.subtract), [t] + tmp_free[s])
                        t = dve.put(lambda e, src=src, g=g: e.tensor_tensor(
                            UP[:, src, 16:32], UP[:, src, 16:32], INV[:, g, :], ALU.mult), [t2, t_inv])
                        t = dve.put(lambda e, src=src, s=s: e.tensor_tensor(
                            TMP[:, s, 0:16], UP[:, src, 16:32], UP[:, 0, 16:32], ALU.subtract), [t])
                        th = dve.put(lambda e: e.tensor_copy(DH[:, i, :], TMP[:, s, :]), [t] + d_free + prev)
                        tl = dve.put(lambda e, s=s, i=i: e.tensor_tensor(DL[:, i, :], TMP[:, s, :],
                                                                        DH[:, i, :].bitcast(F32), ALU.subtract),
                                     [th])
                        tmp_free[s] = [th]
                        t_d[i] = [th, tl]
                    t_z = {}
                    for half in range(2):
                      for i in range(4 * half, 4 * half + 4):
                          bank, ps, t = tile_k(A, t_a)
                          t = dve.put(lambda e, ps=ps, i=i: e.tensor_tensor(ZS[:, i % 4, :], ps, R[:, :], ALU.mult),
                                      [t, rr["t"]])
                          mbank.give(bank, [t])
                          r_read[:] = [t]
                          t_z[i] = act.put(lambda e, i=i: e.activation(ZS[:, i % 4, :], ZS[:, i % 4, :], ACT.Silu), [t])
                      for c in range(2 * half, 2 * half + 2):
                          jobs = []
                          held = []
                          for o in range(2):
                              bank, freed = mbank.take()
                              mark = []
                              held.append((bank, mark))
                              for k in range(8):
                                  jobs.append((bank[:, 0:T], o * 8 + k, DH[:, k, :], DL[:, k, :], k == 0, k == 7,
                                               freed + t_d[k], mark.append if k == 7 else None))
                          d_free = [chunk(jobs)]
                          for o in range(2):
                              i = 2 * c + o
                              n = 8 * g + i
                              bank, mark = held[o]
                              ps = bank[:, 0:T]
                              s = i % 2
                              t = dve.put(lambda e, ps=ps, s=s, n=n: e.tensor_scalar(
                                  TMP[:, s, :], ps, vec("pool_b_2", n), vec("pool_scale_2", n), ALU.add, ALU.mult),
                                  [mark[-1]] + tmp_free[s])
                              mbank.give(bank, [t])
                              t = dve.put(lambda e, s=s, i=i: e.tensor_tensor(TMP[:, s, :], TMP[:, s, :], ZS[:, i % 4, :],
                                                                             ALU.mult), [t, t_z[i]])
                              th = dve.put(lambda e: e.tensor_copy(YH[:, n, :], TMP[:, s, :]), [t] + prev)
                              tl = dve.put(lambda e, s=s, n=n, YH=YH, YL=YL: e.tensor_tensor(
                                  YL[:, n, :], TMP[:, s, :], YH[:, n, :].bitcast(F32), ALU.subtract), [th])
                              tmp_free[s] = [th]
                              t_y[n] = [th, tl]
            else:
                UP = sb("UQ", [128, 4 + T], c=sU)
                UCS = sb("UCS", [128, 2, 4, T], c=sU)
                ZBS = sb("ZB", [128, 2, 4, T], c=sU)
                RG = sb("RG", [128, 4, T], c=sU)
                IG = sb("IG", [128, 4, T], c=sU)
                t_u0 = dve.put(lambda e: e.memset(UP[:, 0:4], 0.0), prev)
                conv_prev = [t_u0]
                rg_read, ig_read, uc_read, z_read = [], [], [[], []], [[], []]

                def recur(g, tg, held, t_z):
                    UC, ZB = UCS[:, g % 2], ZBS[:, g % 2]
                    for ax, dst, bn, rd in ((0, RG, "lru_ba_2", rg_read), (1, IG, "lru_bx_2", ig_read)):
                        for hh in range(2):
                            bank = held[2 * hh + ax]
                            for o in range(2):
                                i = 2 * hh + o
                                ts = act.put(lambda e: e.activation(
                                    dst[:, i, :], bank[:, o * T:o * T + T], ACT.Sigmoid, bias=vec(bn, 4 * g + i)),
                                    [tg] + rd + prev)
                            abank.give(bank, [ts])
                        yield
                    t1 = dve.put(lambda e: e.tensor_tensor(UC, UC, IG[:, :, :], ALU.mult), [ts])
                    yield
                    for i in range(4):
                        n = 4 * g + i
                        t2 = act.put(lambda e: e.activation(IG[:, i, :], RG[:, i, :], ACT.Tanh,
                                                            scale=SP8[:, 1, n:n + 1]), [ts, t_sp, t1])
                    for i in range(4):
                        n = 4 * g + i
                        t4 = act.put(lambda e: e.activation(RG[:, i, :], RG[:, i, :], ACT.Exp,
                                                            scale=SP8[:, 2, n:n + 1]), [t2])
                    yield
                    for i in range(4):
                        t5 = dve.put(lambda e: e.tensor_tensor(UP[:, 4:4 + T], RG[:, i, :], RG[:, i, :], ALU.mult),
                                     [t4] + conv_prev)
                        t5 = dve.put(lambda e: e.scalar_tensor_tensor(
                            IG[:, i, :], UP[:, 4:4 + T], 1.0, IG[:, i, :], ALU.add, ALU.mult), [t5])
                        conv_prev[:] = [t5]
                        if i == 1:
                            yield
                    yield
                    t5 = dve.put(lambda e: e.tensor_scalar(IG[:, :, :], IG[:, :, :], 0.0, None, ALU.max), [t5])
                    yield
                    t6 = act.put(lambda e: e.activation(IG[:, :, :], IG[:, :, :], ACT.Sqrt), [t5])
                    yield
                    t7 = dve.put(lambda e: e.tensor_tensor(UC, UC, IG[:, :, :], ALU.mult), [t6])
                    for i in range(4):
                        t8 = dve.put(lambda e: e.tensor_tensor_scan(IG[:, i, :], RG[:, i, :], UC[:, i, :], 0.0,
                                                                    ALU.mult, ALU.add), [t7, t4])
                    uc_read[g % 2] = rg_read[:] = [t8]
                    yield
                    t9 = dve.put(lambda e: e.tensor_tensor(ZB, ZB, IG[:, :, :], ALU.mult),
                                 [t8, t_z])
                    ig_read[:] = [t9]
                    n0 = 4 * g
                    th = dve.put(lambda e: e.tensor_copy(YH[:, n0:n0 + 4, :], ZB), [t9, tg] + prev)
                    tl = dve.put(lambda e: e.tensor_tensor(
                        YL[:, n0:n0 + 4, :], ZB, YH[:, n0:n0 + 4, :].bitcast(F32), ALU.subtract), [th])
                    z_read[g % 2] = [tl]
                    for i in range(4):
                        t_y[n0 + i] = [tl]
                    yield

                for g in range(8):
                    UH, UL = YH[:, 4 * g:4 * g + 4, :], YL[:, 4 * g:4 * g + 4, :]
                    UC, ZB = UCS[:, g % 2], ZBS[:, g % 2]
                    t_d = {}
                    for i, bank, ps, t in each_tile(4, A, LA, late=0 if g == 0 else None, steps=0 if g == 0 else 1):
                        if g == i == 0:
                            prev = prev + marks_now()
                        n = 4 * g + i
                        t = dve.put(lambda e: e.tensor_tensor(UP[:, 4:4 + T], ps, R[:, :], ALU.mult),
                                    [t, rr["t"]] + conv_prev)
                        mbank.give(bank, [t])
                        t = dve.put(lambda e: e.tensor_scalar(
                            UC[:, i, :], UP[:, 4:4 + T], vec("conv_w_2", 96 + n), vec("conv_b_2", n), ALU.mult,
                            ALU.add), [t] + uc_read[g % 2])
                        for k in (2, 1, 0):
                            t = dve.put(lambda e: e.scalar_tensor_tensor(
                                UC[:, i, :], UP[:, 1 + k:1 + k + T], vec("conv_w_2", 32 * k + n), UC[:, i, :],
                                ALU.mult, ALU.add), [t])
                        conv_prev[:] = [t]
                        th = dve.put(lambda e: e.tensor_copy(UH[:, i, :], UC[:, i, :]), [t] + prev)
                        tl = dve.put(lambda e: e.tensor_tensor(UL[:, i, :], UC[:, i, :],
                                                               UH[:, i, :].bitcast(F32), ALU.subtract), [th])
                        t_d[i] = [tl]
                    zs = []

                    def z_mult():
                        i, ts = zs.pop(0)
                        tz = dve.put(lambda e: e.tensor_tensor(ZB[:, i, :], ZB[:, i, :], TMP[:, i % 2, :], ALU.mult),
                                     [ts])
                        tmp_free[i % 2] = [tz]
                        return tz

                    for i in range(4):
                        bank, ps, t = tile_k(A, t_a, steps=2)
                        t_zz = dve.put(lambda e: e.tensor_tensor(ZB[:, i, :], ps, R[:, :], ALU.mult),
                                       [t, rr["t"]] + z_read[g % 2])
                        mbank.give(bank, [t_zz])
                        r_read[:] = [t_zz]
                        ts = act.put(lambda e: e.activation(TMP[:, i % 2, :], ZB[:, i, :], ACT.Sigmoid),
                                     [t_zz] + tmp_free[i % 2])
                        if zs:
                            z_mult()
                        zs.append((i, ts))
                    drain()
                    jobs = []
                    held = []
                    for hh in range(2):
                        for ax in range(2):
                            bank, freed = abank.take()
                            held.append(bank)
                            for o in range(2):
                                for k in range(2):
                                    jobs.append((bank[:, o * T:o * T + T], ((hh * 2 + ax) * 2 + k) * 2 + o,
                                                 UH[:, 2 * hh + k, :], UL[:, 2 * hh + k, :], k == 0 and o == 0,
                                                 k == 1, freed + t_d[2 * hh + k], None))
                    tg = chunk(jobs)
                    tz = z_mult()
                    bg.append(recur(g, tg, held, tz))
            a_free = [t_used[st["used"] - 1]]
            sU.close()
            sO2 = ExitStack()
            OO = sb(f"OO{l}", [128, 16, T], c=sO2)

            t_o = {}
            end_u = []

            def evac_o(n, bank, ps, t):
                if n == 0:
                    drain()
                    end_u[:] = marks_now()
                t_o[n] = act.put(lambda e: e.activation(OO[:, n, :], ps, ACT.Copy,
                                                        scale=vec("g_post_2", 16 * l + n)), [t] + end_u)
                ts = square(ps, [t], n, KD)
                mbank.give(bank, [t_o[n], ts])

            th = act.put(lambda e: e.activation(PH[:, :, :], PT[:, :, :], ACT.Copy), [t_pt] + p_free)
            t_p2 = dve.put(lambda e: e.tensor_tensor(PL[:, :, :], PT[:, :, :], PH[:, :, :].bitcast(F32),
                                                     ALU.subtract), [th] + p_free)
            out_tiles(16, (YH, YL), t_y, 32, evac_o)
            end_y = marks_now()
            t_ro = norm_stat(D)
            sO2.close()
            sY.close()
            sE = ExitStack()
            EE = sb(f"EE{l}", [128, 16, T], c=sE)
            def add_o(k):
                t = dve.put(lambda e: e.tensor_tensor(OO[:, k, :], OO[:, k, :], R[:, :], ALU.mult),
                            [t_ro, t_o[k]])
                r_read[:] = [t]
                return [dve.put(lambda e: e.tensor_tensor(XT[:, k, :], XT[:, k, :], OO[:, k, :], ALU.add), [t])]

            enter(add_o, lambda k: vec("g_ple_in_2", 16 * l + k), a_free)
            t_e = {}
            for c in range(2):
                jobs = []
                held = []
                for o in range(8):
                    if o % 2 == 0:
                        bank, freed = mbank.take()
                        held.append((bank, []))
                    for k in range(2):
                        jobs.append((bank[:, (o % 2) * T:(o % 2) * T + T], o * 2 + k, PH[:, k, :], PL[:, k, :],
                                     k == 0 and o % 2 == 0, k == 1, freed + [t_p2],
                                     held[-1][1].append if (o % 2 and k == 1) else None))
                chunk(jobs, 3 * c)
                for q, (bank, mark) in enumerate(held):
                    te = act.put(lambda e, c=c, q=q, bank=bank, EE=EE: e.activation(
                        EE[:, 8 * c + 2 * q:8 * c + 2 * q + 2, :], bank[:, :].rearrange("p (a t) -> p a t", a=2),
                        ACT.Copy), [mark[-1]] + end_y)
                    t_e[8 * c + 2 * q] = t_e[8 * c + 2 * q + 1] = te
                    mbank.give(bank, [te])

            p_free = marks_now()
            t_eg = {}

            def evac_g(n, bank, ps, t):
                s = n % 2
                t1 = dve.put(lambda e: e.tensor_tensor(TMP[:, s, :], ps, R[:, :], ALU.mult), [t, rr["t"]] + tmp_free[s])
                mbank.give(bank, [t1])
                r_read[:] = [t1]
                t1 = act.put(lambda e: e.activation(TMP[:, s, :], TMP[:, s, :], ACT.Sigmoid), [t1])
                t1 = dve.put(lambda e: e.tensor_tensor(EE[:, n, :], EE[:, n, :], TMP[:, s, :], ALU.mult),
                             [t1, t_e[n]])
                tmp_free[s] = [t1]
                t_eg[n] = t1
                square(EE[:, n, :], [t1], n, KD)

            out_tiles(16, A, LA, 16, evac_g, 0, 0)
            a_free = [t_used[st["used"] - 1]]
            t_rg = norm_stat(D)

            def add_e(k, l=l, EE=EE, t_rg=t_rg):
                t = dve.put(lambda e: e.scalar_tensor_tensor(
                    EE[:, k, :], EE[:, k, :], vec("g_ple_out_2", 16 * l + k), R[:, :], ALU.mult, ALU.mult), [t_rg])
                r_read[:] = [t]
                return [dve.put(lambda e: e.tensor_tensor(XT[:, k, :], XT[:, k, :], EE[:, k, :], ALU.add), [t])]

            if l == 0:
                enter(add_e, lambda k: vec("g_pre_2", 16 + k), a_free)
            else:
                for k in range(KD):
                    t = add_e(k)
                    if k % 4 == 3:
                        q = k // 4
                        sp.dma(lambda e: e.dma_start(
                            out.rearrange("p (k t) -> p k t", k=KD)[:, 4 * q:4 * q + 4, :],
                            XT[:, 4 * q:4 * q + 4, :]), s_out, t)
            prev = marks_now()
            sE.close()
        sp.wait([(s_out, 64)])
        s2.close()
        assert st["used"] == NCH, (st["used"], NCH)
        assert not sq["late"]


def _panels(np, w, kt=16):
    k, n = w.shape
    a = w.reshape(k // (kt * 128), kt, 128, n // 128, 128).transpose(3, 0, 2, 1, 4)
    return a.reshape(-1, 128, kt * 128)


def _layout(np, x):
    f = np.float32
    o = {}

    def col(v):
        v = np.asarray(v).reshape(-1)
        return v.reshape(-1, 128).T

    def tok(v):
        t, n = v.shape
        return v.T.reshape(n // 128, 128, t).transpose(1, 0, 2)

    cols = {}
    for name, _ in VECS:
        if name == "gla_bias":
            cols[name] = np.concatenate([col(x["gla_bias_f"]), col(x["gla_bias_b"])], axis=1)
        elif name == "eps":
            cols[name] = np.full((128, 1), 1e-6, f)
        elif name == "one":
            cols[name] = np.ones((128, 1), f)
        else:
            cols[name] = col(x[name])
    o["vecs"] = np.concatenate([cols[n] for n, _ in VECS], axis=1)
    o["xt"] = tok(x["x"][0]).reshape(128, -1)
    o["ones"] = np.ones((128, 128), f)
    o["ident"] = np.eye(128, dtype=f)
    w = x["w_in"][0]
    o["w_in"] = np.concatenate([_panels(np, w[:, 0:1024]), _panels(np, w[:, 1024:1152]),
                                _panels(np, w[:, 1056:1568]), _panels(np, w[:, 1568:])], axis=0)
    z = np.zeros((16, 256), f)
    o["gla_up"] = np.concatenate([np.concatenate([x["gla_up_f"][0], z], axis=1),
                                  np.concatenate([z, x["gla_up_b"][0]], axis=1)], axis=0)
    o["w_out"] = _panels(np, x["w_out"][0])
    o["w_query"] = _panels(np, x["peer_w_query"][0])
    o["sub_keys"] = x["peer_sub_keys"][0].reshape(16, 128, 128).transpose(2, 0, 1).reshape(128, 2048)
    o["peer_down"] = x["peer_down"][0].reshape(128, 128, 16, 128).transpose(1, 3, 2, 0).reshape(128, 128, 2048)
    o["peer_up"] = x["peer_up"][0]
    o["w_in_2"] = np.concatenate([_panels(np, x["w_in_2"][l]) for l in range(2)], axis=0)
    o["w_out_2"] = np.concatenate([_panels(np, x["w_out_2"][l]) for l in range(2)], axis=0)
    o["w_gate"] = np.concatenate([_panels(np, x["w_ple_gate_2"][l]) for l in range(2)], axis=0)
    pw = x["pool_w_2"][0].reshape(4, 8, 128, 4, 2, 128).transpose(0, 3, 2, 4, 1, 5)
    o["pool_w"] = pw.reshape(16, 128, 2048)
    pl = x["w_ple_2"].reshape(2, 2, 128, 2, 8, 128).transpose(0, 3, 2, 4, 1, 5)
    o["w_ple"] = pl.reshape(4, 128, 2048)
    lw = np.stack([x["lru_wa_2"][0], x["lru_wx_2"][0]], axis=1)
    lw = lw.reshape(8, 2, 2, 2, 128, 2, 128).transpose(0, 4, 1, 2, 3, 5, 6)
    o["lru_w"] = lw.reshape(8, 128, 2048)
    o["p_2"] = np.stack([tok(x["p_2"][l, 0]) for l in range(2)], axis=1).reshape(128, 1024)
    i = np.arange(256)
    rel = i[:, None] - i[None, :]
    cnt = (np.abs(rel) <= 64).astype(f) + (rel % 4 == 0).astype(f) + (rel % 16 == 0).astype(f)
    bias = np.where(cnt > 0, np.log(np.maximum(cnt, 1.0)), -1e30).astype(f)
    o["c_bias"] = bias.reshape(2, 128, 256).transpose(1, 0, 2).reshape(128, 512)
    j = np.arange(128)
    same = (j[:, None] // 64) == (j[None, :] // 64)
    mf = (same & (j[:, None] <= j[None, :])).astype(f)
    mb = (same & (j[:, None] > j[None, :])).astype(f)
    o["c_gmask"] = np.concatenate([mf, mb], axis=1)
    inv = np.float32(500000.0) ** (-np.arange(16, dtype=f) / f(16))
    ang = inv.astype(f)[:, None] * np.arange(256, dtype=f)[None, :]
    c, s = np.cos(ang).astype(f), np.sin(ang).astype(f)
    c2, s2 = np.concatenate([c, c], 0), np.concatenate([-s, s], 0)
    o["c_rope"] = np.concatenate([c2, s2], axis=1)
    rot = np.zeros((32, 32), f)
    rot[np.arange(16) + 16, np.arange(16)] = 1.0
    rot[np.arange(16), np.arange(16) + 16] = 1.0
    o["c_rot"] = rot
    o["c_scan"] = np.tile((i % 64 != 0).astype(f), (128, 1))
    o["c_iota"] = np.tile(j.astype(f), (128, 1))
    o["c_inv"] = np.tile(np.concatenate([1.0 / np.minimum(i[:16] + 1, w) for w in (2, 4, 8, 16)]).astype(f), (128, 1))
    return {k: np.ascontiguousarray(v) for k, v in o.items()}


def kernel(**inputs):
    import numpy as np
    import concourse.bacc as bacc
    from concourse.bass_utils import run_bass_kernel_spmd as run

    arrays = _layout(np, {k: np.asarray(v) for k, v in inputs.items()})
    nc = bacc.Bacc("TRN2", target_bir_lowering=False, num_devices=1, dynamic_dma_scratch_size=512)
    d = {k: nc.dram_tensor("in_" + k, a.shape, mybir.dt.from_np(a.dtype), kind="ExternalInput").ap()
         for k, a in arrays.items()}
    out = nc.dram_tensor("out_0", (128, 4096), F32, kind="ExternalOutput").ap()
    build(nc, d, out)
    r = run(nc, [{"in_" + k: a for k, a in arrays.items()}], core_ids=[0])
    y = r.results[0]["out_0"].reshape(128, 16, 256).transpose(2, 1, 0).reshape(1, 256, 2048)
    return np.ascontiguousarray(y)
```
